# Optimizing a Trainium2 kernel written in Bass

```python
import jax
import jax.numpy as jnp
from jax import lax
import numpy as np

D_MODEL = 1024
BATCH = 1
SEQ = 128
DEPTH = 2
DEC_BATCH = 1
DEC_SEQ = 512
PAST_LEN = 128

GRID_W = 64
BLOCK = 128
WINDOW = 128
ATTN_HEADS = 8
KV_HEADS = 2
GROUP = ATTN_HEADS // KV_HEADS
HEAD_DIM = 64
D_ATTN = ATTN_HEADS * HEAD_DIM
D_ATTN_IN = D_ATTN + 2 * KV_HEADS * HEAD_DIM
RWKV_HEADS = 8
RWKV_HEAD_DIM = 64
D_RWKV = RWKV_HEADS * RWKV_HEAD_DIM
LORA_W = 64
LORA_A = 64
LORA_G = 128
D_RWKV_IN = 3 * D_RWKV + 2 * LORA_W + 2 * LORA_A + LORA_G
D_IN_AB = D_ATTN_IN + D_RWKV_IN
SHIFT_WIDTH = 3
ROPE_BASE = 10000.0
D_CONV = D_MODEL
CONV_WIDTH = 31
PEER_HEADS = 8
N_KEYS = 128
N_EXPERTS = N_KEYS * N_KEYS
D_QUERY = 256
PEER_TOPK = 16
N_EVEN = (DEPTH + 1) // 2
N_ODD = DEPTH // 2
RMS_EPS = 1e-6
LN_EPS = 1e-5
GN_EPS = 64e-5

kernel_name = 'hybrid_diffusion_prefix_trunk_step'

def rmsnorm(x, g):
    xf = x.astype(jnp.float32)
    y = xf * lax.rsqrt(jnp.mean(xf * xf, axis=-1, keepdims=True) + RMS_EPS)
    return (y * g.astype(jnp.float32)).astype(x.dtype)

def layernorm(x, g, b, eps):
    xf = x.astype(jnp.float32)
    mu = jnp.mean(xf, axis=-1, keepdims=True)
    var = jnp.mean(jnp.square(xf - mu), axis=-1, keepdims=True)
    y = (xf - mu) * lax.rsqrt(var + eps)
    return (y * g.astype(jnp.float32) + b.astype(jnp.float32)).astype(x.dtype)

def modulation(cond, w, b):
    m = jax.nn.silu(cond) @ w + b
    return jnp.split(m[:, None, :], 6, axis=-1)

def modulate(h, shift, scale):
    return h * (1 + scale) + shift

def depthwise_conv(x, w):
    return lax.conv_general_dilated(
        x, w[:, None, :].astype(x.dtype), window_strides=(1,), padding='SAME',
        dimension_numbers=('NWC', 'WIO', 'NWC'), feature_group_count=x.shape[-1])

def axial_rope(x):
    t = x.shape[1]
    rows = t // GRID_W
    row_id = jnp.repeat(jnp.arange(rows, dtype=jnp.float32), GRID_W)
    col_id = jnp.tile(jnp.arange(GRID_W, dtype=jnp.float32), rows)
    half = HEAD_DIM // 2
    quarter = half // 2
    freqs = ROPE_BASE ** (-jnp.arange(quarter, dtype=jnp.float32) / quarter)

    def rotate(xa, pos):
        ang = pos[:, None] * freqs[None, :]
        cos = jnp.cos(ang)[None, :, None, :]
        sin = jnp.sin(ang)[None, :, None, :]
        xa = xa.astype(jnp.float32)
        a, b = xa[..., :quarter], xa[..., quarter:]
        return jnp.concatenate([a * cos - b * sin, b * cos + a * sin], axis=-1)

    y = jnp.concatenate([rotate(x[..., :half], row_id), rotate(x[..., half:], col_id)], axis=-1)
    return y.astype(x.dtype)

def context_attention(q, k, v, sink):
    b, c = q.shape[:2]
    nqb = c // BLOCK
    scale = HEAD_DIM ** -0.5
    qb = q.reshape(b, nqb, BLOCK, KV_HEADS, GROUP, HEAD_DIM).transpose(1, 0, 2, 3, 4, 5)
    sink_l = jnp.broadcast_to(sink.astype(jnp.float32).reshape(1, KV_HEADS, GROUP, 1, 1),
                              (b, KV_HEADS, GROUP, BLOCK, 1))

    def one(qblk):
        s = jnp.einsum('bqkgd,bckd->bkgqc', qblk, k).astype(jnp.float32) * scale
        p = jax.nn.softmax(jnp.concatenate([s, sink_l], axis=-1), axis=-1)[..., :c]
        return jnp.einsum('bkgqc,bckd->bqkgd', p.astype(v.dtype), v)

    out = lax.map(one, qb)
    return out.transpose(1, 0, 2, 3, 4, 5).reshape(b, c, D_ATTN)

def window_attention(q, k, v, k_ctx, v_ctx, sink):
    b, t = q.shape[:2]
    c = k_ctx.shape[1]
    nb = t // BLOCK
    scale = HEAD_DIM ** -0.5
    qb = q.reshape(b, nb, BLOCK, KV_HEADS, GROUP, HEAD_DIM)
    pad = ((0, 0), (BLOCK, BLOCK), (0, 0), (0, 0))
    kp = jnp.pad(k, pad).reshape(b, nb + 2, BLOCK, KV_HEADS, HEAD_DIM)
    vp = jnp.pad(v, pad).reshape(b, nb + 2, BLOCK, KV_HEADS, HEAD_DIM)
    kb = jnp.concatenate([kp[:, :-2], kp[:, 1:-1], kp[:, 2:]], axis=2)
    vb = jnp.concatenate([vp[:, :-2], vp[:, 1:-1], vp[:, 2:]], axis=2)
    qpos = jnp.arange(t).reshape(nb, BLOCK)
    kpos = (jnp.arange(nb)[:, None] - 1) * BLOCK + jnp.arange(3 * BLOCK)[None, :]
    rel = kpos[:, None, :] - qpos[:, :, None]
    valid = (jnp.abs(rel) <= WINDOW) & (kpos[:, None, :] >= 0) & (kpos[:, None, :] < t)
    s_loc = jnp.einsum('bnqkgd,bnskd->bnkgqs', qb, kb).astype(jnp.float32) * scale
    s_loc = jnp.where(valid[None, :, None, None], s_loc, -jnp.inf)
    s_ctx = jnp.einsum('bnqkgd,bckd->bnkgqc', qb, k_ctx).astype(jnp.float32) * scale
    sink_l = jnp.broadcast_to(sink.astype(jnp.float32).reshape(1, 1, KV_HEADS, GROUP, 1, 1),
                              s_loc.shape[:-1] + (1,))
    p = jax.nn.softmax(jnp.concatenate([s_loc, s_ctx, sink_l], axis=-1), axis=-1)
    p_loc = p[..., :3 * BLOCK].astype(v.dtype)
    p_ctx = p[..., 3 * BLOCK:3 * BLOCK + c].astype(v.dtype)
    o = (jnp.einsum('bnkgqs,bnskd->bnqkgd', p_loc, vb)
         + jnp.einsum('bnkgqc,bckd->bnqkgd', p_ctx, v_ctx))
    return o.reshape(b, t, D_ATTN)

def rwkv_scan(r, w, kh, ka, kt, v, s0, reverse):
    def step(s, inp):
        r_t, w_t, kh_t, ka_t, kt_t, v_t = inp
        s = (s * w_t[:, :, None, :]
             - jnp.einsum('bhvk,bhk->bhv', s, kh_t)[..., None] * ka_t[:, :, None, :]
             + v_t[..., None] * kt_t[:, :, None, :])
        return s, jnp.einsum('bhvk,bhk->bhv', s, r_t)

    xs = tuple(jnp.moveaxis(a, 1, 0) for a in (r, w, kh, ka, kt, v))
    s_fin, y = lax.scan(step, s0, xs, reverse=reverse)
    return jnp.moveaxis(y, 0, 1), s_fin

def rwkv_mix(u, k_k, k_a, r_k, w0, w2, a0, a2, g2, gn_g, gn_b, s0):
    f32 = jnp.float32
    b, t = u.shape[:2]
    u = u.astype(f32)
    cuts = [D_RWKV, 2 * D_RWKV, 3 * D_RWKV, 3 * D_RWKV + LORA_W, 3 * D_RWKV + 2 * LORA_W,
            3 * D_RWKV + 2 * LORA_W + LORA_A, 3 * D_RWKV + 2 * LORA_W + 2 * LORA_A]
    r, k, v, wl_f, wl_b, al_f, al_b, gl = jnp.split(u, cuts, axis=-1)

    def heads(z):
        return z.reshape(b, t, RWKV_HEADS, RWKV_HEAD_DIM)

    kk = heads(k * k_k)
    kh = kk / jnp.maximum(jnp.linalg.norm(kk, axis=-1, keepdims=True), 1e-12)
    s0 = s0.astype(f32)

    def direction(idx, wl, al, reverse):
        logw = -jax.nn.softplus(-(w0[idx] + jnp.tanh(wl) @ w2[idx])) - 0.5
        decay = jnp.exp(-jnp.exp(logw))
        a = jax.nn.sigmoid(a0[idx] + al @ a2[idx])
        kt = heads(k * (1 + (a - 1) * k_a))
        y, s = rwkv_scan(heads(r), heads(decay), kh, kh * heads(a), kt, heads(v), s0[:, idx], reverse)
        return y, s, kt

    y_f, s_f, kt_f = direction(0, wl_f, al_f, False)
    y_b, s_b, kt_b = direction(1, wl_b, al_b, True)
    y = layernorm(y_f + y_b, gn_g.reshape(RWKV_HEADS, RWKV_HEAD_DIM),
                  gn_b.reshape(RWKV_HEADS, RWKV_HEAD_DIM), GN_EPS)
    bonus = jnp.sum(heads(r) * 0.5 * (kt_f + kt_b) * r_k.reshape(RWKV_HEADS, RWKV_HEAD_DIM),
                    axis=-1, keepdims=True) * heads(v)
    g = jax.nn.sigmoid(gl) @ g2
    out = (y + bonus).reshape(b, t, D_RWKV) * g
    return out, jnp.stack([s_f, s_b], axis=1)

def mixer_even(h, w_in, w_out, sink, shift_w, k_k, k_a, r_k, w0, w2, a0, a2, g2, gn_g, gn_b, ctx):
    b, t = h.shape[:2]
    d_kv = KV_HEADS * HEAD_DIM
    u = h @ w_in
    q = u[..., :D_ATTN].reshape(b, t, ATTN_HEADS, HEAD_DIM)
    k = u[..., D_ATTN:D_ATTN + d_kv].reshape(b, t, KV_HEADS, HEAD_DIM)
    v = u[..., D_ATTN + d_kv:D_ATTN_IN].reshape(b, t, KV_HEADS, HEAD_DIM)
    u_r = depthwise_conv(u[..., D_ATTN_IN:], shift_w)
    if ctx is None:
        a_out = context_attention(q, k, v, sink)
        s0 = jnp.zeros((b, 2, RWKV_HEADS, RWKV_HEAD_DIM, RWKV_HEAD_DIM), jnp.float32)
    else:
        k_ctx, v_ctx, s0 = ctx
        a_out = window_attention(axial_rope(q), axial_rope(k), v,
                                 k_ctx.astype(h.dtype), v_ctx.astype(h.dtype), sink)
    b_out, s_fin = rwkv_mix(u_r, k_k, k_a, r_k, w0, w2, a0, a2, g2, gn_g, gn_b, s0)
    y = jnp.concatenate([a_out, b_out.astype(a_out.dtype)], axis=-1) @ w_out
    return y, k, v, s_fin

def mixer_odd(h, w_pw1, b_pw1, w_dw, b_dw, ln_g, ln_b, w_pw2, b_pw2):
    u = h @ w_pw1 + b_pw1
    u = u[..., :D_CONV] * jax.nn.sigmoid(u[..., D_CONV:])
    u = depthwise_conv(u, w_dw) + b_dw
    u = jax.nn.silu(layernorm(u, ln_g, ln_b, LN_EPS))
    return u @ w_pw2 + b_pw2

def peer(h, w_q, keys, u_tab, v_tab):
    b, t, d = h.shape
    x = h.reshape(-1, BLOCK, d)
    half = D_QUERY // 2

    def one(xb):
        q = (xb @ w_q).reshape(BLOCK, PEER_HEADS, D_QUERY)
        s1 = jnp.einsum('thd,hnd->thn', q[..., :half], keys[0]).astype(jnp.float32)
        s2 = jnp.einsum('thd,hnd->thn', q[..., half:], keys[1]).astype(jnp.float32)
        v1, i1 = lax.top_k(s1, PEER_TOPK)
        v2, i2 = lax.top_k(s2, PEER_TOPK)
        cand = (v1[..., :, None] + v2[..., None, :]).reshape(BLOCK, PEER_HEADS, PEER_TOPK * PEER_TOPK)
        cidx = (i1[..., :, None] * N_KEYS + i2[..., None, :]).reshape(BLOCK, PEER_HEADS, PEER_TOPK * PEER_TOPK)
        sv, pos = lax.top_k(cand, PEER_TOPK)
        eidx = jnp.take_along_axis(cidx, pos, axis=-1)
        g = jax.nn.softmax(sv, axis=-1)
        act = jax.nn.gelu(jnp.einsum('thkd,td->thk', u_tab[eidx], xb), approximate=False)
        wgt = (g * act.astype(jnp.float32)).astype(xb.dtype)
        return jnp.einsum('thk,thkd->td', wgt, v_tab[eidx])

    return lax.map(one, x).reshape(b, t, d)

def setup_inputs(seed: int = 0) -> dict:
    key = jax.random.key(seed)
    keys = iter(jax.random.split(key, 64))

    def nrm(shape, scale):
        return jax.random.normal(next(keys), shape, jnp.float32) * scale

    d = D_MODEL
    return {
        'x_prompt': nrm((BATCH, SEQ, d), 1.0),
        'x_sample': nrm((DEC_BATCH, DEC_SEQ, d), 1.0),
        'cache_k': nrm((DEC_BATCH, N_EVEN, PAST_LEN, KV_HEADS, HEAD_DIM), 1.0),
        'cache_v': nrm((DEC_BATCH, N_EVEN, PAST_LEN, KV_HEADS, HEAD_DIM), 1.0),
        'state_rwkv': nrm((DEC_BATCH, N_EVEN, 2, RWKV_HEADS, RWKV_HEAD_DIM, RWKV_HEAD_DIM), 0.3),
        'c': nrm((DEC_BATCH, d), 1.0),
        'c_ctx': nrm((d,), 1.0),
        'mod_w': nrm((DEPTH, d, 6 * d), 0.5 * d ** -0.5),
        'mod_b': nrm((DEPTH, 6 * d), 0.02),
        'norm_g': 1.0 + nrm((DEPTH, 2, d), 0.05),
        'ab_w_in': nrm((N_EVEN, d, D_IN_AB), d ** -0.5),
        'ab_w_out': nrm((N_EVEN, D_ATTN + D_RWKV, d), (D_ATTN + D_RWKV) ** -0.5),
        'ab_sink': nrm((N_EVEN, ATTN_HEADS), 0.5),
        'ab_shift_w': nrm((N_EVEN, SHIFT_WIDTH, D_RWKV_IN), 0.1).at[:, SHIFT_WIDTH // 2].add(1.0),
        'ab_k_k': 0.85 + nrm((N_EVEN, D_RWKV), 0.05),
        'ab_k_a': 1.0 + nrm((N_EVEN, D_RWKV), 0.05),
        'ab_r_k': nrm((N_EVEN, D_RWKV), 0.1),
        'ab_w0': nrm((N_EVEN, 2, D_RWKV), 0.5),
        'ab_w2': nrm((N_EVEN, 2, LORA_W, D_RWKV), 0.1),
        'ab_a0': nrm((N_EVEN, 2, D_RWKV), 0.1),
        'ab_a2': nrm((N_EVEN, 2, LORA_A, D_RWKV), 0.1),
        'ab_g2': nrm((N_EVEN, LORA_G, D_RWKV), LORA_G ** -0.5),
        'ab_gn_g': 1.0 + nrm((N_EVEN, D_RWKV), 0.05),
        'ab_gn_b': nrm((N_EVEN, D_RWKV), 0.02),
        'cv_w_pw1': nrm((N_ODD, d, 2 * D_CONV), d ** -0.5),
        'cv_b_pw1': nrm((N_ODD, 2 * D_CONV), 0.02),
        'cv_w_dw': nrm((N_ODD, CONV_WIDTH, D_CONV), CONV_WIDTH ** -0.5),
        'cv_b_dw': nrm((N_ODD, D_CONV), 0.02),
        'cv_ln_g': 1.0 + nrm((N_ODD, D_CONV), 0.05),
        'cv_ln_b': nrm((N_ODD, D_CONV), 0.02),
        'cv_w_pw2': nrm((N_ODD, D_CONV, d), D_CONV ** -0.5),
        'cv_b_pw2': nrm((N_ODD, d), 0.02),
        'peer_w_q': nrm((DEPTH, d, PEER_HEADS * D_QUERY), d ** -0.5),
        'peer_keys': nrm((DEPTH, 2, PEER_HEADS, N_KEYS, D_QUERY // 2), (D_QUERY // 2) ** -0.5),
        'peer_u': nrm((DEPTH, N_EXPERTS, d), d ** -0.5),
        'peer_v': nrm((DEPTH, N_EXPERTS, d), 0.5),
        'final_g': 1.0 + nrm((d,), 0.05),
    }

def reference(x_prompt, x_sample, cache_k, cache_v, state_rwkv, c, c_ctx, mod_w, mod_b, norm_g,
              ab_w_in, ab_w_out, ab_sink, ab_shift_w, ab_k_k, ab_k_a, ab_r_k, ab_w0, ab_w2,
              ab_a0, ab_a2, ab_g2, ab_gn_g, ab_gn_b, cv_w_pw1, cv_b_pw1, cv_w_dw, cv_b_dw,
              cv_ln_g, cv_ln_b, cv_w_pw2, cv_b_pw2, peer_w_q, peer_keys, peer_u, peer_v, final_g):
    xp = x_prompt
    xs = x_sample
    new_k, new_v, new_s = [], [], []
    for layer in range(DEPTH):
        i = layer // 2
        sp1, cp1, gp1, sp2, cp2, gp2 = modulation(c_ctx[None, :], mod_w[layer], mod_b[layer])
        ss1, cs1, gs1, ss2, cs2, gs2 = modulation(c, mod_w[layer], mod_b[layer])
        hp = modulate(rmsnorm(xp, norm_g[layer, 0]), sp1, cp1)
        hs = modulate(rmsnorm(xs, norm_g[layer, 0]), ss1, cs1)
        if layer % 2 == 0:
            prm = (ab_w_in[i], ab_w_out[i], ab_sink[i], ab_shift_w[i], ab_k_k[i], ab_k_a[i],
                   ab_r_k[i], ab_w0[i], ab_w2[i], ab_a0[i], ab_a2[i], ab_g2[i], ab_gn_g[i], ab_gn_b[i])
            yp, k_c, v_c, s_c = mixer_even(hp, *prm, None)
            ys, _, _, _ = mixer_even(hs, *prm, (cache_k[:, i], cache_v[:, i], state_rwkv[:, i]))
            new_k.append(k_c)
            new_v.append(v_c)
            new_s.append(s_c)
        else:
            prm = (cv_w_pw1[i], cv_b_pw1[i], cv_w_dw[i], cv_b_dw[i], cv_ln_g[i], cv_ln_b[i],
                   cv_w_pw2[i], cv_b_pw2[i])
            yp = mixer_odd(hp, *prm)
            ys = mixer_odd(hs, *prm)
        xp = xp + gp1 * yp
        xs = xs + gs1 * ys
        hp = modulate(rmsnorm(xp, norm_g[layer, 1]), sp2, cp2)
        hs = modulate(rmsnorm(xs, norm_g[layer, 1]), ss2, cs2)
        pprm = (peer_w_q[layer], peer_keys[layer], peer_u[layer], peer_v[layer])
        xp = xp + gp2 * peer(hp, *pprm)
        xs = xs + gs2 * peer(hs, *pprm)
    y_prompt = rmsnorm(xp, final_g)
    y_sample = rmsnorm(xs, final_g)
    new_cache_k = jnp.stack(new_k, axis=1)
    new_cache_v = jnp.stack(new_v, axis=1)
    new_state_rwkv = jnp.stack(new_s, axis=1)
    return (y_prompt, y_sample, new_cache_k, new_cache_v, new_state_rwkv)


_drawn_inputs = setup_inputs


def setup_inputs(seed=0):
    import zlib

    import numpy as np

    out = dict(_drawn_inputs(seed))
    spreads = {}
    factors = {'cache_k': 3.108,
     'cache_v': 2.824,
     'state_rwkv': 8.0,
     'ab_sink': 33.679,
     'ab_k_k': 43.475,
     'ab_gn_g': 4.554,
     'ab_gn_b': 19.825,
     'cv_b_pw1': 8.0,
     'cv_b_dw': 6.378,
     'cv_ln_g': 3.938,
     'cv_ln_b': 8.0,
     'cv_b_pw2': 5.945}
    for name, (base, spread) in spreads.items():
        noise = np.random.default_rng([zlib.crc32(name.encode()), seed]).standard_normal(out[name].shape)
        drawn = base * np.exp(spread * noise) if base else spread * noise
        out[name] = jnp.asarray(drawn.astype(out[name].dtype))
    for name, factor in factors.items():
        out[name] = (out[name] * factor).astype(out[name].dtype)
    return out
```

```python
from contextlib import ExitStack

import numpy as np

import concourse.bass as bass
from concourse import mybir

F32 = mybir.dt.float32
U32 = mybir.dt.uint32
ALU = mybir.AluOpType
ACT = mybir.ActivationFunctionType
AXX = mybir.AxisListType.X

P = 128
D = 1024
KD = D // P
T_CTX, T_LAT = 128, 512
T = T_CTX + T_LAT
NT = T // P
DEPTH = 2
HEADS, KV, HD = 8, 2, 64
D_ATTN = HEADS * HD
D_AIN = D_ATTN + 2 * KV * HD
D_RW = 512
NCC = D_RW // P
D_IN = D_AIN + 3 * D_RW + 3 * P
CONVW = 31
PADC = CONVW // 2
PH, NKEY, TOPK = 8, 128, 16
NEXP = NKEY * NKEY
GRID_W = 64
CH = 64
NEG = -1.0e30
LOW = -3.0e38
SQ = 384


def shape_constants():
    c = {}
    c["ident"] = np.eye(P, dtype=np.float32)
    blk = np.zeros((P, P), np.float32)
    blk[:64, :64] = 1
    blk[64:, 64:] = 1
    c["headsum"] = blk
    half, quarter = HD // 2, HD // 4
    freqs = np.float32(10000.0) ** (-np.arange(quarter, dtype=np.float32) / np.float32(quarter))
    t = np.arange(T_LAT)
    row = (t // GRID_W).astype(np.float32)
    col = (t % GRID_W).astype(np.float32)
    cos = np.zeros((HD, T_LAT), np.float32)
    sin = np.zeros((HD, T_LAT), np.float32)
    perm = np.zeros((P, P), np.float32)
    for d in range(HD):
        pos = row if d < half else col
        ang = pos * freqs[d % quarter]
        cos[d], sin[d] = np.cos(ang), np.sin(ang)
        first = (d % half) < quarter
        for g in range(2):
            if first:
                perm[g * HD + d + quarter, g * HD + d] = -1
            else:
                perm[g * HD + d - quarter, g * HD + d] = 1
    c["rope"] = np.concatenate([np.tile(cos, (2, 1)), np.tile(sin, (2, 1))], axis=1)
    c["ropeperm"] = perm
    q = np.arange(P)[:, None]
    k = np.arange(P)[None, :]
    z = np.zeros((P, P), np.float32)
    prev = np.where(k >= q, 0, NEG).astype(np.float32)
    nxt = np.where(k <= q, 0, NEG).astype(np.float32)
    c["amask"] = np.concatenate([z, prev, z, nxt, z, z, nxt], axis=1)
    r = np.arange(CH)[:, None]
    s = np.arange(CH)[None, :]
    strict = (s < r).astype(np.float32)
    diag = np.eye(CH, dtype=np.float32)
    sm = []
    for d in range(2):
        st = strict if d == 0 else strict.T
        sm.append([-st, -st.T, st.T, st.T + diag, -(st.T + diag)])
    sm = np.array(sm).transpose(1, 0, 2, 3)
    c["scanmask"] = np.tile(sm.transpose(2, 0, 1, 3).reshape(CH, -1), (2, 1)).astype(np.float32)
    lev = []
    b = 1
    while b < CH:
        m = ((r // (2 * b)) == (s // (2 * b))) & (r % (2 * b) >= b) & (s % (2 * b) < b)
        lev.append([[m, m.T], [m.T, m]])
        b *= 2
    lev = np.array(lev).astype(np.float32)
    c["levmask"] = np.tile(lev.transpose(3, 0, 1, 2, 4).reshape(CH, -1), (2, 1)).copy()
    reset = np.ones((P, T), np.float32)
    reset[:, ::CH] = 0
    c["reset"] = reset
    c["eye64"] = np.tile(np.eye(CH, dtype=np.float32), (2, 1))
    c["iota16"] = np.tile(np.tile(np.arange(TOPK, dtype=np.float32), TOPK), (P, 1))
    return c


class Ctx:

    def __init__(self, nc, io):
        self.nc, self.io, self.live = nc, io, []

    def sem(self, name):
        self.live.append(self.nc.alloc_semaphore(name))
        return self.live[-1]

    def recycle(self):
        self.nc.clear_and_free_semaphores(self.live)
        self.nc.all_engine_barrier()
        self.live = []


def chain_on(eng, sem):
    n = [0]

    def step(ins, wait=True):
        n[0] += 1
        ins.then_inc(sem, 1)
        if wait:
            eng.wait_ge(sem, n[0])
        return n[0]
    return step


def phase_modulation(K):
    nc, io = K.nc, K.io
    NCH = 6 * D // 512
    RING = 4
    with ExitStack() as mem:
        sb = lambda n, s, d=F32: mem.enter_context(nc.sbuf_tensor(n, s, d))
        cond = sb("cond", [P, 2, KD])
        csil = sb("csil", [P, KD, 2])
        wring = sb("mod_wring", [P, RING, KD, 512])
        bias = sb("mod_bias", [2, DEPTH * 6 * D])
        rows = sb("mod_rows", [2, DEPTH, 6, D])
        normg = sb("mod_normg", [2, DEPTH, 2, D])
        ps = mem.enter_context(nc.psum_tensor("mod_ps", [P, 8, 512], F32))
        cond_in, silu_done = K.sem("cond_in"), K.sem("silu_done")
        small_in = K.sem("mod_small_in")
        w_in = [K.sem(f"mod_w_in{i}") for i in range(RING)]
        chunk_done, row_done = K.sem("mod_chunk_done"), K.sem("mod_row_done")
        scaled, stored = K.sem("mod_scaled"), K.sem("mod_stored")
        with nc.Block() as block:
            @block.sync
            def _(sp):
                sp.dma_start(cond[:, 0, :], io["c_ctx"].rearrange("(p k) -> p k", k=KD)).then_inc(cond_in, 16)
                sp.dma_start(cond[:, 1, :], io["c"].rearrange("a (p k) -> p (a k)", k=KD)).then_inc(cond_in, 16)
                for layer in range(DEPTH):
                    w = io["mod_w"][layer].rearrange("(p k) n -> p k n", k=KD)
                    with sp.Fori(0, NCH // RING) as i:
                        for r in range(RING):
                            sp.wait_ge(chunk_done, i * RING + (layer * NCH + r + 1))
                            sp.dma_start(wring[:, r], w[:, :, bass.ds((i * RING + r) * 512, 512)]).then_inc(w_in[r], 16)
                sp.wait_ge(scaled, DEPTH * 2)
                sp.dma_start(K.modrows, rows[:].rearrange("p l k d -> p (l k d)")).then_inc(stored, 16)
                sp.wait_ge(stored, 16)

            @block.scalar
            def _(act):
                act.dma_start(bias[:], io["mod_b"].rearrange("l n -> (l n)").partition_broadcast(2)).then_inc(small_in, 16)
                act.dma_start(normg[:].rearrange("p l k d -> p (l k d)"),
                              io["norm_g"].rearrange("l k d -> (l k d)").partition_broadcast(2)).then_inc(small_in, 16)
                act.wait_ge(cond_in, 32)
                nc.scalar.activation(csil[:].rearrange("p k s -> p s k"), cond[:], ACT.Silu).then_inc(silu_done, 1)

            @block.tensor
            def _(pe):
                pe.sem_inc(chunk_done, RING)
                pe.wait_ge(silu_done, 1)
                for layer in range(DEPTH):
                    with pe.Fori(0, NCH // RING) as i:
                        for r in range(RING):
                            pe.wait_ge(w_in[r], i * 16 + 16 * (layer * NCH // RING + 1))
                            pe.wait_ge(row_done, i * RING + (layer * NCH + r + 1))
                            for k in range(KD):
                                last = nc.tensor.matmul(ps[0:2, r, :], csil[:, k, :], wring[:, r, k, :],
                                                        start=(k == 0), stop=(k == KD - 1))
                            last.then_inc(chunk_done, 1)

            @block.vector
            def _(dve):
                dve.sem_inc(row_done, RING)
                dve.wait_ge(small_in, 32)
                flat = rows[:].rearrange("p l k d -> p (l k d)")
                for layer in range(DEPTH):
                    with dve.Fori(0, NCH // RING) as i:
                        for r in range(RING):
                            dve.wait_ge(chunk_done, i * RING + (layer * NCH + r + 1 + RING))
                            cols = bass.ds((i * RING + (layer * NCH + r)) * 512, 512)
                            nc.vector.tensor_tensor(flat[:, cols], ps[0:2, r, :], bias[:, cols], ALU.add).then_inc(row_done, 1)
                dve.wait_ge(row_done, DEPTH * NCH + RING)
                for layer in range(DEPTH):
                    for site in range(2):
                        sc = rows[:, layer, 3 * site + 1, :]
                        nc.vector.scalar_tensor_tensor(sc, sc, 1.0, normg[:, layer, site, :], ALU.add, ALU.mult).then_inc(scaled, 1)


def load_row(eng, K, dst, stream, layer, kind, sem):
    eng.dma_start(dst, K.modrows[stream, (layer * 6 + kind) * D:(layer * 6 + kind + 1) * D].partition_broadcast(P)).then_inc(sem, 16)


def phase_norm(K, layer, site, h, hT):
    nc = K.nc
    tag = f"n{layer}{site}_"
    x, ident = K.x, K.ident
    with ExitStack() as mem:
        sb = lambda n, s, d=F32: mem.enter_context(nc.sbuf_tensor(tag + n, s, d))
        rows = sb("rows", [P, 2, 2, D])
        ss = sb("ss", [P, NT])
        ms = sb("ms", [P, NT])
        rt = sb("rt", [P, NT])
        rstd = sb("rstd", [P, NT])
        ps = mem.enter_context(nc.psum_tensor(tag + "ps", [P, 8, 512], F32))
        rows_in, squares, mean_done, root_done = K.sem(tag + "rows_in"), K.sem(tag + "squares"), K.sem(tag + "mean"), K.sem(tag + "root")
        rstd_done, scaled, h_done, turned, hT_done = (K.sem(tag + n) for n in ("rstd", "scaled", "h_done", "turned", "hT_done"))
        with nc.Block() as block:
            @block.sync
            def _(sp):
                for s in range(2):
                    for j, kind in enumerate((3 * site + 1, 3 * site)):
                        load_row(sp, K, rows[:, s, j, :], s, layer, kind, rows_in)

            @block.scalar
            def _(act):
                for t in range(NT):
                    nc.scalar.activation(h[:, t, :], x[:, t, :], ACT.Square, accum_out=ss[:, t:t + 1]).then_inc(squares, 1)
                act.wait_ge(mean_done, 1)
                nc.scalar.activation(rt[:], ms[:], ACT.Sqrt).then_inc(root_done, 1)
                for t in range(NT):
                    for b in range(2):
                        act.wait_ge(turned, 2 * t + b + 1)
                        nc.scalar.copy(hT[:, 4 * b:4 * b + 4, t * P:(t + 1) * P],
                                       ps[:, (2 * t + b) % 8, :].rearrange("p (k c) -> p k c", k=4)).then_inc(hT_done, 1)

            @block.vector
            def _(dve):
                dve.wait_ge(squares, NT)
                nc.vector.tensor_scalar(ms[:], ss[:], 1.0 / D, 1e-6, ALU.mult, ALU.add).then_inc(mean_done, 1)
                dve.wait_ge(root_done, 1)
                nc.vector.reciprocal(rstd[:], rt[:]).then_inc(rstd_done, 1)
                dve.wait_ge(rstd_done, 1)
                dve.wait_ge(rows_in, 64)
                for t in range(NT):
                    s = min(t, 1)
                    nc.vector.scalar_tensor_tensor(h[:, t, :], x[:, t, :], rstd[:, t:t + 1], rows[:, s, 0, :], ALU.mult, ALU.mult).then_inc(scaled, 1)
                    dve.wait_ge(scaled, t + 1)
                    nc.vector.tensor_tensor(h[:, t, :], h[:, t, :], rows[:, s, 1, :], ALU.add).then_inc(h_done, 1)

            @block.tensor
            def _(pe):
                for t in range(NT):
                    pe.wait_ge(h_done, t + 1)
                    for b in range(2):
                        n = 2 * t + b
                        if n >= 8:
                            pe.wait_ge(hT_done, n - 7)
                        for k in range(4):
                            last = nc.tensor.transpose(ps[:, n % 8, k * P:(k + 1) * P], h[:, t, (4 * b + k) * P:(4 * b + k + 1) * P], ident[:])
                        last.then_inc(turned, 1)


def phase_scores(K, layer, hT, scores):
    nc, io, ident = K.nc, K.io, K.ident
    tag = f"s{layer}_"
    NC, RING = 2 * PH, 4
    with ExitStack() as mem:
        sb = lambda n, s, d=F32: mem.enter_context(nc.sbuf_tensor(tag + n, s, d))
        wring = sb("wring", [P, RING, KD, P])
        keys = sb("keys", [P, NC, P])
        keysT = sb("keysT", [P, NC, P])
        qT = sb("qT", [P, 2, T])
        ps = mem.enter_context(nc.psum_tensor(tag + "ps", [P, 4, 1024], F32))
        keys_in, keys_turned, keysT_done = K.sem(tag + "keys_in"), K.sem(tag + "keys_turned"), K.sem(tag + "keysT_done")
        w_in = [K.sem(tag + f"w_in{r}") for r in range(RING)]
        q_done, q_copied, s_done, s_copied = (K.sem(tag + n) for n in ("q_done", "q_copied", "s_done", "s_copied"))
        w_cols = io["peer_w_q"][layer].rearrange("(k p) n -> p k n", p=P)
        with nc.Block() as block:
            @block.sync
            def _(sp):
                sp.dma_start(keys[:], io["peer_keys"][layer].rearrange("a h n d -> n (a h) d")).then_inc(keys_in, 16)
                with sp.Fori(0, NC // RING) as i:
                    for r in range(RING):
                        sp.wait_ge(q_done, i * RING + (r + 1))
                        sp.dma_start(wring[:, r], w_cols[:, :, bass.ds((i * RING + r) * P, P)]).then_inc(w_in[r], 16)

            @block.tensor
            def _(pe):
                pe.sem_inc(q_done, RING)
                pe.wait_ge(keys_in, 16)
                for b in range(4):
                    for j in range(4):
                        c = 4 * b + j
                        last = nc.tensor.transpose(ps[:, b, j * P:(j + 1) * P], keys[:, (c % 2) * PH + c // 2, :], ident[:])
                    last.then_inc(keys_turned, 1)

                def queries(i, r):
                    pe.wait_ge(w_in[r], i * 16 + 16)
                    pe.wait_ge(q_copied, i * RING + (r + 1))
                    for k in range(KD):
                        nc.tensor.matmul(ps[:, r % 2, SQ:512], wring[:, r, k, :], hT[:, k, 0:T_CTX], start=(k == 0), stop=(k == KD - 1))
                        last = nc.tensor.matmul(ps[:, r % 2, 512:1024], wring[:, r, k, :], hT[:, k, T_CTX:T], start=(k == 0), stop=(k == KD - 1))
                    last.then_inc(q_done, 1)

                def score(i, r):
                    pe.wait_ge(q_copied, i * RING + (r + 3))
                    pe.wait_ge(s_copied, i * RING + (r + 1))
                    for t in range(NT):
                        last = nc.tensor.matmul(ps[:, 2 + r % 2, SQ + t * P:SQ + (t + 1) * P], qT[:, r % 2, t * P:(t + 1) * P],
                                                keysT[:, bass.ds(i * RING + r, 1), :].rearrange("p a n -> p (a n)"), start=True, stop=True)
                    last.then_inc(s_done, 1)

                pe.wait_ge(keysT_done, 4)
                with pe.Fori(0, NC // RING) as i:
                    queries(i, 0)
                    for r in range(1, RING):
                        queries(i, r)
                        score(i, r - 1)
                    score(i, RING - 1)

            @block.scalar
            def _(act):
                for b in range(4):
                    act.wait_ge(keys_turned, b + 1)
                    nc.scalar.copy(keysT[:, 4 * b:4 * b + 4, :].rearrange("p c n -> p (c n)"), ps[:, b, 0:512]).then_inc(keysT_done, 1)
                act.wait_ge(keysT_done, 4)
                act.sem_inc(q_copied, 2)
                with act.Fori(0, NC // RING) as i:
                    for r in range(RING):
                        act.wait_ge(q_done, i * RING + (r + 1 + RING))
                        act.wait_ge(s_done, i * RING + (r + 1))
                        nc.scalar.copy(qT[:, r % 2, :], ps[:, r % 2, SQ:1024]).then_inc(q_copied, 1)

            @block.vector
            def _(dve):
                dve.sem_inc(s_done, 2)
                dve.sem_inc(s_copied, 2)
                with dve.Fori(0, NC // RING) as i:
                    for r in range(RING):
                        dve.wait_ge(s_done, i * RING + (r + 3))
                        nc.vector.tensor_copy(scores[:, :, bass.ds((i * RING + r) * P, P)],
                                              ps[:, 2 + r % 2, SQ:1024].rearrange("p (t n) -> p t n", t=NT)).then_inc(s_copied, 1)


def phase_experts(K, layer, h, scores, yacc):
    nc, io, ident = K.nc, K.io, K.ident
    tag = f"e{layer}_"
    NI = NT * PH
    R = 8
    G = TOPK
    with ExitStack() as mem:
        sb = lambda n, s, d=F32: mem.enter_context(nc.sbuf_tensor(tag + n, s, d))
        uring = sb("uring", [P, R, D])
        vring = sb("vring", [P, R, D])
        diag = sb("diag", [P, G, P])
        eidx = sb("eidx", [P, NI * G], U32)
        uslot, vslot = sb("uslot", [P, 2, G], U32), sb("vslot", [P, 2, G], U32)
        gate = sb("gate", [P, NI * G])
        dots = sb("dots", [P, 2, G])
        gelu = sb("gelu", [P, 2, G])
        wgt = sb("wgt", [P, 2, G])
        iota = sb("iota", [P, G * G])
        item = sb("item", [P, 2, P])
        sub = sb("sub", [P, 2, P])
        top = sb("top", [P, 2, G])
        topi = sb("topi", [P, 2, G], U32)
        cand = sb("cand", [P, G * G])
        cand2 = sb("cand2", [P, G * G])
        best = sb("best", [P, G])
        besti = sb("besti", [P, G], U32)
        part = sb("part", [P, 2, G], U32)
        hot = sb("hot", [P, 2, G * G])
        half = sb("half", [P, 2, G])
        nbest = sb("nbest", [P, 1])
        expd = sb("expd", [P, G])
        esum = sb("esum", [P, 1])
        rsum = sb("rsum", [P, 1])
        ps = mem.enter_context(nc.psum_tensor(tag + "ps", [P, 4, D], F32))
        iota_in = K.sem(tag + "iota_in")
        u_in = [K.sem(tag + f"u_in{r}") for r in range(R)]
        v_in = [K.sem(tag + f"v_in{r}") for r in range(R)]
        u_used, v_used, granted, uslot_set, vslot_set = (K.sem(tag + n) for n in ("u_used", "v_used", "granted", "uslot_set", "vslot_set"))
        chosen, dve_own, neg_ready, exp_ready = (K.sem(tag + n) for n in ("chosen", "dve_own", "neg_ready", "exp_ready"))
        carried = K.sem(tag + "carried")
        gelu_ready, wgt_ready, diag_ready, summed = (K.sem(tag + n) for n in ("gelu_ready", "wgt_ready", "diag_ready", "summed"))
        u_tab = io["peer_u"].rearrange("l e d -> (l e) d")
        v_tab = io["peer_v"].rearrange("l e d -> (l e) d")
        flat = scores[:].rearrange("p t c -> p (t c)")
        with nc.Block() as block:
            def at(i, par):
                return 2 * i + par

            @block.gpsimd
            def _(pool):
                def set_uslot(i, par, first=False):
                    n = at(i, par)
                    pool.wait_ge(chosen, n + 1)
                    if not first:
                        pool.wait_ge(u_used, n * G + (R - G))
                    pool.sem_inc(granted, 1)
                    nc.gpsimd.tensor_copy(uslot[:, par, :], eidx[:, bass.ds(n * G, G)]).then_inc(uslot_set, 1)
                    pool.wait_ge(uslot_set, n + 1)

                def set_vslot(i, par, first=False):
                    n = at(i, par)
                    if not first:
                        pool.wait_ge(v_used, n * G + (R - G))
                    pool.sem_inc(granted, 1)
                    nc.gpsimd.tensor_copy(vslot[:, par, :], eidx[:, bass.ds(n * G, G)]).then_inc(vslot_set, 1)
                    pool.wait_ge(vslot_set, n + 1)

                def gather(ring, tab, index, r, sem):
                    pool.sem_inc(granted, 1)
                    pool.indirect_dma_start(ring[:, r % R, :], None, tab,
                                            bass.IndirectOffsetOnAxis(ap=index, axis=0)).then_inc(sem[r % R], 16)

                def u_row(i, par, r):
                    pool.wait_ge(u_used, at(i, par) * G + (r + 1))
                    gather(uring, u_tab, uslot[:, par, r:r + 1], r, u_in)

                def v_row(i, par, r):
                    pool.wait_ge(v_used, at(i, par) * G + (r + 1))
                    gather(vring, v_tab, vslot[:, par, r:r + 1], r, v_in)

                set_uslot(0, 0, first=True)
                for r in range(G):
                    u_row(0, 0, r)
                set_uslot(0, 1, first=True)
                set_vslot(0, 0, first=True)
                for r in range(G):
                    u_row(0, 1, r)
                    v_row(0, 0, r)
                set_uslot(1, 0)
                set_vslot(0, 1, first=True)
                for r in range(G):
                    u_row(1, 0, r)
                    v_row(0, 1, r)
                set_uslot(1, 1)
                set_vslot(1, 0)
                for r in range(G):
                    u_row(1, 1, r)
                    v_row(1, 0, r)
                with pool.Fori(2, NI // 2) as i:
                    set_uslot(i, 0)
                    set_vslot(i - 1, 1)
                    for r in range(G):
                        u_row(i, 0, r)
                        v_row(i - 1, 1, r)
                    set_uslot(i, 1)
                    set_vslot(i, 0)
                    for r in range(G):
                        u_row(i, 1, r)
                        v_row(i, 0, r)
                set_vslot(NI // 2 - 1, 1)
                for r in range(G):
                    v_row(NI // 2 - 1, 1, r)

            @block.vector
            def _(dve):
                def choosing(i, par):
                    n = at(i, par)
                    base = n * STEPS
                    count = [0]

                    def own(*instructions):
                        for ins in instructions:
                            count[0] += 1
                            ins.then_inc(dve_own, 1)

                    def after_own():
                        dve.wait_ge(dve_own, base + count[0])
                        dve.sem_inc(carried, 1)

                    s = [item[:, a, :] for a in range(2)]
                    c3 = cand[:].rearrange("p (a b) -> p a b", a=G)
                    io3 = iota[:].rearrange("p (a b) -> p a b", a=G)
                    hots = [hot[:, a, :].rearrange("p (a b) -> p a b", a=G) for a in range(2)]
                    V = nc.vector
                    own(V.tensor_copy(item[:].rearrange("p a n -> p (a n)"), flat[:, bass.ds(n * 2 * P, 2 * P)]))
                    yield
                    after_own()
                    own(*(V.max(top[:, a, 0:8], s[a]) for a in range(2)))
                    yield
                    after_own()
                    own(*(V.max_index(topi[:, a, 0:8], top[:, a, 0:8], s[a]) for a in range(2)))
                    own(*(V.match_replace(sub[:, a, :], top[:, a, 0:8], s[a], LOW) for a in range(2)))
                    yield
                    after_own()
                    own(*(V.max(top[:, a, 8:16], sub[:, a, :]) for a in range(2)))
                    yield
                    after_own()
                    own(*(V.max_index(topi[:, a, 8:16], top[:, a, 8:16], sub[:, a, :]) for a in range(2)))
                    own(V.tensor_tensor(c3, top[:, 0, :].unsqueeze(2).to_broadcast([P, G, G]),
                                        top[:, 1, :].unsqueeze(1).to_broadcast([P, G, G]), ALU.add))
                    yield
                    after_own()
                    own(V.max(best[:, 0:8], cand[:]))
                    yield
                    after_own()
                    own(V.max_index(besti[:, 0:8], best[:, 0:8], cand[:]), V.match_replace(cand2[:], best[:, 0:8], cand[:], LOW))
                    yield
                    after_own()
                    own(V.max(best[:, 8:16], cand2[:]))
                    yield
                    after_own()
                    own(V.tensor_scalar(nbest[:], best[:, 0:1], -1.0, None, ALU.mult), V.max_index(besti[:, 8:16], best[:, 8:16], cand2[:]))
                    yield
                    after_own()
                    dve.sem_inc(neg_ready, 1)
                    own(V.tensor_scalar(part[:, 0, :], besti[:], 4, None, ALU.logical_shift_right),
                        V.tensor_scalar(part[:, 1, :], besti[:], 15, None, ALU.bitwise_and))
                    yield
                    after_own()
                    own(*(V.tensor_tensor(hots[a], io3, part[:, a, :].unsqueeze(2).to_broadcast([P, G, G]), ALU.is_equal) for a in range(2)))
                    yield
                    after_own()
                    own(*(V.tensor_tensor(hots[a], hots[a], topi[:, a, :].unsqueeze(1).to_broadcast([P, G, G]), ALU.mult) for a in range(2)))
                    yield
                    after_own()
                    own(*(V.tensor_reduce(half[:, a, :], hots[a], AXX, ALU.add) for a in range(2)))
                    yield
                    after_own()
                    own(V.tensor_scalar(half[:, 0, :], half[:, 0, :], float(NKEY), float(layer * NEXP), ALU.mult, ALU.add))
                    yield
                    after_own()
                    own(V.tensor_tensor(eidx[:, bass.ds(n * G, G)], half[:, 0, :], half[:, 1, :], ALU.add))
                    dve.wait_ge(exp_ready, n + 1)
                    dve.sem_inc(carried, 1)
                    own(V.reciprocal(rsum[:], esum[:]))
                    yield
                    after_own()
                    dve.sem_inc(chosen, 1)
                    own(V.tensor_scalar(gate[:, bass.ds(n * G, G)], expd[:], rsum[:, 0:1], None, ALU.mult))
                    after_own()
                    assert count[0] == STEPS, count[0]
                    yield

                def choose(i, par):
                    for _ in choosing(i, par):
                        pass

                def dot(i, par, beside=None):
                    n = at(i, par)
                    for r in range(G):
                        if beside is not None:
                            next(beside)
                        dve.wait_ge(u_in[r % R], i * 64 + (32 * par + 16 * (r // R) + 16))
                        nc.vector.scalar_tensor_tensor(uring[:, r % R, :], uring[:, r % R, :], 1.0,
                                                       h[:, bass.ds(n // PH, 1), :].rearrange("p a d -> p (a d)"),
                                                       ALU.mult, ALU.mult, accum_out=dots[:, par, r:r + 1]).then_inc(u_used, 1)

                def weigh(i, par):
                    n = at(i, par)
                    dve.wait_ge(gelu_ready, n + 1)
                    nc.vector.tensor_tensor(wgt[:, par, :], gelu[:, par, :], gate[:, bass.ds(n * G, G)], ALU.mult).then_inc(wgt_ready, 1)

                def add_up(i, par):
                    n = at(i, par)
                    dve.wait_ge(v_used, n * G + (R + G))
                    dve.wait_ge(summed, n + 2)
                    y = yacc[:, bass.ds(n // PH, 1), :].rearrange("p a d -> p (a d)")
                    nc.vector.tensor_tensor(y, ps[:, par, :], y, ALU.add).then_inc(summed, 1)

                nc.vector.memset(yacc[:], 0.0).then_inc(summed, 2)
                dve.sem_inc(u_used, R)
                dve.wait_ge(iota_in, 16)
                choose(0, 0)
                choose(0, 1)
                for par in range(2):
                    dot(0, par, choosing(1, par))
                    weigh(0, par)
                with dve.Fori(1, NI // 2 - 1) as i:
                    for par in range(2):
                        dot(i, par, choosing(i + 1, par))
                        weigh(i, par)
                        add_up(i - 1, par)
                last = NI // 2 - 1
                for par in range(2):
                    dot(last, par)
                    weigh(last, par)
                    add_up(last - 1, par)
                for par in range(2):
                    add_up(last, par)

            @block.scalar
            def _(act):
                def exponents(i, par):
                    act.wait_ge(neg_ready, at(i, par) + 1)
                    nc.scalar.activation(expd[:], best[:], ACT.Exp, bias=nbest[:, 0:1], accum_out=esum[:]).then_inc(exp_ready, 1)

                def gelus(i, par):
                    n = at(i, par)
                    act.wait_ge(u_used, n * G + (R + G))
                    nc.scalar.activation(gelu[:, par, :], dots[:, par, :], ACT.Gelu).then_inc(gelu_ready, 1)

                def diags(i, par, first=False):
                    n = at(i, par)
                    act.wait_ge(wgt_ready, n + 1)
                    for r in range(G):
                        if not first:
                            act.wait_ge(v_used, n * G + (R + r + 1 - G))
                        nc.scalar.activation(diag[:, r, :], ident[:], ACT.Copy, scale=wgt[:, par, r:r + 1]).then_inc(diag_ready, 1)

                act.dma_start(iota[:], K.const["iota16"]).then_inc(iota_in, 16)
                exponents(0, 0)
                exponents(0, 1)
                for par in range(2):
                    exponents(1, par)
                    gelus(0, par)
                    diags(0, par, first=(par == 0))
                with act.Fori(1, NI // 2 - 1) as i:
                    for par in range(2):
                        exponents(i + 1, par)
                        gelus(i, par)
                        diags(i, par)
                last = NI // 2 - 1
                for par in range(2):
                    gelus(last, par)
                    diags(last, par)

            @block.tensor
            def _(pe):
                pe.sem_inc(v_used, R)
                with pe.Fori(0, NI // 2) as i:
                    for par in range(2):
                        n = at(i, par)
                        pe.wait_ge(summed, n + 1)
                        for r in range(G):
                            pe.wait_ge(diag_ready, n * G + (r + 1))
                            pe.wait_ge(v_in[r % R], i * 64 + (32 * par + 16 * (r // R) + 16))
                            nc.tensor.matmul(ps[:, par, 0:512], diag[:, r, :], vring[:, r % R, 0:512], start=(r == 0), stop=(r == G - 1))
                            nc.tensor.matmul(ps[:, par, 512:D], diag[:, r, :], vring[:, r % R, 512:D], start=(r == 0), stop=(r == G - 1)).then_inc(v_used, 1)


def phase_gate_add(K, layer, site, y, tag):
    nc = K.nc
    with ExitStack() as mem:
        rows = mem.enter_context(nc.sbuf_tensor(tag + "rows", [P, 2, D], F32))
        rows_in, gated, added = K.sem(tag + "rows_in"), K.sem(tag + "gated"), K.sem(tag + "added")
        with nc.Block() as block:
            @block.sync
            def _(sp):
                for s in range(2):
                    load_row(sp, K, rows[:, s, :], s, layer, 3 * site + 2, rows_in)

            @block.vector
            def _(dve):
                dve.wait_ge(rows_in, 32)
                nc.vector.tensor_tensor(y[:, 0, :], y[:, 0, :], rows[:, 0, :], ALU.mult).then_inc(gated, 1)
                nc.vector.tensor_tensor(y[:, 1:NT, :], y[:, 1:NT, :], rows[:, 1, :].unsqueeze(1).to_broadcast([P, NT - 1, D]), ALU.mult).then_inc(gated, 1)
                dve.wait_ge(gated, 2)
                nc.vector.tensor_tensor(K.x[:], K.x[:], y[:], ALU.add).then_inc(added, 1)


STEPS = 30


def phase_peer(K, layer):
    nc = K.nc
    with ExitStack() as mem:
        sb = lambda n, s: mem.enter_context(nc.sbuf_tensor(f"peer{layer}_{n}", s, F32))
        h = sb("h", [P, NT, D])
        scores = sb("scores", [P, NT, 2 * PH * NKEY])
        with ExitStack() as first:
            hT = first.enter_context(nc.sbuf_tensor(f"peer{layer}_hT", [P, KD, T], F32))
            phase_norm(K, layer, 1, h, hT)
            phase_scores(K, layer, hT, scores)
        yacc = sb("yacc", [P, NT, D])
        phase_experts(K, layer, h, scores, yacc)
        phase_gate_add(K, layer, 1, yacc, f"g{layer}_")


VEC_ROWS = [("ab_shift_w", 3 * 15), ("ab_k_k", 4), ("ab_k_a", 4), ("ab_r_k", 4), ("ab_w0", 8), ("ab_a0", 8),
            ("ab_gn_g", 4), ("ab_gn_b", 4), ("cv_b_pw1", 16), ("cv_b_dw", 8), ("cv_ln_g", 8), ("cv_ln_b", 8)]
VEC = {}
_at = 0
for _name, _n in VEC_ROWS:
    VEC[_name] = _at
    _at += _n
VEC_DW = P
TAP_ROWS = CONVW * KD // 2


def phase_vectors(K):
    nc, io = K.nc, K.io
    with ExitStack() as mem:
        rows = mem.enter_context(nc.sbuf_tensor("vec_rows", [P, 3, P], F32))
        ps = mem.enter_context(nc.psum_tensor("vec_ps", [P, 3, P], F32))
        rows_in, cleared, turned, copied = K.sem("vec_rows_in"), K.sem("vec_cleared"), K.sem("vec_turned"), K.sem("vec_copied")
        with nc.Block() as block:
            @block.sync
            def _(sp):
                sp.wait_ge(cleared, 1)
                for name, n in VEC_ROWS:
                    a = io[name]
                    dims = " ".join("abcd"[:len(a.shape)])
                    sp.dma_start(rows[VEC[name]:VEC[name] + n, 0, :],
                                 a.rearrange(f"{dims} -> ({dims})").rearrange("(n p) -> n p", p=P)).then_inc(rows_in, 16)
                taps = io["cv_w_dw"].rearrange("a w d -> (a w d)").rearrange("(j n p) -> j n p", p=P, j=2)
                for j in range(2):
                    sp.dma_start(rows[0:TAP_ROWS, 1 + j, :], taps[j]).then_inc(rows_in, 16)

            @block.vector
            def _(dve):
                nc.vector.memset(rows[:], 0.0).then_inc(cleared, 1)
                dve.wait_ge(turned, 1)
                nc.vector.tensor_copy(K.vec[:, 0:P], ps[:, 0, :]).then_inc(copied, 1)
                for j in range(2):
                    nc.vector.tensor_copy(K.vec[:, P + j * TAP_ROWS:P + (j + 1) * TAP_ROWS], ps[:, 1 + j, 0:TAP_ROWS]).then_inc(copied, 1)

            @block.tensor
            def _(pe):
                pe.wait_ge(rows_in, 16 * (len(VEC_ROWS) + 2))
                for j in range(3):
                    last = nc.tensor.transpose(ps[:, j, :], rows[:, j, :], K.ident[:])
                last.then_inc(turned, 1)


def phase_inproj(K, hT, qT, kT, vT, u):
    nc, io = K.nc, K.io
    RING, NB = 3, D_IN // P
    NA = D_AIN // P
    PAD = T + 4
    segs = [(0, T_CTX, 0), (T_CTX, T_LAT, T_CTX + 2)]
    with ExitStack() as mem:
        wring = mem.enter_context(nc.sbuf_tensor("in_wring", [P, RING, KD, P], F32))
        pad = mem.enter_context(nc.sbuf_tensor("in_pad", [P, RING, PAD], F32))
        ps = mem.enter_context(nc.psum_tensor("in_ps", [P, RING, 1024], F32))
        w_in = [K.sem(f"in_w_in{r}") for r in range(RING)]
        block_done, copied, padded, conv_step = (K.sem("in_" + n) for n in ("block_done", "copied", "padded", "conv_step"))
        w = io["ab_w_in"][0].rearrange("(k p) n -> p k n", p=P)
        wq = w[:, :, 0:D_ATTN].rearrange("p k (g c e) -> p k c g e", g=2, e=HD)
        with nc.Block() as block:
            @block.sync
            def _(sp):
                for b in range(NA):
                    r = b % RING
                    sp.wait_ge(block_done, b + 1)
                    if b < 4:
                        for g in range(2):
                            sp.dma_start(wring[:, r, :, g * HD:(g + 1) * HD], wq[:, :, b, g, :]).then_inc(w_in[r], 16)
                    else:
                        sp.dma_start(wring[:, r], w[:, :, b * P:(b + 1) * P]).then_inc(w_in[r], 32)
                with sp.Fori(0, (NB - NA) // RING) as i:
                    for r in range(RING):
                        sp.wait_ge(block_done, i * RING + (NA + r + 1))
                        sp.dma_start(wring[:, r], w[:, :, bass.ds(i * RING * P + (NA + r) * P, P)]).then_inc(w_in[r], 16)

            @block.tensor
            def _(pe):
                def project(r):
                    for k in range(KD):
                        nc.tensor.matmul(ps[:, r, SQ:512], wring[:, r, k, :], hT[:, k, 0:T_CTX], start=(k == 0), stop=(k == KD - 1))
                        last = nc.tensor.matmul(ps[:, r, 512:1024], wring[:, r, k, :], hT[:, k, T_CTX:T], start=(k == 0), stop=(k == KD - 1))
                    last.then_inc(block_done, 1)

                pe.sem_inc(block_done, RING)
                for b in range(NA):
                    pe.wait_ge(w_in[b % RING], 32 * (b // RING + 1))
                    pe.wait_ge(copied, b + 1)
                    project(b % RING)
                with pe.Fori(0, (NB - NA) // RING) as i:
                    for r in range(RING):
                        pe.wait_ge(w_in[r], i * 16 + (32 * NA // RING + 16))
                        pe.wait_ge(copied, i * RING + (NA + r + 1))
                        project(r)

            @block.scalar
            def _(act):
                act.sem_inc(copied, RING)
                for b in range(NA):
                    act.wait_ge(block_done, RING + b + 1)
                    dst = qT[:, b, :] if b < 4 else (kT, vT)[b - 4][:]
                    nc.scalar.activation(dst, ps[:, b % RING, SQ:1024], ACT.Copy, scale=HD ** -0.5 if b < 4 else 1.0).then_inc(copied, 1)
                with act.Fori(0, (NB - NA) // RING) as i:
                    for r in range(RING):
                        act.wait_ge(block_done, i * RING + (RING + NA + r + 1))
                        act.wait_ge(padded, i * RING + (r + 1))
                        nc.scalar.copy(pad[:, r, 1:1 + T_CTX], ps[:, r, SQ:512])
                        nc.scalar.copy(pad[:, r, T_CTX + 3:T + 3], ps[:, r, 512:1024]).then_inc(copied, 1)

            @block.vector
            def _(dve):
                nc.vector.memset(pad[:], 0.0).then_inc(padded, RING)
                with dve.Fori(0, (NB - NA) // RING) as i:
                    for r in range(RING):
                        dve.wait_ge(copied, i * RING + (RING + NA + r + 1))
                        for tap in range(3):
                            for n, (c, width, start) in enumerate(segs):
                                dst = u[:, bass.ds(i * RING + r, 1), c:c + width].rearrange("p a t -> p (a t)")
                                src = pad[:, r, start + tap:start + tap + width]
                                wt = K.vec[:, bass.ds(i * RING + (VEC["ab_shift_w"] + 15 * tap + r), 1)]
                                if tap == 0:
                                    ins = nc.vector.tensor_scalar(dst, src, wt, None, ALU.mult)
                                else:
                                    dve.wait_ge(conv_step, i * (RING * 6) + (r * 6 + 2 * (tap - 1) + n + 1))
                                    ins = nc.vector.scalar_tensor_tensor(dst, src, wt, dst, ALU.mult, ALU.add)
                                ins.then_inc(conv_step, 1)
                        dve.wait_ge(conv_step, i * (RING * 6) + (r * 6 + 6))
                        dve.sem_inc(padded, 1)


def phase_attention(K, qT, kT, vT, mixT):
    nc, io, ident = K.nc, K.io, K.ident
    with ExitStack() as mem:
        sb = lambda n, s, d=F32: mem.enter_context(nc.sbuf_tensor("at_" + n, s, d))
        rope, perm, mask = sb("rope", [P, 2, T_LAT]), sb("perm", [P, P]), sb("mask", [P, 7 * P])
        kctx, vctx, kcT = sb("kctx", [P, P]), sb("vctx", [P, P]), sb("kcT", [P, P])
        kvtok = sb("kvtok", [P, NT + 1, P])
        sink, rot = sb("sink", [P, HEADS]), sb("rot", [P, 2, T_LAT])
        s, pT = sb("s", [P, 2, 4 * P]), sb("pT", [P, 2, 4 * P])
        st = sb("st", [P, 2, 6])
        ps_s = mem.enter_context(nc.psum_tensor("at_ps_s", [P, 2, 512], F32))
        ps_t = mem.enter_context(nc.psum_tensor("at_ps_t", [P, 2, 512], F32))
        ps_o = mem.enter_context(nc.psum_tensor("at_ps_o", [P, 2, 512], F32))
        const_in, kv_turned, kv_copied, kv_out = (K.sem("at_" + n) for n in ("const_in", "kv_turned", "kv_copied", "kv_out"))
        rot_done, rot_step, roped = (K.sem("at_" + n) for n in ("rot_done", "rot_step", "roped"))
        s_done, masked, negated, expd, den_step, normed, p_turned, p_copied, o_done, o_copied = (
            K.sem("at_" + n) for n in ("s_done", "masked", "negated", "expd", "den_step", "normed", "p_turned", "p_copied", "o_done", "o_copied"))
        blocks = [(4, [0]), (4, [None, 1, 2]), (0, [None, 1, 2, 3]), (0, [None, 2, 3, 4]), (0, [None, 3, 4])]
        items = [(t, c, g) for t in range(NT) for c in range(4) for g in range(2)]
        with nc.Block() as block:
            @block.sync
            def _(sp):
                sp.dma_start(perm[:], K.const["ropeperm"]).then_inc(const_in, 16)
                sp.dma_start(rope[:].rearrange("p a t -> p (a t)"), K.const["rope"]).then_inc(const_in, 16)
                sp.dma_start(kctx[:], io["cache_k"][0, 0].rearrange("t g e -> t (g e)")).then_inc(const_in, 16)
                sp.dma_start(vctx[:], io["cache_v"][0, 0].rearrange("t g e -> t (g e)")).then_inc(const_in, 16)
                sp.dma_start(mask[:], K.const["amask"]).then_inc(const_in, 16)
                sp.dma_start(sink[:], io["ab_sink"][0].partition_broadcast(P)).then_inc(const_in, 16)
                sp.wait_ge(kv_copied, 3)
                sp.dma_start(K.outs[2][0, 0].rearrange("t g e -> t (g e)"), kvtok[:, NT, :]).then_inc(kv_out, 16)
                sp.dma_start(K.outs[3][0, 0].rearrange("t g e -> t (g e)"), kvtok[:, 0, :]).then_inc(kv_out, 16)
                sp.wait_ge(kv_out, 32)

            @block.tensor
            def _(pe):
                for n in range(NT + 1):
                    src = vT[:, n * P:(n + 1) * P] if n < NT else kT[:, 0:P]
                    last = nc.tensor.transpose(ps_t[:, n // 4, (n % 4) * P:(n % 4 + 1) * P], src, ident[:])
                    if n == 3:
                        last.then_inc(kv_turned, 1)
                pe.wait_ge(const_in, 96)
                nc.tensor.transpose(ps_t[:, 1, 2 * P:3 * P], kctx[:], ident[:]).then_inc(kv_turned, 1)
                for n in range(5):
                    if n >= 2:
                        pe.wait_ge(rot_step, 3 * (n - 1))
                    src = qT[:, n, T_CTX:T] if n < 4 else kT[:, T_CTX:T]
                    nc.tensor.matmul(ps_s[:, n % 2, :], perm[:], src, start=True, stop=True).then_inc(rot_done, 1)

                def scores(n):
                    t, c, g = items[n]
                    if n >= 2:
                        pe.wait_ge(masked, n - 1)
                    rows = slice(g * HD, (g + 1) * HD)
                    q = qT[rows, c, t * P:(t + 1) * P]
                    tiles = blocks[t][1]
                    at = 0
                    if tiles[0] is None:
                        nc.tensor.matmul(ps_s[:, n % 2, 0:P], q, kcT[rows, :], start=True, stop=True)
                        tiles, at = tiles[1:], P
                    width = len(tiles) * P
                    nc.tensor.matmul(ps_s[:, n % 2, at:at + width], q, kT[rows, tiles[0] * P:tiles[0] * P + width],
                                     start=True, stop=True).then_inc(s_done, 1)

                def turn(n):
                    pe.wait_ge(normed, n + 1)
                    if n >= 2:
                        pe.wait_ge(p_copied, n - 1)
                    for b in range(len(blocks[items[n][0]][1])):
                        last = nc.tensor.transpose(ps_t[:, n % 2, b * P:(b + 1) * P], s[:, n % 2, b * P:(b + 1) * P], ident[:])
                    last.then_inc(p_turned, 1)

                def weigh(n):
                    t, c, g = items[n]
                    pe.wait_ge(p_copied, n + 1)
                    if c == 0 and g == 0 and t >= 2:
                        pe.wait_ge(o_copied, t - 1)
                    tiles = blocks[t][1]
                    for b, kt in enumerate(tiles):
                        v = vctx[:, g * HD:(g + 1) * HD] if kt is None else kvtok[:, kt, g * HD:(g + 1) * HD]
                        last = nc.tensor.matmul(ps_o[g * HD:(g + 1) * HD, t % 2, c * P:(c + 1) * P], v, pT[:, n % 2, b * P:(b + 1) * P],
                                                start=(b == 0), stop=(b == len(tiles) - 1))
                    last.then_inc(o_done, 1)

                pe.wait_ge(roped, 5)
                pe.wait_ge(kv_copied, 3)
                N = len(items)
                for n in range(N + 2):
                    if n < N:
                        scores(n)
                    if 1 <= n <= N:
                        turn(n - 1)
                    if n >= 2:
                        weigh(n - 2)

            @block.vector
            def _(dve):
                dve.wait_ge(const_in, 96)
                for n in range(5):
                    dst = qT[:, n, T_CTX:T] if n < 4 else kT[:, T_CTX:T]
                    dve.wait_ge(rot_done, n + 1)
                    if n == 4:
                        dve.wait_ge(kv_turned, 1)
                    if n >= 2:
                        dve.wait_ge(roped, n - 1)
                    nc.vector.tensor_tensor(rot[:, n % 2, :], ps_s[:, n % 2, :], rope[:, 1, :], ALU.mult).then_inc(rot_step, 1)
                    nc.vector.tensor_tensor(dst, dst, rope[:, 0, :], ALU.mult).then_inc(rot_step, 1)
                    dve.wait_ge(rot_step, 3 * n + 2)
                    nc.vector.sem_inc(rot_step, 1)
                    nc.vector.tensor_tensor(dst, dst, rot[:, n % 2, :], ALU.add).then_inc(roped, 1)
                for n, (t, c, g) in enumerate(items):
                    p = n % 2
                    first, tiles = blocks[t]
                    width = len(tiles) * P
                    dve.wait_ge(s_done, n + 1)
                    if n >= 2:
                        dve.wait_ge(p_turned, n - 1)
                    nc.vector.tensor_tensor_reduce(out=s[:, p, 0:width], in0=ps_s[:, p, 0:width], in1=mask[:, first * P:first * P + width], scale=1.0,
                                                   scalar=sink[:, g * 4 + c:g * 4 + c + 1], op0=ALU.add, op1=ALU.max,
                                                   accum_out=st[:, p, 0:1]).then_inc(masked, 1)
                    dve.wait_ge(masked, n + 1)
                    nc.vector.tensor_scalar(st[:, p, 1:2], st[:, p, 0:1], -1.0, None, ALU.mult).then_inc(negated, 1)
                    dve.wait_ge(expd, 2 * (n + 1))
                    nc.vector.tensor_tensor(st[:, p, 4:5], st[:, p, 2:3], st[:, p, 3:4], ALU.add).then_inc(den_step, 1)
                    dve.wait_ge(den_step, 2 * n + 1)
                    nc.vector.reciprocal(st[:, p, 5:6], st[:, p, 4:5]).then_inc(den_step, 1)
                    dve.wait_ge(den_step, 2 * n + 2)
                    nc.vector.tensor_scalar(s[:, p, 0:width], s[:, p, 0:width], st[:, p, 5:6], None, ALU.mult).then_inc(normed, 1)

            @block.scalar
            def _(act):
                act.wait_ge(kv_turned, 1)
                nc.scalar.copy(kvtok[:, 0:4, :].rearrange("p t c -> p (t c)"), ps_t[:, 0, :]).then_inc(kv_copied, 1)
                act.wait_ge(kv_turned, 2)
                nc.scalar.copy(kvtok[:, 4:6, :].rearrange("p t c -> p (t c)"), ps_t[:, 1, 0:2 * P]).then_inc(kv_copied, 1)
                nc.scalar.copy(kcT[:], ps_t[:, 1, 2 * P:3 * P]).then_inc(kv_copied, 1)

                def copy_p(n):
                    width = len(blocks[items[n][0]][1]) * P
                    act.wait_ge(p_turned, n + 1)
                    if n >= 2:
                        act.wait_ge(o_done, n - 1)
                    nc.scalar.copy(pT[:, n % 2, 0:width], ps_t[:, n % 2, 0:width]).then_inc(p_copied, 1)

                def copy_o(t):
                    act.wait_ge(o_done, 8 * (t + 1))
                    nc.scalar.copy(mixT[:, 0:4, t * P:(t + 1) * P], ps_o[:, t % 2, :].rearrange("p (c q) -> p c q", c=4)).then_inc(o_copied, 1)

                N = len(items)
                for n in range(N):
                    t, c, g = items[n]
                    p, width = n % 2, len(blocks[t][1]) * P
                    act.wait_ge(negated, n + 1)
                    nc.scalar.activation(s[:, p, 0:width], s[:, p, 0:width], ACT.Exp, bias=st[:, p, 1:2], accum_out=st[:, p, 2:3]).then_inc(expd, 1)
                    nc.scalar.activation(st[:, p, 3:4], sink[:, g * 4 + c:g * 4 + c + 1], ACT.Exp, bias=st[:, p, 1:2]).then_inc(expd, 1)
                    if n >= 1:
                        copy_p(n - 1)
                    if n >= 10 and n % 8 == 2:
                        copy_o(n // 8 - 1)
                copy_p(N - 1)
                copy_o(NT - 1)


def mm640(nc, ps, b, lhsT, rhs):
    nc.tensor.matmul(ps[:, b, SQ:512], lhsT, rhs[:, 0:T_CTX], start=True, stop=True)
    return nc.tensor.matmul(ps[:, b, 512:1024], lhsT, rhs[:, T_CTX:T], start=True, stop=True)


def phase_scan_prep(K, u, q1, q2, k1, k2, pc, mixT):
    nc, io = K.nc, K.io
    NCK = T // CH
    N = 2 * NCC
    with ExitStack() as mem:
        sb = lambda n, s, d=F32: mem.enter_context(nc.sbuf_tensor("sp_" + n, s, d))
        w2, a2, g2 = sb("w2", [P, D_RW]), sb("a2", [P, D_RW]), sb("g2", [P, D_RW])
        hsum, reset = sb("hsum", [P, P]), sb("reset", [P, T])
        oneka, rkh = sb("oneka", [P, NCC]), sb("rkh", [P, NCC])
        kh, sq, nrm, a, kt, ktsum = (sb(n, [P, T]) for n in ("kh", "sq", "nrm", "a", "kt", "ktsum"))
        ld, cs, ce, en = (sb(n, [P, T]) for n in ("ld", "cs", "ce", "en"))
        ps = mem.enter_context(nc.psum_tensor("sp_ps", [P, 4, 1024], F32))
        S = {n: K.sem("sp_" + n) for n in ("par_in", "own", "lora_done", "kk_done", "sq_done", "n2_done", "root_done",
                                           "z_done", "az_done", "sig_done", "a_done", "c_ready", "exps_done", "ops_done",
                                           "g_done", "g_copied", "bonus_prod", "bonus_sum")}
        vcol = lambda name, j: K.vec[:, VEC[name] + j:VEC[name] + j + 1]
        with nc.Block() as block:
            @block.sync
            def _(sp):
                sp.dma_start(w2[:], io["ab_w2"][0].rearrange("d r c -> (d r) c")).then_inc(S["par_in"], 16)
                sp.dma_start(a2[:], io["ab_a2"][0].rearrange("d r c -> (d r) c")).then_inc(S["par_in"], 16)
                sp.dma_start(g2[:], io["ab_g2"][0]).then_inc(S["par_in"], 16)
                sp.dma_start(hsum[:], K.const["headsum"]).then_inc(S["par_in"], 16)
                sp.dma_start(reset[:], K.const["reset"]).then_inc(S["par_in"], 16)

            @block.tensor
            def _(pe):
                pe.wait_ge(S["par_in"], 80)
                pe.wait_ge(S["lora_done"], 2)
                for cc in range(NCC):
                    cols = slice(cc * P, (cc + 1) * P)
                    pe.wait_ge(S["sq_done"], cc + 1)
                    mm640(nc, ps, 0, hsum[:], sq).then_inc(S["n2_done"], 1)
                    for d in range(2):
                        n, rows = 2 * cc + d, slice(64 * d, 64 * d + 64)
                        if n:
                            pe.wait_ge(S["sig_done"], n)
                            pe.wait_ge(S["a_done"], n)
                        mm640(nc, ps, 1, w2[rows, cols], u[rows, 12, :]).then_inc(S["z_done"], 1)
                        mm640(nc, ps, 2, a2[rows, cols], u[rows, 13, :]).then_inc(S["az_done"], 1)
                    if cc:
                        pe.wait_ge(S["g_copied"], cc)
                    mm640(nc, ps, 3, g2[:, cols], u[:, 14, :]).then_inc(S["g_done"], 1)
                    pe.wait_ge(S["bonus_prod"], cc + 1)
                    mm640(nc, ps, 0, hsum[:], ktsum).then_inc(S["bonus_sum"], 1)

            @block.scalar
            def _(act):
                nc.scalar.activation(u[:, 12, :], u[:, 12, :], ACT.Tanh).then_inc(S["lora_done"], 1)
                nc.scalar.activation(u[:, 14, :], u[:, 14, :], ACT.Sigmoid).then_inc(S["lora_done"], 1)
                for cc in range(NCC):
                    act.wait_ge(S["kk_done"], cc + 1)
                    nc.scalar.activation(sq[:], kh[:], ACT.Square).then_inc(S["sq_done"], 1)
                    act.wait_ge(S["n2_done"], cc + 1)
                    nc.scalar.activation(nrm[:], ps[:, 0, SQ:1024], ACT.Sqrt).then_inc(S["root_done"], 1)
                    for d in range(2):
                        n = 2 * cc + d
                        if n:
                            act.wait_ge(S["ops_done"], n)
                        act.wait_ge(S["z_done"], n + 1)
                        nc.scalar.activation(ld[:], ps[:, 1, SQ:1024], ACT.Sigmoid, bias=vcol("ab_w0", 4 * d + cc)).then_inc(S["sig_done"], 1)
                        act.wait_ge(S["az_done"], n + 1)
                        nc.scalar.activation(a[:], ps[:, 2, SQ:1024], ACT.Sigmoid, bias=vcol("ab_a0", 4 * d + cc)).then_inc(S["a_done"], 1)
                        act.wait_ge(S["c_ready"], n + 1)
                        nc.scalar.activation(ce[:], ce[:], ACT.Exp).then_inc(S["exps_done"], 1)
                        nc.scalar.activation(en[:], cs[:], ACT.Exp, scale=-1.0).then_inc(S["exps_done"], 1)
                        nc.scalar.activation(q2[:, d, cc, :], cs[:], ACT.Exp).then_inc(S["exps_done"], 1)
                    act.wait_ge(S["g_done"], cc + 1)
                    nc.scalar.copy(mixT[:, 4 + cc, :], ps[:, 3, SQ:1024]).then_inc(S["g_copied"], 1)

            @block.vector
            def _(dve):
                step = chain_on(dve, S["own"])
                step(nc.vector.tensor_scalar(oneka[:], K.vec[:, VEC["ab_k_a"]:VEC["ab_k_a"] + NCC], -1.0, 1.0, ALU.mult, ALU.add), False)
                step(nc.vector.tensor_scalar(rkh[:], K.vec[:, VEC["ab_r_k"]:VEC["ab_r_k"] + NCC], 0.5, None, ALU.mult))
                dve.wait_ge(S["par_in"], 80)
                for cc in range(NCC):
                    r, k, v = u[:, cc, :], u[:, 4 + cc, :], u[:, 8 + cc, :]
                    nc.vector.tensor_scalar(kh[:], k, vcol("ab_k_k", cc), None, ALU.mult).then_inc(S["kk_done"], 1)
                    dve.wait_ge(S["root_done"], cc + 1)
                    step(nc.vector.tensor_scalar(nrm[:], nrm[:], 1e-12, None, ALU.max))
                    step(nc.vector.reciprocal(nrm[:], nrm[:]))
                    step(nc.vector.tensor_tensor(kh[:], kh[:], nrm[:], ALU.mult))
                    for d in range(2):
                        n = 2 * cc + d
                        kd = ktsum if d == 0 else kt
                        dve.wait_ge(S["sig_done"], n + 1)
                        step(nc.vector.tensor_scalar(ld[:], ld[:], -float(np.exp(-0.5)), None, ALU.mult))
                        step(nc.vector.tensor_tensor_scan(cs[:], reset[:], ld[:], 0.0, ALU.mult, ALU.add))
                        if d == 0:
                            nc.vector.tensor_tensor(ce[:], cs[:], ld[:], ALU.subtract).then_inc(S["c_ready"], 1)
                        else:
                            c3, e3 = (b[:].rearrange("p (n c) -> p n c", c=CH) for b in (cs, ce))
                            step(nc.vector.tensor_tensor(e3, c3[:, :, CH - 1:CH].to_broadcast([P, NCK, CH]), c3, ALU.subtract))
                            nc.vector.tensor_tensor(cs[:], ce[:], ld[:], ALU.add).then_inc(S["c_ready"], 1)
                        dve.wait_ge(S["a_done"], n + 1)
                        step(nc.vector.tensor_scalar(kd[:], a[:], vcol("ab_k_a", cc), oneka[:, cc:cc + 1], ALU.mult, ALU.add), False)
                        step(nc.vector.tensor_tensor(a[:], a[:], kh[:], ALU.mult))
                        step(nc.vector.tensor_tensor(kd[:], kd[:], k, ALU.mult))
                        dve.wait_ge(S["exps_done"], 3 * (n + 1))
                        last = CH - 1 if d == 0 else 0
                        step(nc.vector.tensor_copy(pc[:, :, d, cc], q2[:, d, cc, :].rearrange("p (n c) -> p n c", c=CH)[:, :, last]), False)
                        step(nc.vector.tensor_tensor(k1[:, d, cc, :], a[:], en[:], ALU.mult), False)
                        step(nc.vector.tensor_tensor(k2[:, d, cc, :], kd[:], en[:], ALU.mult), False)
                        step(nc.vector.tensor_tensor(q1[:, d, cc, :], kh[:], ce[:], ALU.mult))
                        nc.vector.tensor_tensor(q2[:, d, cc, :], q2[:, d, cc, :], r, ALU.mult).then_inc(S["ops_done"], 1)
                    dve.wait_ge(S["ops_done"], 2 * cc + 2)
                    step(nc.vector.tensor_tensor(ktsum[:], ktsum[:], kt[:], ALU.add))
                    nc.vector.scalar_tensor_tensor(ktsum[:], ktsum[:], rkh[:, cc:cc + 1], r, ALU.mult, ALU.mult).then_inc(S["bonus_prod"], 1)
                    dve.wait_ge(S["bonus_sum"], cc + 1)
                    step(nc.vector.tensor_tensor(r, ps[:, 0, SQ:1024], v, ALU.mult))


def phase_scan(K, tag, first, chunks, u, q1, q2, k1, k2, pc, state_in, state_out):
    nc = K.nc
    G = 2
    LEVELS = 5
    PE_N, ACT_N, DVE_N, POOL_N = 8 + 3 * LEVELS + 4, 2 + LEVELS + 3, 5 + LEVELS + 2, 8
    with ExitStack() as mem:
        sb = lambda n, s=(P, G, NCC, CH), d=F32: mem.enter_context(nc.sbuf_tensor(f"sc{tag}_{n}", list(s), d))
        q1c, q2c, k1c, k2c, vc = sb("q1c"), sb("q2c"), sb("k1c"), sb("k2c"), sb("vc")
        pair = (P, G, 2, NCC, CH)
        AA, BD, XX = sb("AA", pair), sb("BD", pair), sb("XX", pair)
        A, AT, BT, DT, X, XT = (b[:, :, w] for b in (AA, BD, XX) for w in range(2))
        ET, V, k1T, k2T = sb("ET"), sb("V"), sb("k1T"), sb("k2T")
        M, W, U, S, Sn = sb("M"), sb("W"), sb("U"), sb("S"), sb("Sn")
        pcc = sb("pcc", (P, G, NCC))
        eye = sb("eye", (P, CH))
        smask = sb("smask", (P, 5, G, CH))
        lmask = sb("lmask", (P, 1 + LEVELS, 2, G, CH), mybir.dt.uint8)
        ps = mem.enter_context(nc.psum_tensor(f"sc{tag}_ps", [P, G, 4, 2, NCC, CH], F32))
        const_in = K.sem(f"sc{tag}_const_in")
        state_ready, state_turned, state_sent = (K.sem(f"sc{tag}_" + n) for n in ("state_ready", "state_turned", "state_sent"))
        pool_done, pe_done, act_done, dve_done = ([K.sem(f"sc{tag}_{e}{g}") for g in range(G)] for e in ("pool", "pe", "act", "dve"))
        LM = (1 + LEVELS) * 2 * G * CH // 2
        masks_set = K.sem(f"sc{tag}_masks_set")
        carried = K.sem(f"sc{tag}_carried")
        state_done = K.sem(f"sc{tag}_state_done")
        region = lambda g, r: ps[:, g, r // 2, r % 2]

        PE_W = 8 + 3 * LEVELS
        ACT_W = 2 + LEVELS
        DVE_S = 5 + LEVELS
        after_pe = lambda eng, g, i, k: eng.wait_ge(pe_done[g], i * PE_N + (PE_N + k))
        after_act = lambda eng, g, i, k: eng.wait_ge(act_done[g], i * ACT_N + (ACT_N + k))
        after_dve = lambda eng, g, i, k: eng.wait_ge(dve_done[g], i * DVE_N + (DVE_N + k))
        after_pool = lambda eng, g, i, k: eng.wait_ge(pool_done[g], i * POOL_N + (POOL_N + k))
        start = lambda g, i: i * CH + first if g == 0 else i * (-CH) + (first + (chunks - 1) * CH)
        number = lambda g, i: i + first // CH if g == 0 else i * -1 + (first // CH + chunks - 1)

        with nc.Block() as block:
            def state_rows(dram, d, e):
                return dram[0, 0, d].rearrange("(c e) v k -> e v c k", e=2)[e]

            @block.sync
            def _(sp):
                sp.dma_start(smask[:].rearrange("p a g c -> p (a g c)"), K.const["scanmask"]).then_inc(const_in, 16)
                for n, buf in enumerate((AA, BD)):
                    sp.dma_start(buf[:].rearrange("p g w c t -> p (g w c t)")[:, 0:LM], K.const["levmask"][:, n * LM:(n + 1) * LM]).then_inc(const_in, 16)
                sp.dma_start(eye[:], K.const["eye64"]).then_inc(const_in, 16)
                if state_in is not None:
                    for d in range(G):
                        for e in range(2):
                            sp.dma_start(Sn[64 * e:64 * e + 64, d], state_rows(state_in, d, e)).then_inc(const_in, 16)
                if state_out is not None:
                    sp.wait_ge(state_sent, 1)
                    for d in range(G):
                        for e in range(2):
                            sp.dma_start(state_rows(state_out, d, e), W[64 * e:64 * e + 64, d]).then_inc(state_done, 16)
                    sp.wait_ge(state_done, 64)

            N_CONST = 64 + (64 if state_in is not None else 0)

            @block.gpsimd
            def _(pool):
                pool.wait_ge(const_in, N_CONST)
                for g in range(G):
                    pool.sem_inc(pool_done[g], POOL_N)
                with pool.Fori(0, chunks) as i:
                    for g in range(G):
                        cols, num = bass.ds(start(g, i), CH), number(g, i)
                        after_pe(pool, g, i, -PE_N + PE_W + 3)
                        nc.gpsimd.tensor_copy(k1c[:, g], k1[:, g, :, cols]).then_inc(pool_done[g], 1)
                        nc.gpsimd.tensor_copy(k2c[:, g], k2[:, g, :, cols]).then_inc(pool_done[g], 1)
                        nc.gpsimd.tensor_copy(q1c[:, g], q1[:, g, :, cols]).then_inc(pool_done[g], 1)
                        nc.gpsimd.tensor_copy(q2c[:, g], q2[:, g, :, cols]).then_inc(pool_done[g], 1)
                        nc.gpsimd.tensor_copy(vc[:, g], u[:, 8:12, cols]).then_inc(pool_done[g], 1)
                        after_dve(pool, g, i, 0)
                        nc.gpsimd.tensor_copy(pcc[:, g], pc[:, bass.ds(num, 1), g, :].rearrange("p a c -> p (a c)")).then_inc(pool_done[g], 1)
                        for buf in (X, XT):
                            nc.gpsimd.tensor_copy(buf[:, g], eye[:].unsqueeze(1).to_broadcast([P, NCC, CH])).then_inc(pool_done[g], 1)

            @block.tensor
            def _(pe):
                def heads(g, r, *terms, n_chunk=0):
                    if n_chunk is not None:
                        pe.sem_inc(carried, 1)
                    for c in range(NCC):
                        for e in range(2):
                            rows = slice(64 * e, 64 * e + 64)
                            for n, (l, m) in enumerate(terms):
                                last = nc.tensor.matmul(region(g, r)[rows, c, :], l[rows] if l is eye else l[rows, g, c, :],
                                                        m[rows] if m is eye else m[rows, g, c, :],
                                                        start=(n == 0), stop=(n == len(terms) - 1))
                    last.then_inc(pe_done[g], 1)

                pe.wait_ge(const_in, N_CONST)
                if state_in is not None:
                    for g in range(G):
                        for c in range(NCC):
                            for e in range(2):
                                rows = slice(64 * e, 64 * e + 64)
                                last = nc.tensor.matmul(region(g, 0)[rows, c, :], Sn[rows, g, c, :], eye[rows], start=True, stop=True)
                    last.then_inc(state_turned, 1)
                for g in range(G):
                    pe.sem_inc(pe_done[g], PE_N)
                pe.wait_ge(state_ready, 1)
                with pe.Fori(0, chunks) as i:
                    for g in range(G):
                        after_act(pe, g, i, 0)
                        after_dve(pe, g, i, 0)
                        after_pool(pe, g, i, 5)
                        heads(g, 0, (q1c, k1c))
                        for r, term in enumerate(((k1c, q1c), (k2c, q1c), (k2c, q2c), (k1c, q2c), (vc, eye), (k1c, eye), (k2c, eye))):
                            heads(g, 1 + r, term, n_chunk=None)
                    for l in range(LEVELS):
                        for g in range(G):
                            after_dve(pe, g, i, 5 + l)
                            heads(g, 0, (AT, X))
                        for g in range(G):
                            after_act(pe, g, i, 2 + l + 1)
                            heads(g, 2, (XT, M))
                            heads(g, 3, (M, XT), n_chunk=None)
                    for g in range(G):
                        after_dve(pe, g, i, DVE_S)
                        heads(g, 4, (q1c, S), (BT, V))
                    for g in range(G):
                        after_act(pe, g, i, ACT_W + 1)
                        heads(g, 6, (XT, W))
                    for g in range(G):
                        after_act(pe, g, i, ACT_W + 2)
                        heads(g, 0, (S, q2c), (V, DT), (U, ET))
                        heads(g, 2, (k2T, V), (k1T, U), n_chunk=None)
                if state_out is not None:
                    for g in range(G):
                        pe.wait_ge(dve_done[g], DVE_N * (chunks + 1))
                        pe.wait_ge(act_done[g], ACT_N * (chunks + 1))
                        for c in range(NCC):
                            for e in range(2):
                                rows = slice(64 * e, 64 * e + 64)
                                last = nc.tensor.matmul(region(g, 0)[rows, c, :], S[rows, g, c, :], eye[rows], start=True, stop=True)
                    last.then_inc(state_turned, 1)

            @block.scalar
            def _(act):
                act.wait_ge(const_in, N_CONST)
                for g in range(G):
                    act.sem_inc(act_done[g], ACT_N)
                with act.Fori(0, chunks) as i:
                    for g in range(G):
                        for k, (buf, scale) in enumerate(((k1T, -1.0), (k2T, 1.0))):
                            after_pe(act, g, i, 8)
                            nc.scalar.activation(buf[:, g], region(g, 6 + k), ACT.Copy, scale=scale).then_inc(act_done[g], 1)
                    for l in range(LEVELS):
                        for g in range(G):
                            after_pe(act, g, i, 8 + 3 * l + 1)
                            nc.scalar.copy(M[:, g], region(g, 0)).then_inc(act_done[g], 1)
                    for g in range(G):
                        after_pe(act, g, i, PE_W + 1)
                        nc.scalar.copy(W[:, g], region(g, 4)).then_inc(act_done[g], 1)
                    for g in range(G):
                        after_pe(act, g, i, PE_W + 2)
                        nc.scalar.copy(U[:, g], region(g, 6)).then_inc(act_done[g], 1)
                    for g in range(G):
                        after_pe(act, g, i, PE_W + 3)
                        after_pool(act, g, i, 4)
                        nc.scalar.copy(q2[:, g, :, bass.ds(start(g, i), CH)], region(g, 0)).then_inc(act_done[g], 1)
                if state_out is not None:
                    act.wait_ge(state_turned, 1)
                    nc.scalar.copy(W[:], ps[:, :, 0, 0]).then_inc(state_sent, 1)

            @block.vector
            def _(dve):
                dve.wait_ge(const_in, N_CONST)
                for n, buf in enumerate((AA, BD)):
                    nc.vector.tensor_copy(lmask[:].rearrange("p l w g c -> p (l w g c)")[:, n * LM:(n + 1) * LM],
                                          buf[:].rearrange("p g w c t -> p (g w c t)")[:, 0:LM]).then_inc(masks_set, 1)
                dve.wait_ge(masks_set, 2)
                if state_in is None:
                    nc.vector.memset(S[:], 0.0).then_inc(state_ready, 1)
                else:
                    dve.wait_ge(state_turned, 1)
                    nc.vector.tensor_copy(S[:], ps[:, :, 0, 0]).then_inc(state_ready, 1)
                for g in range(G):
                    dve.sem_inc(dve_done[g], DVE_N)
                dve.wait_ge(state_ready, 1)
                with dve.Fori(0, chunks) as i:
                    for g in range(G):
                        both = lambda b: ps[:, g, b]
                        for k, buf in enumerate((AA, BD)):
                            after_pe(dve, g, i, 2 * k + 2)
                            nc.vector.tensor_tensor(buf[:, g], both(k), smask[:, 2 * k:2 * k + 2, g].unsqueeze(2).to_broadcast([P, 2, NCC, CH]),
                                                    ALU.mult).then_inc(dve_done[g], 1)
                        after_pe(dve, g, i, 6)
                        nc.vector.tensor_tensor(ET[:, g], region(g, 4), smask[:, 4, g].unsqueeze(1).to_broadcast([P, NCC, CH]), ALU.mult).then_inc(dve_done[g], 1)
                        nc.vector.tensor_copy(V[:, g], region(g, 5)).then_inc(dve_done[g], 1)
                        after_pool(dve, g, i, 8)
                        after_dve(dve, g, i, 1)
                        dve.sem_inc(carried, 1)
                        nc.vector.copy_predicated(XX[:, g], lmask[:, 0, :, g].unsqueeze(2).to_broadcast([P, 2, NCC, CH]), AA[:, g]).then_inc(dve_done[g], 1)
                    for l in range(LEVELS):
                        for g in range(G):
                            after_pe(dve, g, i, 8 + 3 * l + 3)
                            after_dve(dve, g, i, 5 + l)
                            dve.sem_inc(carried, 1)
                            nc.vector.copy_predicated(XX[:, g], lmask[:, l + 1, :, g].unsqueeze(2).to_broadcast([P, 2, NCC, CH]),
                                                      ps[:, g, 1]).then_inc(dve_done[g], 1)
                    for g in range(G):
                        after_pe(dve, g, i, PE_W + 4)
                        nc.vector.tensor_tensor(Sn[:, g], S[:, g], region(g, 2), ALU.add).then_inc(dve_done[g], 1)
                        after_dve(dve, g, i, DVE_S + 1)
                        nc.vector.tensor_tensor(S[:, g], Sn[:, g], pcc[:, g].unsqueeze(2).to_broadcast([P, NCC, CH]), ALU.mult).then_inc(dve_done[g], 1)


def phase_scan_out(K, u, q2, mixT):
    nc = K.nc
    with ExitStack() as mem:
        sb = lambda n, s, d=F32: mem.enter_context(nc.sbuf_tensor("so_" + n, s, d))
        hmean = sb("hmean", [P, P])
        y, sq, sd = sb("y", [P, NCC, T]), sb("sq", [P, NCC, T]), sb("sd", [P, NCC, T])
        ps = mem.enter_context(nc.psum_tensor("so_ps", [P, 4, 1024], F32))
        S = {n: K.sem("so_" + n) for n in ("hsum_in", "own", "mean_const", "y_done", "mean_done", "centred", "squared", "var_done", "root_done")}
        with nc.Block() as block:
            @block.sync
            def _(sp):
                sp.dma_start(hmean[:], K.const["headsum"]).then_inc(S["hsum_in"], 16)

            @block.tensor
            def _(pe):
                pe.wait_ge(S["mean_const"], 1)
                for cc in range(NCC):
                    pe.wait_ge(S["y_done"], cc + 1)
                    if cc >= 2:
                        pe.wait_ge(S["centred"], cc - 1)
                    mm640(nc, ps, cc % 2, hmean[:], y[:, cc, :]).then_inc(S["mean_done"], 1)
                for cc in range(NCC):
                    pe.wait_ge(S["squared"], cc + 1)
                    if cc >= 2:
                        pe.wait_ge(S["root_done"], cc - 1)
                    mm640(nc, ps, 2 + cc % 2, hmean[:], sq[:, cc, :]).then_inc(S["var_done"], 1)

            @block.scalar
            def _(act):
                for cc in range(NCC):
                    act.wait_ge(S["centred"], cc + 1)
                    nc.scalar.activation(sq[:, cc, :], y[:, cc, :], ACT.Square).then_inc(S["squared"], 1)
                for cc in range(NCC):
                    act.wait_ge(S["var_done"], cc + 1)
                    nc.scalar.activation(sd[:, cc, :], ps[:, 2 + cc % 2, SQ:1024], ACT.Sqrt, bias=K.gneps[:, 0:1]).then_inc(S["root_done"], 1)

            @block.vector
            def _(dve):
                step = chain_on(dve, S["own"])
                dve.wait_ge(S["hsum_in"], 16)
                nc.vector.tensor_scalar(hmean[:], hmean[:], 1.0 / HD, None, ALU.mult).then_inc(S["mean_const"], 1)
                for cc in range(NCC):
                    nc.vector.tensor_tensor(y[:, cc, :], q2[:, 0, cc, :], q2[:, 1, cc, :], ALU.add).then_inc(S["y_done"], 1)
                for cc in range(NCC):
                    dve.wait_ge(S["mean_done"], cc + 1)
                    nc.vector.tensor_tensor(y[:, cc, :], y[:, cc, :], ps[:, cc % 2, SQ:1024], ALU.subtract).then_inc(S["centred"], 1)
                for cc in range(NCC):
                    g, b = (K.vec[:, VEC[n] + cc:VEC[n] + cc + 1] for n in ("ab_gn_g", "ab_gn_b"))
                    out = mixT[:, 4 + cc, :]
                    dve.wait_ge(S["root_done"], cc + 1)
                    step(nc.vector.reciprocal(sd[:, cc, :], sd[:, cc, :]))
                    step(nc.vector.tensor_tensor(y[:, cc, :], y[:, cc, :], sd[:, cc, :], ALU.mult))
                    step(nc.vector.tensor_scalar(y[:, cc, :], y[:, cc, :], g, b, ALU.mult, ALU.add))
                    step(nc.vector.tensor_tensor(y[:, cc, :], y[:, cc, :], u[:, cc, :], ALU.add))
                    step(nc.vector.tensor_tensor(out, out, y[:, cc, :], ALU.mult))


def phase_outproj(K, tag, srcT, load_w, w_total, layer, bias=None):
    nc = K.nc
    with ExitStack() as mem:
        sb = lambda n, s, d=F32: mem.enter_context(nc.sbuf_tensor(tag + n, s, d))
        w = sb("w", [P, KD, D])
        rows = sb("rows", [P, 2, D])
        brow = sb("brow", [P, D])
        y = sb("y", [P, NT, D])
        ps = mem.enter_context(nc.psum_tensor(tag + "ps", [P, 4, D], F32))
        w_in, rows_in, y_done, own = (K.sem(tag + n) for n in ("w_in", "rows_in", "y_done", "own"))
        gated = K.sem(tag + "gated")
        with nc.Block() as block:
            @block.sync
            def _(sp):
                load_w(sp, w, w_in)
                for s in range(2):
                    load_row(sp, K, rows[:, s, :], s, layer, 2, rows_in)
                if bias is not None:
                    sp.dma_start(brow[:], bias.partition_broadcast(P)).then_inc(rows_in, 16)
            @block.tensor
            def _(pe):
                pe.wait_ge(w_in, w_total)
                for t in range(NT):
                    if t >= 4:
                        pe.wait_ge(gated, t - 3)
                    for half in range(2):
                        for k in range(KD):
                            last = nc.tensor.matmul(ps[:, t % 4, half * 512:(half + 1) * 512], srcT[:, k, t * P:(t + 1) * P],
                                                    w[:, k, half * 512:(half + 1) * 512], start=(k == 0), stop=(k == KD - 1))
                    last.then_inc(y_done, 1)

            @block.vector
            def _(dve):
                step = chain_on(dve, own)
                dve.wait_ge(rows_in, 32 if bias is None else 48)
                for t in range(NT):
                    dve.wait_ge(y_done, t + 1)
                    if bias is None:
                        nc.vector.tensor_tensor(y[:, t, :], ps[:, t % 4, :], rows[:, min(t, 1), :], ALU.mult).then_inc(gated, 1)
                        dve.wait_ge(gated, t + 1)
                    else:
                        nc.vector.tensor_tensor(y[:, t, :], ps[:, t % 4, :], brow[:], ALU.add).then_inc(gated, 1)
                        dve.wait_ge(gated, t + 1)
                        step(nc.vector.tensor_tensor(y[:, t, :], y[:, t, :], rows[:, min(t, 1), :], ALU.mult))
                    step(nc.vector.tensor_tensor(K.x[:, t, :], K.x[:, t, :], y[:, t, :], ALU.add))


def load_w_out(K):
    w = K.io["ab_w_out"][0]

    def load(eng, dst, sem):
        for k in range(KD):
            for g in range(2):
                row = (k * HD + g * D_ATTN // 2) if k < 4 else k * P + g * HD
                eng.dma_start(dst[g * HD:(g + 1) * HD, k, :], w[row:row + HD, :]).then_inc(sem, 16)
    return load


def phase_mixer_even(K):
    nc = K.nc
    with ExitStack() as mem:
        sb = lambda s, n, shape: s.enter_context(nc.sbuf_tensor("ev_" + n, shape, F32))
        mixT = sb(mem, "mixT", [P, KD, T])
        with ExitStack() as mixing:
            u = sb(mixing, "u", [P, 15, T])
            with ExitStack() as first:
                qT, kT, vT = sb(first, "qT", [P, 4, T]), sb(first, "kT", [P, T]), sb(first, "vT", [P, T])
                with ExitStack() as normed:
                    hT = sb(normed, "hT", [P, KD, T])
                    with ExitStack() as token:
                        h = sb(token, "h", [P, NT, D])
                        phase_norm(K, 0, 0, h, hT)
                    phase_inproj(K, hT, qT, kT, vT, u)
                phase_attention(K, qT, kT, vT, mixT)
            q1, q2, k1, k2 = (sb(mixing, n, [P, 2, NCC, T]) for n in ("q1", "q2", "k1", "k2"))
            pc = sb(mixing, "pc", [P, T // CH, 2, NCC])
            phase_scan_prep(K, u, q1, q2, k1, k2, pc, mixT)
            phase_scan(K, "p", 0, T_CTX // CH, u, q1, q2, k1, k2, pc, None, K.outs[4])
            phase_scan(K, "l", T_CTX, T_LAT // CH, u, q1, q2, k1, k2, pc, K.io["state_rwkv"], None)
            phase_scan_out(K, u, q2, mixT)
        phase_outproj(K, "wo_", mixT, load_w_out(K), 2 * KD * 16, 0)


CPAD = T + 4 * PADC
CSEGS = [(0, T_CTX, 0), (T_CTX, T_LAT, T_CTX + 2 * PADC)]


def phase_glu(K, hT, glu):
    nc, io = K.nc, K.io
    RING = 2
    with ExitStack() as mem:
        wring = mem.enter_context(nc.sbuf_tensor("gl_wring", [P, RING, 2, KD, P], F32))
        sg = mem.enter_context(nc.sbuf_tensor("gl_sg", [P, RING, T], F32))
        ps = mem.enter_context(nc.psum_tensor("gl_ps", [P, 2 * RING, 1024], F32))
        w_in = [K.sem(f"gl_w_in{r}") for r in range(RING)]
        block_done, sig_done, glu_done = (K.sem("gl_" + n) for n in ("block_done", "sig_done", "glu_done"))
        w = io["cv_w_pw1"][0].rearrange("(k p) n -> p k n", p=P)
        bias = VEC["cv_b_pw1"]
        with nc.Block() as block:
            @block.sync
            def _(sp):
                with sp.Fori(0, KD // RING) as i:
                    for r in range(RING):
                        sp.wait_ge(block_done, i * RING + (r + 1))
                        for a in range(2):
                            sp.dma_start(wring[:, r, a], w[:, :, bass.ds(i * RING * P + (r * P + a * D), P)]).then_inc(w_in[r], 16)

            @block.tensor
            def _(pe):
                pe.sem_inc(block_done, RING)
                with pe.Fori(0, KD // RING) as i:
                    for r in range(RING):
                        pe.wait_ge(w_in[r], i * 32 + 32)
                        pe.wait_ge(glu_done, i * RING + (r + 1))
                        for a in range(2):
                            for k in range(KD):
                                nc.tensor.matmul(ps[:, 2 * r + a, SQ:512], wring[:, r, a, k, :], hT[:, k, 0:T_CTX], start=(k == 0), stop=(k == KD - 1))
                                last = nc.tensor.matmul(ps[:, 2 * r + a, 512:1024], wring[:, r, a, k, :], hT[:, k, T_CTX:T], start=(k == 0), stop=(k == KD - 1))
                        last.then_inc(block_done, 1)

            @block.scalar
            def _(act):
                with act.Fori(0, KD // RING) as i:
                    for r in range(RING):
                        act.wait_ge(block_done, i * RING + (RING + r + 1))
                        act.wait_ge(glu_done, i * RING + (r + 1))
                        nc.scalar.activation(sg[:, r, :], ps[:, 2 * r + 1, SQ:1024], ACT.Sigmoid,
                                             bias=K.vec[:, bass.ds(i * RING + (bias + KD + r), 1)]).then_inc(sig_done, 1)

            @block.vector
            def _(dve):
                nc.vector.memset(glu[:], 0.0).then_inc(glu_done, RING)
                dve.wait_ge(glu_done, RING)
                with dve.Fori(0, KD // RING) as i:
                    for r in range(RING):
                        dve.wait_ge(sig_done, i * RING + (r + 1))
                        for n, (c, width, start) in enumerate(CSEGS):
                            ins = nc.vector.scalar_tensor_tensor(
                                glu[:, bass.ds(i * RING + r, 1), start + PADC:start + PADC + width].rearrange("p a t -> p (a t)"),
                                ps[:, 2 * r, SQ + c:SQ + c + width], K.vec[:, bass.ds(i * RING + (bias + r), 1)], sg[:, r, c:c + width], ALU.add, ALU.mult)
                        ins.then_inc(glu_done, 1)


def phase_depthwise(K, glu, cv):
    nc = K.nc
    NPE, RING = 3, 8
    with ExitStack() as mem:
        diag = mem.enter_context(nc.sbuf_tensor("dw_diag", [P, RING, P], F32))
        ps = mem.enter_context(nc.psum_tensor("dw_ps", [P, NPE, 1024], F32))
        diag_ready, tap_done, block_out, own = (K.sem("dw_" + n) for n in ("diag_ready", "tap_done", "block_out", "own"))
        tap_col = lambda w, c: K.vec[:, VEC_DW + w * KD + c:VEC_DW + w * KD + c + 1]
        with nc.Block() as block:
            @block.scalar
            def _(act):
                for c in range(NPE):
                    for w in range(CONVW):
                        n = c * CONVW + w
                        if n >= RING:
                            act.wait_ge(tap_done, n - RING + 1)
                        nc.scalar.activation(diag[:, n % RING, :], K.ident[:], ACT.Copy, scale=tap_col(w, c)).then_inc(diag_ready, 1)
                    act.wait_ge(tap_done, (c + 1) * CONVW)
                    b = VEC["cv_b_dw"] + c
                    nc.scalar.activation(cv[:, c, :], ps[:, c, SQ:1024], ACT.Identity, bias=K.vec[:, b:b + 1]).then_inc(block_out, 1)

            @block.tensor
            def _(pe):
                for c in range(NPE):
                    for w in range(CONVW):
                        n = c * CONVW + w
                        pe.wait_ge(diag_ready, n + 1)
                        nc.tensor.matmul(ps[:, c, SQ:512], diag[:, n % RING, :], glu[:, c, CSEGS[0][2] + w:CSEGS[0][2] + w + T_CTX],
                                         start=(w == 0), stop=(w == CONVW - 1))
                        nc.tensor.matmul(ps[:, c, 512:1024], diag[:, n % RING, :], glu[:, c, CSEGS[1][2] + w:CSEGS[1][2] + w + T_LAT],
                                         start=(w == 0), stop=(w == CONVW - 1)).then_inc(tap_done, 1)

            @block.vector
            def _(dve):
                with dve.Fori(0, KD - NPE) as i:
                    for w in range(CONVW):
                        for n, (c, width, start) in enumerate(CSEGS):
                            dst = cv[:, bass.ds(i + NPE, 1), c:c + width].rearrange("p a t -> p (a t)")
                            src = glu[:, bass.ds(i + NPE, 1), start + w:start + w + width].rearrange("p a t -> p (a t)")
                            wt = K.vec[:, bass.ds(i + (VEC_DW + w * KD + NPE), 1)]
                            if w == 0:
                                ins = nc.vector.tensor_scalar(dst, src, wt, K.vec[:, bass.ds(i + (VEC["cv_b_dw"] + NPE), 1)], ALU.mult, ALU.add)
                            else:
                                dve.wait_ge(own, i * (2 * CONVW) + (2 * (w - 1) + n + 1))
                                ins = nc.vector.scalar_tensor_tensor(dst, src, wt, dst, ALU.mult, ALU.add)
                            ins.then_inc(own, 1)


def phase_conv_norm(K, cv):
    nc = K.nc
    with ExitStack() as mem:
        sb = lambda n, s, d=F32: mem.enter_context(nc.sbuf_tensor("cn_" + n, s, d))
        mean = sb("mean", [P, P])
        sq = sb("sq", [P, KD, T])
        sd = sb("sd", [P, T])
        ps = mem.enter_context(nc.psum_tensor("cn_ps", [P, 2, 1024], F32))
        S = {n: K.sem("cn_" + n) for n in ("mean_const", "mean_done", "centred", "squared", "var_done", "root_done", "inverted", "scaled", "out")}
        with nc.Block() as block:
            @block.tensor
            def _(pe):
                pe.wait_ge(S["mean_const"], 1)
                for b, src, ready in ((0, cv, None), (1, sq, S["squared"])):
                    for k in range(KD):
                        if ready is not None:
                            pe.wait_ge(ready, k + 1)
                        nc.tensor.matmul(ps[:, b, SQ:512], mean[:], src[:, k, 0:T_CTX], start=(k == 0), stop=(k == KD - 1))
                        last = nc.tensor.matmul(ps[:, b, 512:1024], mean[:], src[:, k, T_CTX:T], start=(k == 0), stop=(k == KD - 1))
                    last.then_inc(S["mean_done"] if b == 0 else S["var_done"], 1)

            @block.scalar
            def _(act):
                for k in range(KD):
                    act.wait_ge(S["centred"], k + 1)
                    nc.scalar.activation(sq[:, k, :], cv[:, k, :], ACT.Square).then_inc(S["squared"], 1)
                act.wait_ge(S["var_done"], 1)
                nc.scalar.activation(sd[:], ps[:, 1, SQ:1024], ACT.Sqrt, bias=K.gneps[:, 1:2]).then_inc(S["root_done"], 1)
                for k in range(KD):
                    g, b = (K.vec[:, VEC[n] + k:VEC[n] + k + 1] for n in ("cv_ln_g", "cv_ln_b"))
                    act.wait_ge(S["scaled"], k + 1)
                    nc.scalar.activation(cv[:, k, :], cv[:, k, :], ACT.Silu, bias=b, scale=g).then_inc(S["out"], 1)

            @block.vector
            def _(dve):
                nc.vector.memset(mean[:], 1.0 / D).then_inc(S["mean_const"], 1)
                dve.wait_ge(S["mean_done"], 1)
                for k in range(KD):
                    nc.vector.tensor_tensor(cv[:, k, :], cv[:, k, :], ps[:, 0, SQ:1024], ALU.subtract).then_inc(S["centred"], 1)
                dve.wait_ge(S["root_done"], 1)
                nc.vector.reciprocal(sd[:], sd[:]).then_inc(S["inverted"], 1)
                dve.wait_ge(S["inverted"], 1)
                for k in range(KD):
                    nc.vector.tensor_tensor(cv[:, k, :], cv[:, k, :], sd[:], ALU.mult).then_inc(S["scaled"], 1)


def load_pw2(K):
    def load(eng, dst, sem):
        eng.dma_start(dst[:], K.io["cv_w_pw2"][0].rearrange("(k p) n -> p k n", p=P)).then_inc(sem, 16)
    return load


def phase_mixer_odd(K):
    nc = K.nc
    with ExitStack() as mem:
        sb = lambda s, n, shape: s.enter_context(nc.sbuf_tensor("od_" + n, shape, F32))
        cv = sb(mem, "cv", [P, KD, T])
        with ExitStack() as mixing:
            glu = sb(mixing, "glu", [P, KD, CPAD])
            with ExitStack() as first:
                h, hT = sb(first, "h", [P, NT, D]), sb(first, "hT", [P, KD, T])
                phase_norm(K, 1, 0, h, hT)
                phase_glu(K, hT, glu)
            phase_depthwise(K, glu, cv)
        phase_conv_norm(K, cv)
        phase_outproj(K, "pw2_", cv, load_pw2(K), 16, 1, bias=K.io["cv_b_pw2"][0])


def phase_final(K):
    nc, x = K.nc, K.x
    with ExitStack() as mem:
        sb = lambda n, s: mem.enter_context(nc.sbuf_tensor("fin_" + n, s, F32))
        g, y = sb("g", [P, D]), sb("y", [P, NT, D])
        ss, ms, rt, rstd = (sb(n, [P, NT]) for n in ("ss", "ms", "rt", "rstd"))
        g_in, squares, mean_done, root_done, inverted, y_done, out = (K.sem("fin_" + n) for n in ("g_in", "squares", "mean", "root", "inverted", "y", "out"))
        with nc.Block() as block:
            @block.sync
            def _(sp):
                sp.dma_start(g[:], K.io["final_g"].partition_broadcast(P)).then_inc(g_in, 16)
                for t in range(NT):
                    sp.wait_ge(y_done, t + 1)
                    dst = K.outs[0][0] if t == 0 else K.outs[1][0, (t - 1) * P:t * P, :]
                    sp.dma_start(dst, y[:, t, :]).then_inc(out, 16)
                sp.wait_ge(out, 16 * NT)

            @block.scalar
            def _(act):
                for t in range(NT):
                    nc.scalar.activation(y[:, t, :], x[:, t, :], ACT.Square, accum_out=ss[:, t:t + 1]).then_inc(squares, 1)
                act.wait_ge(mean_done, 1)
                nc.scalar.activation(rt[:], ms[:], ACT.Sqrt).then_inc(root_done, 1)

            @block.vector
            def _(dve):
                dve.wait_ge(squares, NT)
                nc.vector.tensor_scalar(ms[:], ss[:], 1.0 / D, 1e-6, ALU.mult, ALU.add).then_inc(mean_done, 1)
                dve.wait_ge(root_done, 1)
                nc.vector.reciprocal(rstd[:], rt[:]).then_inc(inverted, 1)
                dve.wait_ge(inverted, 1)
                dve.wait_ge(g_in, 16)
                for t in range(NT):
                    nc.vector.scalar_tensor_tensor(y[:, t, :], x[:, t, :], rstd[:, t:t + 1], g[:], ALU.mult, ALU.mult).then_inc(y_done, 1)


def all_phases(K):
    phase_mixer_even(K)
    K.recycle()
    phase_peer(K, 0)
    K.recycle()
    phase_mixer_odd(K)
    phase_peer(K, 1)
    phase_final(K)


def build(nc, io, const, outs, phases=all_phases, dump=None):
    with ExitStack() as stack:
        K = Ctx(nc, io)
        K.const, K.outs, K.dump = const, outs, dump
        sb = lambda n, s, d=F32: stack.enter_context(nc.sbuf_tensor(n, s, d))
        K.x = sb("x", [P, NT, D])
        K.ident = sb("ident", [P, P])
        K.vec = sb("vec", [P, P + 2 * TAP_ROWS])
        K.gneps = sb("gneps", [P, 2])
        K.modrows = nc.dram_tensor("modrows", (2, DEPTH * 6 * D), F32, kind="Internal").ap()
        x_in = K.sem("x_in")
        eps_set = K.sem("eps_set")
        with nc.Block() as block:
            @block.vector
            def _(dve):
                nc.vector.memset(K.gneps[:, 0:1], 64e-5).then_inc(eps_set, 1)
                nc.vector.memset(K.gneps[:, 1:2], 1e-5).then_inc(eps_set, 1)

            @block.sync
            def _(sp):
                sp.dma_start(K.x[:, 0, :], io["x_prompt"][0]).then_inc(x_in, 16)
                sp.dma_start(K.x[:, 1:NT, :], io["x_sample"][0].rearrange("(t p) d -> p t d", p=P)).then_inc(x_in, 16)
                sp.dma_start(K.ident[:], const["ident"]).then_inc(x_in, 16)
                sp.wait_ge(x_in, 48)
        phase_vectors(K)
        phase_modulation(K)
        phases(K)


INPUTS = ["x_prompt", "x_sample", "cache_k", "cache_v", "state_rwkv", "c", "c_ctx", "mod_w", "mod_b", "norm_g", "ab_w_in",
          "ab_w_out", "ab_sink", "ab_shift_w", "ab_k_k", "ab_k_a", "ab_r_k", "ab_w0", "ab_w2", "ab_a0", "ab_a2", "ab_g2",
          "ab_gn_g", "ab_gn_b", "cv_w_pw1", "cv_b_pw1", "cv_w_dw", "cv_b_dw", "cv_ln_g", "cv_ln_b", "cv_w_pw2", "cv_b_pw2",
          "peer_w_q", "peer_keys", "peer_u", "peer_v", "final_g"]
OUTPUTS = [(1, T_CTX, D), (1, T_LAT, D), (1, 1, T_CTX, KV, HD), (1, 1, T_CTX, KV, HD), (1, 1, 2, HEADS, HD, HD)]


def kernel(**inputs):
    import concourse.bacc as bacc
    from concourse.bass_utils import run_bass_kernel_spmd

    nc = bacc.Bacc("TRN2", target_bir_lowering=False, num_devices=1)
    arrays, io, const = {}, {}, {}
    for group, named in ((io, {n: np.ascontiguousarray(inputs[n]) for n in INPUTS}), (const, shape_constants())):
        for name, a in named.items():
            full = ("in_" if group is io else "const_") + name
            arrays[full] = a
            group[name] = nc.dram_tensor(full, a.shape, mybir.dt.from_np(a.dtype), kind="ExternalInput").ap()
    outs = [nc.dram_tensor(f"out_{i}", shape, F32, kind="ExternalOutput").ap() for i, shape in enumerate(OUTPUTS)]
    build(nc, io, const, outs)
    r = run_bass_kernel_spmd(nc, [arrays], core_ids=[0])
    return tuple(r.results[0][f"out_{i}"] for i in range(len(OUTPUTS)))
```

```python
from contextlib import ExitStack

import numpy as np

import concourse.bass as bass
from concourse import mybir

F32 = mybir.dt.float32
U32 = mybir.dt.uint32
ALU = mybir.AluOpType
ACT = mybir.ActivationFunctionType
AXX = mybir.AxisListType.X

P = 128
D = 1024
KD = D // P
T_CTX, T_LAT = 128, 512
T = T_CTX + T_LAT
NT = T // P
DEPTH = 2
HEADS, KV, HD = 8, 2, 64
D_ATTN = HEADS * HD
D_AIN = D_ATTN + 2 * KV * HD
D_RW = 512
NCC = D_RW // P
D_IN = D_AIN + 3 * D_RW + 3 * P
CONVW = 31
PADC = CONVW // 2
PH, NKEY, TOPK = 8, 128, 16
NEXP = NKEY * NKEY
GRID_W = 64
CH = 64
NEG = -1.0e30
LOW = -3.0e38
SQ = 384


def shape_constants():
    c = {}
    c["ident"] = np.eye(P, dtype=np.float32)
    blk = np.zeros((P, P), np.float32)
    blk[:64, :64] = 1
    blk[64:, 64:] = 1
    c["headsum"] = blk
    half, quarter = HD // 2, HD // 4
    freqs = np.float32(10000.0) ** (-np.arange(quarter, dtype=np.float32) / np.float32(quarter))
    t = np.arange(T_LAT)
    row = (t // GRID_W).astype(np.float32)
    col = (t % GRID_W).astype(np.float32)
    cos = np.zeros((HD, T_LAT), np.float32)
    sin = np.zeros((HD, T_LAT), np.float32)
    perm = np.zeros((P, P), np.float32)
    for d in range(HD):
        pos = row if d < half else col
        ang = pos * freqs[d % quarter]
        cos[d], sin[d] = np.cos(ang), np.sin(ang)
        first = (d % half) < quarter
        for g in range(2):
            if first:
                perm[g * HD + d + quarter, g * HD + d] = -1
            else:
                perm[g * HD + d - quarter, g * HD + d] = 1
    c["rope"] = np.concatenate([np.tile(cos, (2, 1)), np.tile(sin, (2, 1))], axis=1)
    c["ropeperm"] = perm
    q = np.arange(P)[:, None]
    k = np.arange(P)[None, :]
    z = np.zeros((P, P), np.float32)
    prev = np.where(k >= q, 0, NEG).astype(np.float32)
    nxt = np.where(k <= q, 0, NEG).astype(np.float32)
    c["amask"] = np.concatenate([z, prev, z, nxt, z, z, nxt], axis=1)
    r = np.arange(CH)[:, None]
    s = np.arange(CH)[None, :]
    strict = (s < r).astype(np.float32)
    diag = np.eye(CH, dtype=np.float32)
    sm = []
    for d in range(2):
        st = strict if d == 0 else strict.T
        sm.append([-st, -st.T, st.T, st.T + diag, -(st.T + diag)])
    sm = np.array(sm).transpose(1, 0, 2, 3)
    c["scanmask"] = np.tile(sm.transpose(2, 0, 1, 3).reshape(CH, -1), (2, 1)).astype(np.float32)
    lev = []
    b = 1
    while b < CH:
        m = ((r // (2 * b)) == (s // (2 * b))) & (r % (2 * b) >= b) & (s % (2 * b) < b)
        lev.append([[m, m.T], [m.T, m]])
        b *= 2
    lev = np.array(lev).astype(np.float32)
    c["levmask"] = np.tile(lev.transpose(3, 0, 1, 2, 4).reshape(CH, -1), (2, 1)).copy()
    reset = np.ones((P, T), np.float32)
    reset[:, ::CH] = 0
    c["reset"] = reset
    c["eye64"] = np.tile(np.eye(CH, dtype=np.float32), (2, 1))
    c["iota16"] = np.tile(np.tile(np.arange(TOPK, dtype=np.float32), TOPK), (P, 1))
    return c


class Ctx:

    def __init__(self, nc, io):
        self.nc, self.io, self.live = nc, io, []

    def sem(self, name):
        self.live.append(self.nc.alloc_semaphore(name))
        return self.live[-1]

    def recycle(self):
        self.nc.clear_and_free_semaphores(self.live)
        self.nc.all_engine_barrier()
        self.live = []


def chain_on(eng, sem):
    n = [0]

    def step(ins, wait=True):
        n[0] += 1
        ins.then_inc(sem, 1)
        if wait:
            eng.wait_ge(sem, n[0])
        return n[0]
    return step


def phase_modulation(K):
    nc, io = K.nc, K.io
    NCH = 6 * D // 512
    RING = 4
    with ExitStack() as mem:
        sb = lambda n, s, d=F32: mem.enter_context(nc.sbuf_tensor(n, s, d))
        cond = sb("cond", [P, 2, KD])
        csil = sb("csil", [P, KD, 2])
        wring = sb("mod_wring", [P, RING, KD, 512])
        bias = sb("mod_bias", [2, DEPTH * 6 * D])
        rows = sb("mod_rows", [2, DEPTH, 6, D])
        normg = sb("mod_normg", [2, DEPTH, 2, D])
        ps = mem.enter_context(nc.psum_tensor("mod_ps", [P, 8, 512], F32))
        cond_in, silu_done = K.sem("cond_in"), K.sem("silu_done")
        small_in = K.sem("mod_small_in")
        w_in = [K.sem(f"mod_w_in{i}") for i in range(RING)]
        chunk_done, row_done = K.sem("mod_chunk_done"), K.sem("mod_row_done")
        scaled, stored = K.sem("mod_scaled"), K.sem("mod_stored")
        with nc.Block() as block:
            @block.sync
            def _(sp):
                sp.dma_start(cond[:, 0, :], io["c_ctx"].rearrange("(p k) -> p k", k=KD)).then_inc(cond_in, 16)
                sp.dma_start(cond[:, 1, :], io["c"].rearrange("a (p k) -> p (a k)", k=KD)).then_inc(cond_in, 16)
                for layer in range(DEPTH):
                    w = io["mod_w"][layer].rearrange("(p k) n -> p k n", k=KD)
                    with sp.Fori(0, NCH // RING) as i:
                        for r in range(RING):
                            sp.wait_ge(chunk_done, i * RING + (layer * NCH + r + 1))
                            sp.dma_start(wring[:, r], w[:, :, bass.ds((i * RING + r) * 512, 512)]).then_inc(w_in[r], 16)
                sp.wait_ge(scaled, DEPTH * 2)
                sp.dma_start(K.modrows, rows[:].rearrange("p l k d -> p (l k d)")).then_inc(stored, 16)
                sp.wait_ge(stored, 16)

            @block.scalar
            def _(act):
                act.dma_start(bias[:], io["mod_b"].rearrange("l n -> (l n)").partition_broadcast(2)).then_inc(small_in, 16)
                act.dma_start(normg[:].rearrange("p l k d -> p (l k d)"),
                              io["norm_g"].rearrange("l k d -> (l k d)").partition_broadcast(2)).then_inc(small_in, 16)
                act.wait_ge(cond_in, 32)
                nc.scalar.activation(csil[:].rearrange("p k s -> p s k"), cond[:], ACT.Silu).then_inc(silu_done, 1)

            @block.tensor
            def _(pe):
                pe.sem_inc(chunk_done, RING)
                pe.wait_ge(silu_done, 1)
                for layer in range(DEPTH):
                    with pe.Fori(0, NCH // RING) as i:
                        for r in range(RING):
                            pe.wait_ge(w_in[r], i * 16 + 16 * (layer * NCH // RING + 1))
                            pe.wait_ge(row_done, i * RING + (layer * NCH + r + 1))
                            for k in range(KD):
                                last = nc.tensor.matmul(ps[0:2, r, :], csil[:, k, :], wring[:, r, k, :],
                                                        start=(k == 0), stop=(k == KD - 1))
                            last.then_inc(chunk_done, 1)

            @block.vector
            def _(dve):
                dve.sem_inc(row_done, RING)
                dve.wait_ge(small_in, 32)
                flat = rows[:].rearrange("p l k d -> p (l k d)")
                for layer in range(DEPTH):
                    with dve.Fori(0, NCH // RING) as i:
                        for r in range(RING):
                            dve.wait_ge(chunk_done, i * RING + (layer * NCH + r + 1 + RING))
                            cols = bass.ds((i * RING + (layer * NCH + r)) * 512, 512)
                            nc.vector.tensor_tensor(flat[:, cols], ps[0:2, r, :], bias[:, cols], ALU.add).then_inc(row_done, 1)
                dve.wait_ge(row_done, DEPTH * NCH + RING)
                for layer in range(DEPTH):
                    for site in range(2):
                        sc = rows[:, layer, 3 * site + 1, :]
                        nc.vector.scalar_tensor_tensor(sc, sc, 1.0, normg[:, layer, site, :], ALU.add, ALU.mult).then_inc(scaled, 1)


def load_row(eng, K, dst, stream, layer, kind, sem):
    eng.dma_start(dst, K.modrows[stream, (layer * 6 + kind) * D:(layer * 6 + kind + 1) * D].partition_broadcast(P)).then_inc(sem, 16)


def phase_norm(K, layer, site, h, hT):
    nc = K.nc
    tag = f"n{layer}{site}_"
    x, ident = K.x, K.ident
    with ExitStack() as mem:
        sb = lambda n, s, d=F32: mem.enter_context(nc.sbuf_tensor(tag + n, s, d))
        rows = sb("rows", [P, 2, 2, D])
        ss = sb("ss", [P, NT])
        ms = sb("ms", [P, NT])
        rt = sb("rt", [P, NT])
        rstd = sb("rstd", [P, NT])
        ps = mem.enter_context(nc.psum_tensor(tag + "ps", [P, 8, 512], F32))
        rows_in, squares, mean_done, root_done = K.sem(tag + "rows_in"), K.sem(tag + "squares"), K.sem(tag + "mean"), K.sem(tag + "root")
        rstd_done, scaled, h_done, turned, hT_done = (K.sem(tag + n) for n in ("rstd", "scaled", "h_done", "turned", "hT_done"))
        with nc.Block() as block:
            @block.sync
            def _(sp):
                for s in range(2):
                    for j, kind in enumerate((3 * site + 1, 3 * site)):
                        load_row(sp, K, rows[:, s, j, :], s, layer, kind, rows_in)

            @block.scalar
            def _(act):
                for t in range(NT):
                    nc.scalar.activation(h[:, t, :], x[:, t, :], ACT.Square, accum_out=ss[:, t:t + 1]).then_inc(squares, 1)
                act.wait_ge(mean_done, 1)
                nc.scalar.activation(rt[:], ms[:], ACT.Sqrt).then_inc(root_done, 1)
                for t in range(NT):
                    for b in range(2):
                        act.wait_ge(turned, 2 * t + b + 1)
                        nc.scalar.copy(hT[:, 4 * b:4 * b + 4, t * P:(t + 1) * P],
                                       ps[:, (2 * t + b) % 8, :].rearrange("p (k c) -> p k c", k=4)).then_inc(hT_done, 1)

            @block.vector
            def _(dve):
                dve.wait_ge(squares, NT)
                nc.vector.tensor_scalar(ms[:], ss[:], 1.0 / D, 1e-6, ALU.mult, ALU.add).then_inc(mean_done, 1)
                dve.wait_ge(root_done, 1)
                nc.vector.reciprocal(rstd[:], rt[:]).then_inc(rstd_done, 1)
                dve.wait_ge(rstd_done, 1)
                dve.wait_ge(rows_in, 64)
                for t in range(NT):
                    s = min(t, 1)
                    nc.vector.scalar_tensor_tensor(h[:, t, :], x[:, t, :], rstd[:, t:t + 1], rows[:, s, 0, :], ALU.mult, ALU.mult).then_inc(scaled, 1)
                    dve.wait_ge(scaled, t + 1)
                    nc.vector.tensor_tensor(h[:, t, :], h[:, t, :], rows[:, s, 1, :], ALU.add).then_inc(h_done, 1)

            @block.tensor
            def _(pe):
                for t in range(NT):
                    pe.wait_ge(h_done, t + 1)
                    for b in range(2):
                        n = 2 * t + b
                        if n >= 8:
                            pe.wait_ge(hT_done, n - 7)
                        for k in range(4):
                            last = nc.tensor.transpose(ps[:, n % 8, k * P:(k + 1) * P], h[:, t, (4 * b + k) * P:(4 * b + k + 1) * P], ident[:])
                        last.then_inc(turned, 1)


def phase_experts(K, layer, h, hT, yacc):
    nc, io, ident = K.nc, K.io, K.ident
    tag = f"e{layer}_"
    NI, NC = NT * PH, 2 * PH
    R = 8
    G = TOPK
    PAIR = [0, 1, 2, 0, 1]
    QCHUNK = {0: 0, 2: 1}
    with ExitStack() as mem:
        sb = lambda n, s, d=F32: mem.enter_context(nc.sbuf_tensor(tag + n, s, d))
        uring = sb("uring", [P, R, D])
        vring = sb("vring", [P, R, D])
        diag = sb("diag", [P, G, P])
        keys = vring[:, R - 2:R, :].rearrange("p a (b n) -> p (a b) n", n=P)
        keysT = sb("keysT", [P, NC, P])
        wring = sb("wring", [P, 2, KD, P])
        qT = sb("qT", [P, T])
        scores = sb("scores", [P, 4, NT, 2 * P])
        eidx = sb("eidx", [P, NI * G], U32)
        uslot, vslot = sb("uslot", [P, NT, G], U32), sb("vslot", [P, NT, G], U32)
        gate = sb("gate", [P, NI * G])
        dots = sb("dots", [P, NT, G])
        gelu = sb("gelu", [P, NT, G])
        wgt = sb("wgt", [P, NT, G])
        iota = sb("iota", [P, G * G])
        item = sb("item", [P, 2, P])
        sub = sb("sub", [P, 2, P])
        top = sb("top", [P, 2, G])
        topi = sb("topi", [P, 2, G], U32)
        cand = sb("cand", [P, G * G])
        cand2 = sb("cand2", [P, G * G])
        best = sb("best", [P, G])
        besti = sb("besti", [P, G], U32)
        part = sb("part", [P, 2, G], U32)
        hot = sb("hot", [P, 2, G * G])
        half = sb("half", [P, 2, G])
        nbest = sb("nbest", [P, 1])
        expd = sb("expd", [P, G])
        esum = sb("esum", [P, 1])
        rsum = sb("rsum", [P, 1])
        ps = mem.enter_context(nc.psum_tensor(tag + "ps", [P, 4, D], F32))
        iota_in = K.sem(tag + "iota_in")
        keys_in, keys_turned, keysT_done = K.sem(tag + "keys_in"), K.sem(tag + "keys_turned"), K.sem(tag + "keysT_done")
        w_in = [K.sem(tag + f"w_in{a}") for a in range(2)]
        q_done, q_copied, s_done, s_copied = (K.sem(tag + n) for n in ("q_done", "q_copied", "s_done", "s_copied"))
        u_in = [K.sem(tag + f"u_in{r}") for r in range(R)]
        v_in = [K.sem(tag + f"v_in{r}") for r in range(R)]
        u_used, v_used, granted, uslot_set, vslot_set = (K.sem(tag + n) for n in ("u_used", "v_used", "granted", "uslot_set", "vslot_set"))
        chosen, dve_own, neg_ready, exp_ready = (K.sem(tag + n) for n in ("chosen", "dve_own", "neg_ready", "exp_ready"))
        carried = K.sem(tag + "carried")
        gelu_ready, wgt_ready, diag_ready, summed = (K.sem(tag + n) for n in ("gelu_ready", "wgt_ready", "diag_ready", "summed"))
        u_tab = io["peer_u"].rearrange("l e d -> (l e) d")
        v_tab = io["peer_v"].rearrange("l e d -> (l e) d")
        w_cols = io["peer_w_q"][layer].rearrange("(k p) n -> p k n", p=P)
        flat = scores[:].rearrange("p h t c -> p (h t c)")
        slot = lambda hd: hd % 4
        at = lambda hd, t: hd * NT + t
        after = lambda hd, t: (hd + (t + 2) // NT, (t + 2) % NT)
        pair_of = lambda hd, a: 3 if not isinstance(hd, int) or hd > 1 else 3 - a
        with nc.Block() as block:
            @block.sync
            def _(sp):
                sp.dma_start(keys, io["peer_keys"][layer].rearrange("a h n d -> n (a h) d")).then_inc(keys_in, 16)
                with sp.Fori(0, PH) as hd:
                    for a in range(2):
                        sp.wait_ge(q_done, hd * 2 + (a + 1))
                        sp.dma_start(wring[:, a], w_cols[:, :, bass.ds(hd * 2 * P + a * P, P)]).then_inc(w_in[a], 16)

            @block.gpsimd
            def _(pool):
                def set_uslot(hd, t):
                    n = at(hd, t)
                    pool.wait_ge(chosen, n + 1)
                    if not (isinstance(n, int) and n < 2):
                        pool.wait_ge(u_used, n * G + (R - G))
                    pool.sem_inc(granted, 1)
                    nc.gpsimd.tensor_copy(uslot[:, t, :], eidx[:, bass.ds(n * G, G)]).then_inc(uslot_set, 1)
                    pool.wait_ge(uslot_set, n + 1)

                def set_vslot(hd, t):
                    n = at(hd, t)
                    if not (isinstance(n, int) and n < 2):
                        pool.wait_ge(v_used, n * G + (R - G))
                    pool.sem_inc(granted, 1)
                    nc.gpsimd.tensor_copy(vslot[:, t, :], eidx[:, bass.ds(n * G, G)]).then_inc(vslot_set, 1)
                    pool.wait_ge(vslot_set, n + 1)

                def gather(ring, tab, index, r, sem):
                    pool.sem_inc(granted, 1)
                    pool.indirect_dma_start(ring[:, r % R, :], None, tab,
                                            bass.IndirectOffsetOnAxis(ap=index, axis=0)).then_inc(sem[r % R], 16)

                def u_row(hd, t, r):
                    pool.wait_ge(u_used, at(hd, t) * G + (r + 1))
                    gather(uring, u_tab, uslot[:, t, r:r + 1], r, u_in)

                def v_row(hd, t, r):
                    pool.wait_ge(v_used, at(hd, t) * G + (r + 1))
                    gather(vring, v_tab, vslot[:, t, r:r + 1], r, v_in)

                def rows(hd):
                    for t in range(NT):
                        first = isinstance(hd, int) and hd == 0 and t == 0
                        before = (hd, t - 1) if t else (hd - 1, NT - 1)
                        set_uslot(hd, t)
                        if not first:
                            set_vslot(*before)
                        for r in range(G):
                            u_row(hd, t, r)
                            if not first:
                                v_row(*before, r)

                pool.wait_ge(keysT_done, 4)
                rows(0)
                with pool.Fori(1, PH) as hd:
                    rows(hd)
                set_vslot(PH - 1, NT - 1)
                for r in range(G):
                    v_row(PH - 1, NT - 1, r)

            @block.vector
            def _(dve):
                def choosing(hd, t):
                    n = at(hd, t)
                    base = n * STEPS
                    count = [0]

                    def own(*instructions):
                        for ins in instructions:
                            count[0] += 1
                            ins.then_inc(dve_own, 1)

                    def after_own():
                        dve.wait_ge(dve_own, base + count[0])
                        dve.sem_inc(carried, 1)

                    s = [item[:, a, :] for a in range(2)]
                    c3 = cand[:].rearrange("p (a b) -> p a b", a=G)
                    io3 = iota[:].rearrange("p (a b) -> p a b", a=G)
                    hots = [hot[:, a, :].rearrange("p (a b) -> p a b", a=G) for a in range(2)]
                    V = nc.vector
                    own(V.tensor_copy(item[:].rearrange("p a n -> p (a n)"), flat[:, bass.ds(slot(hd) * (NT * 2 * P) + t * 2 * P, 2 * P)]))
                    yield
                    after_own()
                    own(*(V.max(top[:, a, 0:8], s[a]) for a in range(2)))
                    yield
                    after_own()
                    own(*(V.max_index(topi[:, a, 0:8], top[:, a, 0:8], s[a]) for a in range(2)))
                    own(*(V.match_replace(sub[:, a, :], top[:, a, 0:8], s[a], LOW) for a in range(2)))
                    yield
                    after_own()
                    own(*(V.max(top[:, a, 8:16], sub[:, a, :]) for a in range(2)))
                    yield
                    after_own()
                    own(*(V.max_index(topi[:, a, 8:16], top[:, a, 8:16], sub[:, a, :]) for a in range(2)))
                    own(V.tensor_tensor(c3, top[:, 0, :].unsqueeze(2).to_broadcast([P, G, G]),
                                        top[:, 1, :].unsqueeze(1).to_broadcast([P, G, G]), ALU.add))
                    yield
                    after_own()
                    own(V.max(best[:, 0:8], cand[:]))
                    yield
                    after_own()
                    own(V.max_index(besti[:, 0:8], best[:, 0:8], cand[:]), V.match_replace(cand2[:], best[:, 0:8], cand[:], LOW))
                    yield
                    after_own()
                    own(V.max(best[:, 8:16], cand2[:]))
                    yield
                    after_own()
                    own(V.tensor_scalar(nbest[:], best[:, 0:1], -1.0, None, ALU.mult), V.max_index(besti[:, 8:16], best[:, 8:16], cand2[:]))
                    yield
                    after_own()
                    dve.sem_inc(neg_ready, 1)
                    own(V.tensor_scalar(part[:, 0, :], besti[:], 4, None, ALU.logical_shift_right),
                        V.tensor_scalar(part[:, 1, :], besti[:], 15, None, ALU.bitwise_and))
                    yield
                    after_own()
                    own(*(V.tensor_tensor(hots[a], io3, part[:, a, :].unsqueeze(2).to_broadcast([P, G, G]), ALU.is_equal) for a in range(2)))
                    yield
                    after_own()
                    own(*(V.tensor_tensor(hots[a], hots[a], topi[:, a, :].unsqueeze(1).to_broadcast([P, G, G]), ALU.mult) for a in range(2)))
                    yield
                    after_own()
                    own(*(V.tensor_reduce(half[:, a, :], hots[a], AXX, ALU.add) for a in range(2)))
                    yield
                    after_own()
                    own(V.tensor_scalar(half[:, 0, :], half[:, 0, :], float(NKEY), float(layer * NEXP), ALU.mult, ALU.add))
                    yield
                    after_own()
                    own(V.tensor_tensor(eidx[:, bass.ds(n * G, G)], half[:, 0, :], half[:, 1, :], ALU.add))
                    dve.wait_ge(exp_ready, n + 1)
                    dve.sem_inc(carried, 1)
                    own(V.reciprocal(rsum[:], esum[:]))
                    yield
                    after_own()
                    dve.sem_inc(chosen, 1)
                    own(V.tensor_scalar(gate[:, bass.ds(n * G, G)], expd[:], rsum[:, 0:1], None, ALU.mult))
                    after_own()
                    assert count[0] == STEPS, count[0]
                    yield

                def copy_scores(hd, a):
                    dve.wait_ge(s_done, hd * 2 + (a + 1))
                    nc.vector.tensor_copy(scores[:, bass.ds(slot(hd), 1), :, a * P:(a + 1) * P].rearrange("p h t n -> p (h t) n"),
                                          ps[:, pair_of(hd, a), SQ:1024].rearrange("p (t n) -> p t n", t=NT)).then_inc(s_copied, 1)

                def dot(hd, t, beside):
                    for r in range(G):
                        if beside is not None:
                            next(beside)
                        dve.wait_ge(u_in[r % R], at(hd, t) * 32 + (16 * (r // R) + 16))
                        nc.vector.scalar_tensor_tensor(uring[:, r % R, :], uring[:, r % R, :], 1.0, h[:, t, :],
                                                       ALU.mult, ALU.mult, accum_out=dots[:, t, r:r + 1]).then_inc(u_used, 1)

                def weigh(hd, t):
                    n = at(hd, t)
                    dve.wait_ge(gelu_ready, n + 1)
                    nc.vector.tensor_tensor(wgt[:, t, :], gelu[:, t, :], gate[:, bass.ds(n * G, G)], ALU.mult).then_inc(wgt_ready, 1)

                def add_up(hd, t):
                    n = at(hd, t)
                    dve.wait_ge(v_used, n * G + (R + G))
                    dve.wait_ge(summed, n + 2)
                    nc.vector.tensor_tensor(yacc[:, t, :], ps[:, PAIR[t], :], yacc[:, t, :], ALU.add).then_inc(summed, 1)

                def items(hd, scoring=True):
                    for t in range(NT):
                        known = isinstance(hd, int)
                        beside = None if known and at(hd, t) + 2 >= NI else choosing(*after(hd, t))
                        dot(hd, t, beside)
                        weigh(hd, t)
                        if not (known and at(hd, t) < 2):
                            add_up(*((hd, t - 2) if t >= 2 else (hd - 1, t - 2 + NT)))
                        if scoring and t - 1 in QCHUNK:
                            copy_scores(hd + 2, QCHUNK[t - 1])

                nc.vector.memset(yacc[:], 0.0).then_inc(summed, 2)
                dve.sem_inc(u_used, R)
                dve.wait_ge(iota_in, 16)
                for a in range(2):
                    copy_scores(0, a)
                dve.wait_ge(s_copied, 2)
                for t in range(2):
                    for _ in choosing(0, t):
                        pass
                for a in range(2):
                    copy_scores(1, a)
                dve.wait_ge(s_copied, 4)
                items(0)
                with dve.Fori(1, PH - 2) as hd:
                    items(hd)
                items(PH - 2, scoring=False)
                items(PH - 1, scoring=False)
                for t in range(NT - 2, NT):
                    add_up(PH - 1, t)

            @block.scalar
            def _(act):
                def exponents(hd, t):
                    act.wait_ge(neg_ready, at(hd, t) + 1)
                    nc.scalar.activation(expd[:], best[:], ACT.Exp, bias=nbest[:, 0:1], accum_out=esum[:]).then_inc(exp_ready, 1)

                def gelus(hd, t):
                    act.wait_ge(u_used, at(hd, t) * G + (R + G))
                    nc.scalar.activation(gelu[:, t, :], dots[:, t, :], ACT.Gelu).then_inc(gelu_ready, 1)

                def diags(hd, t):
                    n = at(hd, t)
                    act.wait_ge(wgt_ready, n + 1)
                    for r in range(G):
                        if not (isinstance(n, int) and n < 1):
                            act.wait_ge(v_used, n * G + (R + r + 1 - G))
                        nc.scalar.activation(diag[:, r, :], ident[:], ACT.Copy, scale=wgt[:, t, r:r + 1]).then_inc(diag_ready, 1)

                def copy_queries(hd, a):
                    act.wait_ge(q_done, hd * 2 + (a + 3))
                    nc.scalar.copy(qT[:], ps[:, pair_of(hd, a), SQ:1024]).then_inc(q_copied, 1)

                def items(hd, scoring=True):
                    for t in range(NT):
                        if not (isinstance(hd, int) and at(hd, t) + 2 >= NI):
                            exponents(*after(hd, t))
                        gelus(hd, t)
                        diags(hd, t)
                        if scoring and t in QCHUNK:
                            copy_queries(hd + 2, QCHUNK[t])

                act.dma_start(iota[:], K.const["iota16"]).then_inc(iota_in, 16)
                for b in range(4):
                    act.wait_ge(keys_turned, b + 1)
                    nc.scalar.copy(keysT[:, 4 * b:4 * b + 4, :].rearrange("p c n -> p (c n)"), ps[:, b, 0:512]).then_inc(keysT_done, 1)
                for a in range(2):
                    copy_queries(0, a)
                exponents(0, 0)
                exponents(0, 1)
                for a in range(2):
                    copy_queries(1, a)
                items(0)
                with act.Fori(1, PH - 2) as hd:
                    items(hd)
                items(PH - 2, scoring=False)
                items(PH - 1, scoring=False)

            @block.tensor
            def _(pe):
                def queries(hd, a):
                    pe.wait_ge(w_in[a], hd * 16 + 16)
                    if isinstance(hd, int) and hd == 1:
                        pe.wait_ge(s_copied, a + 1)
                    elif not isinstance(hd, int):
                        pe.wait_ge(s_copied, hd * 2 + a)
                    b = pair_of(hd, a)
                    for k in range(KD):
                        nc.tensor.matmul(ps[:, b, SQ:512], wring[:, a, k, :], hT[:, k, 0:T_CTX], start=(k == 0), stop=(k == KD - 1))
                        last = nc.tensor.matmul(ps[:, b, 512:1024], wring[:, a, k, :], hT[:, k, T_CTX:T], start=(k == 0), stop=(k == KD - 1))
                    last.then_inc(q_done, 1)

                def score(hd, a):
                    pe.wait_ge(q_copied, hd * 2 + (a + 1))
                    for t in range(NT):
                        last = nc.tensor.matmul(ps[:, pair_of(hd, a), SQ + t * P:SQ + (t + 1) * P], qT[:, t * P:(t + 1) * P],
                                                keysT[:, bass.ds(hd * 2 + a, 1), :].rearrange("p a n -> p (a n)"), start=True, stop=True)
                    last.then_inc(s_done, 1)

                def items(hd, scoring=True):
                    for t in range(NT):
                        n = at(hd, t)
                        if scoring and t in QCHUNK:
                            queries(hd + 2, QCHUNK[t])
                        pe.wait_ge(summed, n + 1)
                        for r in range(G):
                            if scoring and t in QCHUNK and r == G // 2:
                                score(hd + 2, QCHUNK[t])
                            pe.wait_ge(diag_ready, n * G + (r + 1))
                            pe.wait_ge(v_in[r % R], n * 32 + (16 * (r // R) + 16))
                            nc.tensor.matmul(ps[:, PAIR[t], 0:512], diag[:, r, :], vring[:, r % R, 0:512], start=(r == 0), stop=(r == G - 1))
                            nc.tensor.matmul(ps[:, PAIR[t], 512:D], diag[:, r, :], vring[:, r % R, 512:D], start=(r == 0), stop=(r == G - 1)).then_inc(v_used, 1)

                pe.sem_inc(q_done, 2)
                pe.sem_inc(v_used, R)
                pe.wait_ge(keys_in, 16)
                for b in range(4):
                    for j in range(4):
                        c = 4 * b + j
                        last = nc.tensor.transpose(ps[:, b, j * P:(j + 1) * P], keys[:, (c % 2) * PH + c // 2, :], ident[:])
                    last.then_inc(keys_turned, 1)
                pe.wait_ge(keysT_done, 4)
                for hd in range(2):
                    for a in range(2):
                        queries(hd, a)
                        score(hd, a)
                pe.wait_ge(s_copied, 4)
                with pe.Fori(0, PH - 2) as hd:
                    items(hd)
                with pe.Fori(PH - 2, PH) as hd:
                    items(hd, scoring=False)


def phase_gate_add(K, layer, site, y, tag):
    nc = K.nc
    with ExitStack() as mem:
        rows = mem.enter_context(nc.sbuf_tensor(tag + "rows", [P, 2, D], F32))
        rows_in, gated, added = K.sem(tag + "rows_in"), K.sem(tag + "gated"), K.sem(tag + "added")
        with nc.Block() as block:
            @block.sync
            def _(sp):
                for s in range(2):
                    load_row(sp, K, rows[:, s, :], s, layer, 3 * site + 2, rows_in)

            @block.vector
            def _(dve):
                dve.wait_ge(rows_in, 32)
                nc.vector.tensor_tensor(y[:, 0, :], y[:, 0, :], rows[:, 0, :], ALU.mult).then_inc(gated, 1)
                nc.vector.tensor_tensor(y[:, 1:NT, :], y[:, 1:NT, :], rows[:, 1, :].unsqueeze(1).to_broadcast([P, NT - 1, D]), ALU.mult).then_inc(gated, 1)
                dve.wait_ge(gated, 2)
                nc.vector.tensor_tensor(K.x[:], K.x[:], y[:], ALU.add).then_inc(added, 1)


STEPS = 30


def phase_peer(K, layer):
    nc = K.nc
    with ExitStack() as mem:
        sb = lambda n, s: mem.enter_context(nc.sbuf_tensor(f"peer{layer}_{n}", s, F32))
        h = sb("h", [P, NT, D])
        hT, yacc = sb("hT", [P, KD, T]), sb("yacc", [P, NT, D])
        phase_norm(K, layer, 1, h, hT)
        phase_experts(K, layer, h, hT, yacc)
        phase_gate_add(K, layer, 1, yacc, f"g{layer}_")


VEC_ROWS = [("ab_shift_w", 3 * 15), ("ab_k_k", 4), ("ab_k_a", 4), ("ab_r_k", 4), ("ab_w0", 8), ("ab_a0", 8),
            ("ab_gn_g", 4), ("ab_gn_b", 4), ("cv_b_pw1", 16), ("cv_b_dw", 8), ("cv_ln_g", 8), ("cv_ln_b", 8)]
VEC = {}
_at = 0
for _name, _n in VEC_ROWS:
    VEC[_name] = _at
    _at += _n
VEC_DW = P
TAP_ROWS = CONVW * KD // 2


def phase_vectors(K):
    nc, io = K.nc, K.io
    with ExitStack() as mem:
        rows = mem.enter_context(nc.sbuf_tensor("vec_rows", [P, 3, P], F32))
        ps = mem.enter_context(nc.psum_tensor("vec_ps", [P, 3, P], F32))
        rows_in, cleared, turned, copied = K.sem("vec_rows_in"), K.sem("vec_cleared"), K.sem("vec_turned"), K.sem("vec_copied")
        with nc.Block() as block:
            @block.sync
            def _(sp):
                sp.wait_ge(cleared, 1)
                for name, n in VEC_ROWS:
                    a = io[name]
                    dims = " ".join("abcd"[:len(a.shape)])
                    sp.dma_start(rows[VEC[name]:VEC[name] + n, 0, :],
                                 a.rearrange(f"{dims} -> ({dims})").rearrange("(n p) -> n p", p=P)).then_inc(rows_in, 16)
                taps = io["cv_w_dw"].rearrange("a w d -> (a w d)").rearrange("(j n p) -> j n p", p=P, j=2)
                for j in range(2):
                    sp.dma_start(rows[0:TAP_ROWS, 1 + j, :], taps[j]).then_inc(rows_in, 16)

            @block.vector
            def _(dve):
                nc.vector.memset(rows[:], 0.0).then_inc(cleared, 1)
                dve.wait_ge(turned, 1)
                nc.vector.tensor_copy(K.vec[:, 0:P], ps[:, 0, :]).then_inc(copied, 1)
                for j in range(2):
                    nc.vector.tensor_copy(K.vec[:, P + j * TAP_ROWS:P + (j + 1) * TAP_ROWS], ps[:, 1 + j, 0:TAP_ROWS]).then_inc(copied, 1)

            @block.tensor
            def _(pe):
                pe.wait_ge(rows_in, 16 * (len(VEC_ROWS) + 2))
                for j in range(3):
                    last = nc.tensor.transpose(ps[:, j, :], rows[:, j, :], K.ident[:])
                last.then_inc(turned, 1)


def phase_inproj(K, hT, qT, kT, vT, u):
    nc, io = K.nc, K.io
    RING, NB = 3, D_IN // P
    NA = D_AIN // P
    PAD = T + 4
    segs = [(0, T_CTX, 0), (T_CTX, T_LAT, T_CTX + 2)]
    with ExitStack() as mem:
        wring = mem.enter_context(nc.sbuf_tensor("in_wring", [P, RING, KD, P], F32))
        pad = mem.enter_context(nc.sbuf_tensor("in_pad", [P, RING, PAD], F32))
        ps = mem.enter_context(nc.psum_tensor("in_ps", [P, RING, 1024], F32))
        w_in = [K.sem(f"in_w_in{r}") for r in range(RING)]
        block_done, copied, padded, conv_step = (K.sem("in_" + n) for n in ("block_done", "copied", "padded", "conv_step"))
        w = io["ab_w_in"][0].rearrange("(k p) n -> p k n", p=P)
        wq = w[:, :, 0:D_ATTN].rearrange("p k (g c e) -> p k c g e", g=2, e=HD)
        with nc.Block() as block:
            @block.sync
            def _(sp):
                for b in range(NA):
                    r = b % RING
                    sp.wait_ge(block_done, b + 1)
                    if b < 4:
                        for g in range(2):
                            sp.dma_start(wring[:, r, :, g * HD:(g + 1) * HD], wq[:, :, b, g, :]).then_inc(w_in[r], 16)
                    else:
                        sp.dma_start(wring[:, r], w[:, :, b * P:(b + 1) * P]).then_inc(w_in[r], 32)
                with sp.Fori(0, (NB - NA) // RING) as i:
                    for r in range(RING):
                        sp.wait_ge(block_done, i * RING + (NA + r + 1))
                        sp.dma_start(wring[:, r], w[:, :, bass.ds(i * RING * P + (NA + r) * P, P)]).then_inc(w_in[r], 16)

            @block.tensor
            def _(pe):
                def project(r):
                    for k in range(KD):
                        nc.tensor.matmul(ps[:, r, SQ:512], wring[:, r, k, :], hT[:, k, 0:T_CTX], start=(k == 0), stop=(k == KD - 1))
                        last = nc.tensor.matmul(ps[:, r, 512:1024], wring[:, r, k, :], hT[:, k, T_CTX:T], start=(k == 0), stop=(k == KD - 1))
                    last.then_inc(block_done, 1)

                pe.sem_inc(block_done, RING)
                for b in range(NA):
                    pe.wait_ge(w_in[b % RING], 32 * (b // RING + 1))
                    pe.wait_ge(copied, b + 1)
                    project(b % RING)
                with pe.Fori(0, (NB - NA) // RING) as i:
                    for r in range(RING):
                        pe.wait_ge(w_in[r], i * 16 + (32 * NA // RING + 16))
                        pe.wait_ge(copied, i * RING + (NA + r + 1))
                        project(r)

            @block.scalar
            def _(act):
                act.sem_inc(copied, RING)
                for b in range(NA):
                    act.wait_ge(block_done, RING + b + 1)
                    dst = qT[:, b, :] if b < 4 else (kT, vT)[b - 4][:]
                    nc.scalar.activation(dst, ps[:, b % RING, SQ:1024], ACT.Copy, scale=HD ** -0.5 if b < 4 else 1.0).then_inc(copied, 1)
                with act.Fori(0, (NB - NA) // RING) as i:
                    for r in range(RING):
                        act.wait_ge(block_done, i * RING + (RING + NA + r + 1))
                        act.wait_ge(padded, i * RING + (r + 1))
                        nc.scalar.copy(pad[:, r, 1:1 + T_CTX], ps[:, r, SQ:512])
                        nc.scalar.copy(pad[:, r, T_CTX + 3:T + 3], ps[:, r, 512:1024]).then_inc(copied, 1)

            @block.vector
            def _(dve):
                nc.vector.memset(pad[:], 0.0).then_inc(padded, RING)
                with dve.Fori(0, (NB - NA) // RING) as i:
                    for r in range(RING):
                        dve.wait_ge(copied, i * RING + (RING + NA + r + 1))
                        for tap in range(3):
                            for n, (c, width, start) in enumerate(segs):
                                dst = u[:, bass.ds(i * RING + r, 1), c:c + width].rearrange("p a t -> p (a t)")
                                src = pad[:, r, start + tap:start + tap + width]
                                wt = K.vec[:, bass.ds(i * RING + (VEC["ab_shift_w"] + 15 * tap + r), 1)]
                                if tap == 0:
                                    ins = nc.vector.tensor_scalar(dst, src, wt, None, ALU.mult)
                                else:
                                    dve.wait_ge(conv_step, i * (RING * 6) + (r * 6 + 2 * (tap - 1) + n + 1))
                                    ins = nc.vector.scalar_tensor_tensor(dst, src, wt, dst, ALU.mult, ALU.add)
                                ins.then_inc(conv_step, 1)
                        dve.wait_ge(conv_step, i * (RING * 6) + (r * 6 + 6))
                        dve.sem_inc(padded, 1)


def phase_attention(K, qT, kT, vT, mixT):
    nc, io, ident = K.nc, K.io, K.ident
    with ExitStack() as mem:
        sb = lambda n, s, d=F32: mem.enter_context(nc.sbuf_tensor("at_" + n, s, d))
        rope, perm, mask = sb("rope", [P, 2, T_LAT]), sb("perm", [P, P]), sb("mask", [P, 7 * P])
        kctx, vctx, kcT = sb("kctx", [P, P]), sb("vctx", [P, P]), sb("kcT", [P, P])
        kvtok = sb("kvtok", [P, NT + 1, P])
        sink, rot = sb("sink", [P, HEADS]), sb("rot", [P, 2, T_LAT])
        s, pT = sb("s", [P, 2, 4 * P]), sb("pT", [P, 2, 4 * P])
        st = sb("st", [P, 2, 6])
        ps_s = mem.enter_context(nc.psum_tensor("at_ps_s", [P, 2, 512], F32))
        ps_t = mem.enter_context(nc.psum_tensor("at_ps_t", [P, 2, 512], F32))
        ps_o = mem.enter_context(nc.psum_tensor("at_ps_o", [P, 2, 512], F32))
        const_in, kv_turned, kv_copied, kv_out = (K.sem("at_" + n) for n in ("const_in", "kv_turned", "kv_copied", "kv_out"))
        rot_done, rot_step, roped = (K.sem("at_" + n) for n in ("rot_done", "rot_step", "roped"))
        s_done, masked, negated, expd, den_step, normed, p_turned, p_copied, o_done, o_copied = (
            K.sem("at_" + n) for n in ("s_done", "masked", "negated", "expd", "den_step", "normed", "p_turned", "p_copied", "o_done", "o_copied"))
        blocks = [(4, [0]), (4, [None, 1, 2]), (0, [None, 1, 2, 3]), (0, [None, 2, 3, 4]), (0, [None, 3, 4])]
        items = [(t, c, g) for t in range(NT) for c in range(4) for g in range(2)]
        with nc.Block() as block:
            @block.sync
            def _(sp):
                sp.dma_start(perm[:], K.const["ropeperm"]).then_inc(const_in, 16)
                sp.dma_start(rope[:].rearrange("p a t -> p (a t)"), K.const["rope"]).then_inc(const_in, 16)
                sp.dma_start(kctx[:], io["cache_k"][0, 0].rearrange("t g e -> t (g e)")).then_inc(const_in, 16)
                sp.dma_start(vctx[:], io["cache_v"][0, 0].rearrange("t g e -> t (g e)")).then_inc(const_in, 16)
                sp.dma_start(mask[:], K.const["amask"]).then_inc(const_in, 16)
                sp.dma_start(sink[:], io["ab_sink"][0].partition_broadcast(P)).then_inc(const_in, 16)
                sp.wait_ge(kv_copied, 3)
                sp.dma_start(K.outs[2][0, 0].rearrange("t g e -> t (g e)"), kvtok[:, NT, :]).then_inc(kv_out, 16)
                sp.dma_start(K.outs[3][0, 0].rearrange("t g e -> t (g e)"), kvtok[:, 0, :]).then_inc(kv_out, 16)
                sp.wait_ge(kv_out, 32)

            @block.tensor
            def _(pe):
                for n in range(NT + 1):
                    src = vT[:, n * P:(n + 1) * P] if n < NT else kT[:, 0:P]
                    last = nc.tensor.transpose(ps_t[:, n // 4, (n % 4) * P:(n % 4 + 1) * P], src, ident[:])
                    if n == 3:
                        last.then_inc(kv_turned, 1)
                pe.wait_ge(const_in, 96)
                nc.tensor.transpose(ps_t[:, 1, 2 * P:3 * P], kctx[:], ident[:]).then_inc(kv_turned, 1)
                for n in range(5):
                    if n >= 2:
                        pe.wait_ge(rot_step, 3 * (n - 1))
                    src = qT[:, n, T_CTX:T] if n < 4 else kT[:, T_CTX:T]
                    nc.tensor.matmul(ps_s[:, n % 2, :], perm[:], src, start=True, stop=True).then_inc(rot_done, 1)

                def scores(n):
                    t, c, g = items[n]
                    if n >= 2:
                        pe.wait_ge(masked, n - 1)
                    rows = slice(g * HD, (g + 1) * HD)
                    q = qT[rows, c, t * P:(t + 1) * P]
                    tiles = blocks[t][1]
                    at = 0
                    if tiles[0] is None:
                        nc.tensor.matmul(ps_s[:, n % 2, 0:P], q, kcT[rows, :], start=True, stop=True)
                        tiles, at = tiles[1:], P
                    width = len(tiles) * P
                    nc.tensor.matmul(ps_s[:, n % 2, at:at + width], q, kT[rows, tiles[0] * P:tiles[0] * P + width],
                                     start=True, stop=True).then_inc(s_done, 1)

                def turn(n):
                    pe.wait_ge(normed, n + 1)
                    if n >= 2:
                        pe.wait_ge(p_copied, n - 1)
                    for b in range(len(blocks[items[n][0]][1])):
                        last = nc.tensor.transpose(ps_t[:, n % 2, b * P:(b + 1) * P], s[:, n % 2, b * P:(b + 1) * P], ident[:])
                    last.then_inc(p_turned, 1)

                def weigh(n):
                    t, c, g = items[n]
                    pe.wait_ge(p_copied, n + 1)
                    if c == 0 and g == 0 and t >= 2:
                        pe.wait_ge(o_copied, t - 1)
                    tiles = blocks[t][1]
                    for b, kt in enumerate(tiles):
                        v = vctx[:, g * HD:(g + 1) * HD] if kt is None else kvtok[:, kt, g * HD:(g + 1) * HD]
                        last = nc.tensor.matmul(ps_o[g * HD:(g + 1) * HD, t % 2, c * P:(c + 1) * P], v, pT[:, n % 2, b * P:(b + 1) * P],
                                                start=(b == 0), stop=(b == len(tiles) - 1))
                    last.then_inc(o_done, 1)

                pe.wait_ge(roped, 5)
                pe.wait_ge(kv_copied, 3)
                N = len(items)
                for n in range(N + 2):
                    if n < N:
                        scores(n)
                    if 1 <= n <= N:
                        turn(n - 1)
                    if n >= 2:
                        weigh(n - 2)

            @block.vector
            def _(dve):
                dve.wait_ge(const_in, 96)
                for n in range(5):
                    dst = qT[:, n, T_CTX:T] if n < 4 else kT[:, T_CTX:T]
                    dve.wait_ge(rot_done, n + 1)
                    if n == 4:
                        dve.wait_ge(kv_turned, 1)
                    if n >= 2:
                        dve.wait_ge(roped, n - 1)
                    nc.vector.tensor_tensor(rot[:, n % 2, :], ps_s[:, n % 2, :], rope[:, 1, :], ALU.mult).then_inc(rot_step, 1)
                    nc.vector.tensor_tensor(dst, dst, rope[:, 0, :], ALU.mult).then_inc(rot_step, 1)
                    dve.wait_ge(rot_step, 3 * n + 2)
                    nc.vector.sem_inc(rot_step, 1)
                    nc.vector.tensor_tensor(dst, dst, rot[:, n % 2, :], ALU.add).then_inc(roped, 1)
                for n, (t, c, g) in enumerate(items):
                    p = n % 2
                    first, tiles = blocks[t]
                    width = len(tiles) * P
                    dve.wait_ge(s_done, n + 1)
                    if n >= 2:
                        dve.wait_ge(p_turned, n - 1)
                    nc.vector.tensor_tensor_reduce(out=s[:, p, 0:width], in0=ps_s[:, p, 0:width], in1=mask[:, first * P:first * P + width], scale=1.0,
                                                   scalar=sink[:, g * 4 + c:g * 4 + c + 1], op0=ALU.add, op1=ALU.max,
                                                   accum_out=st[:, p, 0:1]).then_inc(masked, 1)
                    dve.wait_ge(masked, n + 1)
                    nc.vector.tensor_scalar(st[:, p, 1:2], st[:, p, 0:1], -1.0, None, ALU.mult).then_inc(negated, 1)
                    dve.wait_ge(expd, 2 * (n + 1))
                    nc.vector.tensor_tensor(st[:, p, 4:5], st[:, p, 2:3], st[:, p, 3:4], ALU.add).then_inc(den_step, 1)
                    dve.wait_ge(den_step, 2 * n + 1)
                    nc.vector.reciprocal(st[:, p, 5:6], st[:, p, 4:5]).then_inc(den_step, 1)
                    dve.wait_ge(den_step, 2 * n + 2)
                    nc.vector.tensor_scalar(s[:, p, 0:width], s[:, p, 0:width], st[:, p, 5:6], None, ALU.mult).then_inc(normed, 1)

            @block.scalar
            def _(act):
                act.wait_ge(kv_turned, 1)
                nc.scalar.copy(kvtok[:, 0:4, :].rearrange("p t c -> p (t c)"), ps_t[:, 0, :]).then_inc(kv_copied, 1)
                act.wait_ge(kv_turned, 2)
                nc.scalar.copy(kvtok[:, 4:6, :].rearrange("p t c -> p (t c)"), ps_t[:, 1, 0:2 * P]).then_inc(kv_copied, 1)
                nc.scalar.copy(kcT[:], ps_t[:, 1, 2 * P:3 * P]).then_inc(kv_copied, 1)

                def copy_p(n):
                    width = len(blocks[items[n][0]][1]) * P
                    act.wait_ge(p_turned, n + 1)
                    if n >= 2:
                        act.wait_ge(o_done, n - 1)
                    nc.scalar.copy(pT[:, n % 2, 0:width], ps_t[:, n % 2, 0:width]).then_inc(p_copied, 1)

                def copy_o(t):
                    act.wait_ge(o_done, 8 * (t + 1))
                    nc.scalar.copy(mixT[:, 0:4, t * P:(t + 1) * P], ps_o[:, t % 2, :].rearrange("p (c q) -> p c q", c=4)).then_inc(o_copied, 1)

                N = len(items)
                for n in range(N):
                    t, c, g = items[n]
                    p, width = n % 2, len(blocks[t][1]) * P
                    act.wait_ge(negated, n + 1)
                    nc.scalar.activation(s[:, p, 0:width], s[:, p, 0:width], ACT.Exp, bias=st[:, p, 1:2], accum_out=st[:, p, 2:3]).then_inc(expd, 1)
                    nc.scalar.activation(st[:, p, 3:4], sink[:, g * 4 + c:g * 4 + c + 1], ACT.Exp, bias=st[:, p, 1:2]).then_inc(expd, 1)
                    if n >= 1:
                        copy_p(n - 1)
                    if n >= 10 and n % 8 == 2:
                        copy_o(n // 8 - 1)
                copy_p(N - 1)
                copy_o(NT - 1)


def mm640(nc, ps, b, lhsT, rhs):
    nc.tensor.matmul(ps[:, b, SQ:512], lhsT, rhs[:, 0:T_CTX], start=True, stop=True)
    return nc.tensor.matmul(ps[:, b, 512:1024], lhsT, rhs[:, T_CTX:T], start=True, stop=True)


def phase_scan_prep(K, u, q1, q2, k1, k2, pc, mixT):
    nc, io = K.nc, K.io
    NCK = T // CH
    N = 2 * NCC
    with ExitStack() as mem:
        sb = lambda n, s, d=F32: mem.enter_context(nc.sbuf_tensor("sp_" + n, s, d))
        w2, a2, g2 = sb("w2", [P, D_RW]), sb("a2", [P, D_RW]), sb("g2", [P, D_RW])
        hsum, reset = sb("hsum", [P, P]), sb("reset", [P, T])
        oneka, rkh = sb("oneka", [P, NCC]), sb("rkh", [P, NCC])
        nrm, kt, ktsum = (sb(n, [P, T]) for n in ("nrm", "kt", "ktsum"))
        kh, a, ld, cs, ce, en = (sb(n, [P, 2, T]) for n in ("kh", "a", "ld", "cs", "ce", "en"))
        ps = mem.enter_context(nc.psum_tensor("sp_ps", [P, 4, 1024], F32))
        S = {n: K.sem("sp_" + n) for n in ("par_in", "own", "lora_done", "kk_done", "sq_done", "n2_done", "root_done",
                                           "z_done", "az_done", "sig_done", "a_done", "c_ready", "exps_done", "ops_done",
                                           "g_done", "g_copied", "bonus_prod", "bonus_sum", "bonus_read", "kh_done")}
        RATE = float(np.exp(-0.5))
        vcol = lambda name, j: K.vec[:, VEC[name] + j:VEC[name] + j + 1]
        with nc.Block() as block:
            @block.sync
            def _(sp):
                sp.dma_start(w2[:], io["ab_w2"][0].rearrange("d r c -> (d r) c")).then_inc(S["par_in"], 16)
                sp.dma_start(a2[:], io["ab_a2"][0].rearrange("d r c -> (d r) c")).then_inc(S["par_in"], 16)
                sp.dma_start(g2[:], io["ab_g2"][0]).then_inc(S["par_in"], 16)
                sp.dma_start(hsum[:], K.const["headsum"]).then_inc(S["par_in"], 16)
                sp.dma_start(reset[:], K.const["reset"]).then_inc(S["par_in"], 16)

            @block.tensor
            def _(pe):
                def gates(n):
                    cols, rows = slice(n // 2 * P, (n // 2 + 1) * P), slice(64 * (n % 2), 64 * (n % 2) + 64)
                    if n:
                        pe.wait_ge(S["sig_done"], n)
                        pe.wait_ge(S["a_done"], n)
                    mm640(nc, ps, 1, w2[rows, cols], u[rows, 12, :]).then_inc(S["z_done"], 1)
                    mm640(nc, ps, 2, a2[rows, cols], u[rows, 13, :]).then_inc(S["az_done"], 1)

                def norms(cc):
                    pe.wait_ge(S["sq_done"], cc + 1)
                    mm640(nc, ps, 0, hsum[:], nrm).then_inc(S["n2_done"], 1)

                def bonus(cc):
                    pe.wait_ge(S["g_copied"], cc + 1)
                    pe.wait_ge(S["bonus_prod"], cc + 1)
                    mm640(nc, ps, 3, hsum[:], kt).then_inc(S["bonus_sum"], 1)

                pe.wait_ge(S["par_in"], 80)
                pe.wait_ge(S["lora_done"], 2)
                norms(0)
                gates(0)
                for n in range(N):
                    cc, d = n // 2, n % 2
                    if n + 1 < N:
                        gates(n + 1)
                    if d == 0:
                        if cc + 1 < NCC:
                            norms(cc + 1)
                        if cc:
                            bonus(cc - 1)
                    else:
                        if cc:
                            pe.wait_ge(S["bonus_read"], cc)
                        mm640(nc, ps, 3, g2[:, cc * P:(cc + 1) * P], u[:, 14, :]).then_inc(S["g_done"], 1)
                bonus(NCC - 1)

            @block.scalar
            def _(act):
                def root(cc):
                    act.wait_ge(S["kk_done"], cc + 1)
                    if cc:
                        act.wait_ge(S["kh_done"], cc)
                    nc.scalar.activation(nrm[:], kh[:, cc % 2, :], ACT.Square).then_inc(S["sq_done"], 1)
                    act.wait_ge(S["n2_done"], cc + 1)
                    nc.scalar.activation(nrm[:], ps[:, 0, SQ:1024], ACT.Sqrt).then_inc(S["root_done"], 1)

                def gates(n):
                    cc, d, p = n // 2, n % 2, n % 2
                    act.wait_ge(S["z_done"], n + 1)
                    if n >= 2:
                        act.wait_ge(S["ops_done"], n - 1)
                    nc.scalar.activation(ld[:, p, :], ps[:, 1, SQ:1024], ACT.Sigmoid, bias=vcol("ab_w0", 4 * d + cc)).then_inc(S["sig_done"], 1)
                    act.wait_ge(S["az_done"], n + 1)
                    nc.scalar.activation(a[:, p, :], ps[:, 2, SQ:1024], ACT.Sigmoid, bias=vcol("ab_a0", 4 * d + cc)).then_inc(S["a_done"], 1)

                nc.scalar.activation(u[:, 12, :], u[:, 12, :], ACT.Tanh).then_inc(S["lora_done"], 1)
                nc.scalar.activation(u[:, 14, :], u[:, 14, :], ACT.Sigmoid).then_inc(S["lora_done"], 1)
                root(0)
                gates(0)
                for n in range(N):
                    cc, d, p = n // 2, n % 2, n % 2
                    if n + 1 < N:
                        gates(n + 1)
                    act.wait_ge(S["c_ready"], n + 1)
                    nc.scalar.activation(ce[:, p, :], ce[:, p, :], ACT.Exp, scale=-RATE).then_inc(S["exps_done"], 1)
                    nc.scalar.activation(en[:, p, :], cs[:, p, :], ACT.Exp, scale=RATE).then_inc(S["exps_done"], 1)
                    nc.scalar.activation(q2[:, d, cc, :], cs[:, p, :], ACT.Exp, scale=-RATE).then_inc(S["exps_done"], 1)
                    if d == 0:
                        if cc + 1 < NCC:
                            root(cc + 1)
                    else:
                        act.wait_ge(S["g_done"], cc + 1)
                        nc.scalar.copy(mixT[:, 4 + cc, :], ps[:, 3, SQ:1024]).then_inc(S["g_copied"], 1)

            @block.vector
            def _(dve):
                step = chain_on(dve, S["own"])
                rkv = lambda cc: (u[:, cc, :], u[:, 4 + cc, :], u[:, 8 + cc, :])

                def scaled_keys(cc):
                    nc.vector.tensor_scalar(kh[:, cc % 2, :], rkv(cc)[1], vcol("ab_k_k", cc), None, ALU.mult).then_inc(S["kk_done"], 1)

                def unit_keys(cc):
                    dve.wait_ge(S["root_done"], cc + 1)
                    step(nc.vector.tensor_scalar(nrm[:], nrm[:], 1e-12, None, ALU.max))
                    step(nc.vector.reciprocal(nrm[:], nrm[:]))
                    nc.vector.tensor_tensor(kh[:, cc % 2, :], kh[:, cc % 2, :], nrm[:], ALU.mult).then_inc(S["kh_done"], 1)
                    dve.wait_ge(S["kh_done"], cc + 1)

                def decays(n):
                    p = n % 2
                    dve.wait_ge(S["sig_done"], n + 1)
                    step(nc.vector.tensor_tensor_scan(cs[:, p, :], reset[:], ld[:, p, :], 0.0, ALU.mult, ALU.add))
                    if p == 0:
                        nc.vector.tensor_tensor(ce[:, p, :], cs[:, p, :], ld[:, p, :], ALU.subtract).then_inc(S["c_ready"], 1)
                    else:
                        c3, e3 = (b[:, p, :].rearrange("p (n c) -> p n c", c=CH) for b in (cs, ce))
                        step(nc.vector.tensor_tensor(e3, c3[:, :, CH - 1:CH].to_broadcast([P, NCK, CH]), c3, ALU.subtract))
                        nc.vector.tensor_tensor(cs[:, p, :], ce[:, p, :], ld[:, p, :], ALU.add).then_inc(S["c_ready"], 1)

                def operands(n):
                    cc, d, p = n // 2, n % 2, n % 2
                    r, k, _ = rkv(cc)
                    kd = ktsum if d == 0 else kt
                    dve.wait_ge(S["a_done"], n + 1)
                    step(nc.vector.tensor_scalar(kd[:], a[:, p, :], vcol("ab_k_a", cc), oneka[:, cc:cc + 1], ALU.mult, ALU.add), False)
                    step(nc.vector.tensor_tensor(a[:, p, :], a[:, p, :], kh[:, cc % 2, :], ALU.mult))
                    step(nc.vector.tensor_tensor(kd[:], kd[:], k, ALU.mult))
                    dve.wait_ge(S["exps_done"], 3 * (n + 1))
                    last = CH - 1 if d == 0 else 0
                    step(nc.vector.tensor_copy(pc[:, :, d, cc], q2[:, d, cc, :].rearrange("p (n c) -> p n c", c=CH)[:, :, last]), False)
                    step(nc.vector.tensor_tensor(k1[:, d, cc, :], a[:, p, :], en[:, p, :], ALU.mult), False)
                    step(nc.vector.tensor_tensor(k2[:, d, cc, :], kd[:], en[:, p, :], ALU.mult), False)
                    step(nc.vector.tensor_tensor(q1[:, d, cc, :], kh[:, cc % 2, :], ce[:, p, :], ALU.mult))
                    nc.vector.tensor_tensor(q2[:, d, cc, :], q2[:, d, cc, :], r, ALU.mult).then_inc(S["ops_done"], 1)

                def bonus(cc):
                    r, _, v = rkv(cc)
                    dve.wait_ge(S["bonus_sum"], cc + 1)
                    nc.vector.tensor_tensor(r, ps[:, 3, SQ:1024], v, ALU.mult).then_inc(S["bonus_read"], 1)

                step(nc.vector.tensor_scalar(oneka[:], K.vec[:, VEC["ab_k_a"]:VEC["ab_k_a"] + NCC], -1.0, 1.0, ALU.mult, ALU.add), False)
                step(nc.vector.tensor_scalar(rkh[:], K.vec[:, VEC["ab_r_k"]:VEC["ab_r_k"] + NCC], 0.5, None, ALU.mult))
                scaled_keys(0)
                dve.wait_ge(S["par_in"], 80)
                unit_keys(0)
                decays(0)
                for n in range(N):
                    cc, d = n // 2, n % 2
                    if cc + 1 < NCC:
                        if d == 0:
                            scaled_keys(cc + 1)
                        else:
                            unit_keys(cc + 1)
                    if n + 1 < N:
                        decays(n + 1)
                    operands(n)
                    if d == 0:
                        if cc:
                            bonus(cc - 1)
                    else:
                        dve.wait_ge(S["ops_done"], n + 1)
                        step(nc.vector.tensor_tensor(ktsum[:], ktsum[:], kt[:], ALU.add))
                        nc.vector.scalar_tensor_tensor(kt[:], ktsum[:], rkh[:, cc:cc + 1], rkv(cc)[0], ALU.mult, ALU.mult).then_inc(S["bonus_prod"], 1)
                bonus(NCC - 1)


def phase_scan(K, tag, first, chunks, u, q1, q2, k1, k2, pc, state_in, state_out):
    nc = K.nc
    G = 2
    LEVELS = 5
    PE_N, ACT_N, DVE_N, POOL_N = 8 + 3 * LEVELS - 1 + 4, 2 + LEVELS + 3, 5 + LEVELS + 2, 8
    with ExitStack() as mem:
        sb = lambda n, s=(P, G, NCC, CH), d=F32: mem.enter_context(nc.sbuf_tensor(f"sc{tag}_{n}", list(s), d))
        q1c, q2c, k1c, k2c, vc = sb("q1c"), sb("q2c"), sb("k1c"), sb("k2c"), sb("vc")
        pair = (P, G, 2, NCC, CH)
        AA, BD, XX = sb("AA", pair), sb("BD", pair), sb("XX", pair)
        A, AT, BT, DT, X, XT = (b[:, :, w] for b in (AA, BD, XX) for w in range(2))
        ET, V, k1T, k2T = sb("ET"), sb("V"), sb("k1T"), sb("k2T")
        M, W, U, S, Sn = sb("M"), sb("W"), sb("U"), sb("S"), sb("Sn")
        pcc = sb("pcc", (P, G, NCC))
        eye = sb("eye", (P, CH))
        smask = sb("smask", (P, 5, G, CH))
        lmask = sb("lmask", (P, 1 + LEVELS, 2, G, CH), mybir.dt.uint8)
        ps = mem.enter_context(nc.psum_tensor(f"sc{tag}_ps", [P, G, 4, 2, NCC, CH], F32))
        const_in = K.sem(f"sc{tag}_const_in")
        state_ready, state_turned, state_sent = (K.sem(f"sc{tag}_" + n) for n in ("state_ready", "state_turned", "state_sent"))
        pool_done, pe_done, act_done, dve_done = ([K.sem(f"sc{tag}_{e}{g}") for g in range(G)] for e in ("pool", "pe", "act", "dve"))
        LM = (1 + LEVELS) * 2 * G * CH // 2
        masks_set = K.sem(f"sc{tag}_masks_set")
        carried = K.sem(f"sc{tag}_carried")
        state_done = K.sem(f"sc{tag}_state_done")
        region = lambda g, r: ps[:, g, r // 2, r % 2]

        PE_W = 8 + 3 * LEVELS - 1
        ACT_W = 2 + LEVELS
        DVE_S = 5 + LEVELS
        after_pe = lambda eng, g, i, k: eng.wait_ge(pe_done[g], i * PE_N + (PE_N + k))
        after_act = lambda eng, g, i, k: eng.wait_ge(act_done[g], i * ACT_N + (ACT_N + k))
        after_dve = lambda eng, g, i, k: eng.wait_ge(dve_done[g], i * DVE_N + (DVE_N + k))
        after_pool = lambda eng, g, i, k: eng.wait_ge(pool_done[g], i * POOL_N + (POOL_N + k))
        start = lambda g, i: i * CH + first if g == 0 else i * (-CH) + (first + (chunks - 1) * CH)
        number = lambda g, i: i + first // CH if g == 0 else i * -1 + (first // CH + chunks - 1)

        with nc.Block() as block:
            def state_rows(dram, d, e):
                return dram[0, 0, d].rearrange("(c e) v k -> e v c k", e=2)[e]

            @block.sync
            def _(sp):
                sp.dma_start(smask[:].rearrange("p a g c -> p (a g c)"), K.const["scanmask"]).then_inc(const_in, 16)
                for n, buf in enumerate((AA, BD)):
                    sp.dma_start(buf[:].rearrange("p g w c t -> p (g w c t)")[:, 0:LM], K.const["levmask"][:, n * LM:(n + 1) * LM]).then_inc(const_in, 16)
                sp.dma_start(eye[:], K.const["eye64"]).then_inc(const_in, 16)
                if state_in is not None:
                    for d in range(G):
                        for e in range(2):
                            sp.dma_start(Sn[64 * e:64 * e + 64, d], state_rows(state_in, d, e)).then_inc(const_in, 16)
                if state_out is not None:
                    sp.wait_ge(state_sent, 1)
                    for d in range(G):
                        for e in range(2):
                            sp.dma_start(state_rows(state_out, d, e), W[64 * e:64 * e + 64, d]).then_inc(state_done, 16)
                    sp.wait_ge(state_done, 64)

            N_CONST = 64 + (64 if state_in is not None else 0)

            @block.gpsimd
            def _(pool):
                pool.wait_ge(const_in, N_CONST)
                for g in range(G):
                    pool.sem_inc(pool_done[g], POOL_N)
                with pool.Fori(0, chunks) as i:
                    for g in range(G):
                        cols, num = bass.ds(start(g, i), CH), number(g, i)
                        after_pe(pool, g, i, -PE_N + PE_W + 3)
                        nc.gpsimd.tensor_copy(k1c[:, g], k1[:, g, :, cols]).then_inc(pool_done[g], 1)
                        nc.gpsimd.tensor_copy(k2c[:, g], k2[:, g, :, cols]).then_inc(pool_done[g], 1)
                        nc.gpsimd.tensor_copy(q1c[:, g], q1[:, g, :, cols]).then_inc(pool_done[g], 1)
                        nc.gpsimd.tensor_copy(q2c[:, g], q2[:, g, :, cols]).then_inc(pool_done[g], 1)
                        nc.gpsimd.tensor_copy(vc[:, g], u[:, 8:12, cols]).then_inc(pool_done[g], 1)
                        after_dve(pool, g, i, 0)
                        nc.gpsimd.tensor_copy(pcc[:, g], pc[:, bass.ds(num, 1), g, :].rearrange("p a c -> p (a c)")).then_inc(pool_done[g], 1)
                        for buf in (X, XT):
                            nc.gpsimd.tensor_copy(buf[:, g], eye[:].unsqueeze(1).to_broadcast([P, NCC, CH])).then_inc(pool_done[g], 1)

            @block.tensor
            def _(pe):
                def heads(g, r, *terms, n_chunk=0):
                    if n_chunk is not None:
                        pe.sem_inc(carried, 1)
                    for c in range(NCC):
                        for e in range(2):
                            rows = slice(64 * e, 64 * e + 64)
                            for n, (l, m) in enumerate(terms):
                                last = nc.tensor.matmul(region(g, r)[rows, c, :], l[rows] if l is eye else l[rows, g, c, :],
                                                        m[rows] if m is eye else m[rows, g, c, :],
                                                        start=(n == 0), stop=(n == len(terms) - 1))
                    last.then_inc(pe_done[g], 1)

                pe.wait_ge(const_in, N_CONST)
                if state_in is not None:
                    for g in range(G):
                        for c in range(NCC):
                            for e in range(2):
                                rows = slice(64 * e, 64 * e + 64)
                                last = nc.tensor.matmul(region(g, 0)[rows, c, :], Sn[rows, g, c, :], eye[rows], start=True, stop=True)
                    last.then_inc(state_turned, 1)
                for g in range(G):
                    pe.sem_inc(pe_done[g], PE_N)
                pe.wait_ge(state_ready, 1)
                with pe.Fori(0, chunks) as i:
                    for g in range(G):
                        after_act(pe, g, i, 0)
                        after_dve(pe, g, i, 0)
                        after_pool(pe, g, i, 5)
                        heads(g, 0, (q1c, k1c))
                        for r, term in enumerate(((k1c, q1c), (k2c, q1c), (k2c, q2c), (k1c, q2c), (vc, eye), (k1c, eye), (k2c, eye))):
                            heads(g, 1 + r, term, n_chunk=None)
                    for l in range(LEVELS):
                        for g in range(G):
                            after_dve(pe, g, i, 5 + l)
                            heads(g, 0, (AT, X))
                        for g in range(G):
                            after_act(pe, g, i, 2 + l + 1)
                            heads(g, 3, (M, XT))
                            if l < LEVELS - 1:
                                heads(g, 2, (XT, M), n_chunk=None)
                    for g in range(G):
                        after_dve(pe, g, i, DVE_S)
                        heads(g, 4, (q1c, S), (BT, V))
                    for g in range(G):
                        after_act(pe, g, i, ACT_W + 1)
                        heads(g, 6, (XT, W))
                    for g in range(G):
                        after_act(pe, g, i, ACT_W + 2)
                        heads(g, 0, (S, q2c), (V, DT), (U, ET))
                        heads(g, 2, (k2T, V), (k1T, U), n_chunk=None)
                if state_out is not None:
                    for g in range(G):
                        pe.wait_ge(dve_done[g], DVE_N * (chunks + 1))
                        pe.wait_ge(act_done[g], ACT_N * (chunks + 1))
                        for c in range(NCC):
                            for e in range(2):
                                rows = slice(64 * e, 64 * e + 64)
                                last = nc.tensor.matmul(region(g, 0)[rows, c, :], S[rows, g, c, :], eye[rows], start=True, stop=True)
                    last.then_inc(state_turned, 1)

            @block.scalar
            def _(act):
                act.wait_ge(const_in, N_CONST)
                for g in range(G):
                    act.sem_inc(act_done[g], ACT_N)
                with act.Fori(0, chunks) as i:
                    for g in range(G):
                        for k, (buf, scale) in enumerate(((k1T, -1.0), (k2T, 1.0))):
                            after_pe(act, g, i, 8)
                            nc.scalar.activation(buf[:, g], region(g, 6 + k), ACT.Copy, scale=scale).then_inc(act_done[g], 1)
                    for l in range(LEVELS):
                        for g in range(G):
                            after_pe(act, g, i, 8 + 3 * l + 1)
                            nc.scalar.copy(M[:, g], region(g, 0)).then_inc(act_done[g], 1)
                    for g in range(G):
                        after_pe(act, g, i, PE_W + 1)
                        nc.scalar.copy(W[:, g], region(g, 4)).then_inc(act_done[g], 1)
                    for g in range(G):
                        after_pe(act, g, i, PE_W + 2)
                        nc.scalar.copy(U[:, g], region(g, 6)).then_inc(act_done[g], 1)
                    for g in range(G):
                        after_pe(act, g, i, PE_W + 3)
                        after_pool(act, g, i, 4)
                        nc.scalar.copy(q2[:, g, :, bass.ds(start(g, i), CH)], region(g, 0)).then_inc(act_done[g], 1)
                if state_out is not None:
                    act.wait_ge(state_turned, 1)
                    nc.scalar.copy(W[:], ps[:, :, 0, 0]).then_inc(state_sent, 1)

            @block.vector
            def _(dve):
                dve.wait_ge(const_in, N_CONST)
                for n, buf in enumerate((AA, BD)):
                    nc.vector.tensor_copy(lmask[:].rearrange("p l w g c -> p (l w g c)")[:, n * LM:(n + 1) * LM],
                                          buf[:].rearrange("p g w c t -> p (g w c t)")[:, 0:LM]).then_inc(masks_set, 1)
                dve.wait_ge(masks_set, 2)
                if state_in is None:
                    nc.vector.memset(S[:], 0.0).then_inc(state_ready, 1)
                else:
                    dve.wait_ge(state_turned, 1)
                    nc.vector.tensor_copy(S[:], ps[:, :, 0, 0]).then_inc(state_ready, 1)
                for g in range(G):
                    dve.sem_inc(dve_done[g], DVE_N)
                dve.wait_ge(state_ready, 1)
                with dve.Fori(0, chunks) as i:
                    for g in range(G):
                        both = lambda b: ps[:, g, b]
                        for k, buf in enumerate((AA, BD)):
                            after_pe(dve, g, i, 2 * k + 2)
                            nc.vector.tensor_tensor(buf[:, g], both(k), smask[:, 2 * k:2 * k + 2, g].unsqueeze(2).to_broadcast([P, 2, NCC, CH]),
                                                    ALU.mult).then_inc(dve_done[g], 1)
                        after_pe(dve, g, i, 6)
                        nc.vector.tensor_tensor(ET[:, g], region(g, 4), smask[:, 4, g].unsqueeze(1).to_broadcast([P, NCC, CH]), ALU.mult).then_inc(dve_done[g], 1)
                        nc.vector.tensor_copy(V[:, g], region(g, 5)).then_inc(dve_done[g], 1)
                        after_pool(dve, g, i, 8)
                        after_dve(dve, g, i, 1)
                        dve.sem_inc(carried, 1)
                        nc.vector.copy_predicated(XX[:, g], lmask[:, 0, :, g].unsqueeze(2).to_broadcast([P, 2, NCC, CH]), AA[:, g]).then_inc(dve_done[g], 1)
                    for l in range(LEVELS):
                        for g in range(G):
                            last = l == LEVELS - 1
                            after_pe(dve, g, i, 8 + 3 * l + (2 if last else 3))
                            after_dve(dve, g, i, 5 + l)
                            dve.sem_inc(carried, 1)
                            some = slice(1, 2) if last else slice(0, 2)
                            nc.vector.copy_predicated(XX[:, g, some], lmask[:, l + 1, some, g].unsqueeze(2).to_broadcast([P, 2 - last, NCC, CH]),
                                                      ps[:, g, 1, some]).then_inc(dve_done[g], 1)
                    for g in range(G):
                        after_pe(dve, g, i, PE_W + 4)
                        nc.vector.tensor_tensor(Sn[:, g], S[:, g], region(g, 2), ALU.add).then_inc(dve_done[g], 1)
                        after_dve(dve, g, i, DVE_S + 1)
                        nc.vector.tensor_tensor(S[:, g], Sn[:, g], pcc[:, g].unsqueeze(2).to_broadcast([P, NCC, CH]), ALU.mult).then_inc(dve_done[g], 1)


def phase_scan_out(K, u, q2, mixT):
    nc = K.nc
    with ExitStack() as mem:
        sb = lambda n, s, d=F32: mem.enter_context(nc.sbuf_tensor("so_" + n, s, d))
        hmean = sb("hmean", [P, P])
        y, sq, sd = sb("y", [P, NCC, T]), sb("sq", [P, NCC, T]), sb("sd", [P, NCC, T])
        ps = mem.enter_context(nc.psum_tensor("so_ps", [P, 4, 1024], F32))
        S = {n: K.sem("so_" + n) for n in ("hsum_in", "own", "mean_const", "y_done", "mean_done", "centred", "squared", "var_done", "root_done")}
        with nc.Block() as block:
            @block.sync
            def _(sp):
                sp.dma_start(hmean[:], K.const["headsum"]).then_inc(S["hsum_in"], 16)

            @block.tensor
            def _(pe):
                pe.wait_ge(S["mean_const"], 1)
                for cc in range(NCC):
                    pe.wait_ge(S["y_done"], cc + 1)
                    if cc >= 2:
                        pe.wait_ge(S["centred"], cc - 1)
                    mm640(nc, ps, cc % 2, hmean[:], y[:, cc, :]).then_inc(S["mean_done"], 1)
                for cc in range(NCC):
                    pe.wait_ge(S["squared"], cc + 1)
                    if cc >= 2:
                        pe.wait_ge(S["root_done"], cc - 1)
                    mm640(nc, ps, 2 + cc % 2, hmean[:], sq[:, cc, :]).then_inc(S["var_done"], 1)

            @block.scalar
            def _(act):
                for cc in range(NCC):
                    act.wait_ge(S["centred"], cc + 1)
                    nc.scalar.activation(sq[:, cc, :], y[:, cc, :], ACT.Square).then_inc(S["squared"], 1)
                for cc in range(NCC):
                    act.wait_ge(S["var_done"], cc + 1)
                    nc.scalar.activation(sd[:, cc, :], ps[:, 2 + cc % 2, SQ:1024], ACT.Sqrt, bias=K.gneps[:, 0:1]).then_inc(S["root_done"], 1)

            @block.vector
            def _(dve):
                step = chain_on(dve, S["own"])
                dve.wait_ge(S["hsum_in"], 16)
                nc.vector.tensor_scalar(hmean[:], hmean[:], 1.0 / HD, None, ALU.mult).then_inc(S["mean_const"], 1)
                for cc in range(NCC):
                    nc.vector.tensor_tensor(y[:, cc, :], q2[:, 0, cc, :], q2[:, 1, cc, :], ALU.add).then_inc(S["y_done"], 1)
                for cc in range(NCC):
                    dve.wait_ge(S["mean_done"], cc + 1)
                    nc.vector.tensor_tensor(y[:, cc, :], y[:, cc, :], ps[:, cc % 2, SQ:1024], ALU.subtract).then_inc(S["centred"], 1)
                for cc in range(NCC):
                    g, b = (K.vec[:, VEC[n] + cc:VEC[n] + cc + 1] for n in ("ab_gn_g", "ab_gn_b"))
                    out = mixT[:, 4 + cc, :]
                    dve.wait_ge(S["root_done"], cc + 1)
                    step(nc.vector.reciprocal(sd[:, cc, :], sd[:, cc, :]))
                    step(nc.vector.tensor_tensor(y[:, cc, :], y[:, cc, :], sd[:, cc, :], ALU.mult))
                    step(nc.vector.tensor_scalar(y[:, cc, :], y[:, cc, :], g, b, ALU.mult, ALU.add))
                    step(nc.vector.tensor_tensor(y[:, cc, :], y[:, cc, :], u[:, cc, :], ALU.add))
                    step(nc.vector.tensor_tensor(out, out, y[:, cc, :], ALU.mult))


def phase_outproj(K, tag, srcT, load_w, w_total, layer, bias=None):
    nc = K.nc
    with ExitStack() as mem:
        sb = lambda n, s, d=F32: mem.enter_context(nc.sbuf_tensor(tag + n, s, d))
        w = sb("w", [P, KD, D])
        rows = sb("rows", [P, 2, D])
        brow = sb("brow", [P, D])
        y = sb("y", [P, NT, D])
        ps = mem.enter_context(nc.psum_tensor(tag + "ps", [P, 4, D], F32))
        w_in, rows_in, y_done, own = (K.sem(tag + n) for n in ("w_in", "rows_in", "y_done", "own"))
        gated = K.sem(tag + "gated")
        with nc.Block() as block:
            @block.sync
            def _(sp):
                load_w(sp, w, w_in)
                for s in range(2):
                    load_row(sp, K, rows[:, s, :], s, layer, 2, rows_in)
                if bias is not None:
                    sp.dma_start(brow[:], bias.partition_broadcast(P)).then_inc(rows_in, 16)
            @block.tensor
            def _(pe):
                pe.wait_ge(w_in, w_total)
                for t in range(NT):
                    if t >= 4:
                        pe.wait_ge(gated, t - 3)
                    for half in range(2):
                        for k in range(KD):
                            last = nc.tensor.matmul(ps[:, t % 4, half * 512:(half + 1) * 512], srcT[:, k, t * P:(t + 1) * P],
                                                    w[:, k, half * 512:(half + 1) * 512], start=(k == 0), stop=(k == KD - 1))
                    last.then_inc(y_done, 1)

            @block.vector
            def _(dve):
                step = chain_on(dve, own)
                dve.wait_ge(rows_in, 32 if bias is None else 48)
                for t in range(NT):
                    dve.wait_ge(y_done, t + 1)
                    if bias is None:
                        nc.vector.tensor_tensor(y[:, t, :], ps[:, t % 4, :], rows[:, min(t, 1), :], ALU.mult).then_inc(gated, 1)
                        dve.wait_ge(gated, t + 1)
                    else:
                        nc.vector.tensor_tensor(y[:, t, :], ps[:, t % 4, :], brow[:], ALU.add).then_inc(gated, 1)
                        dve.wait_ge(gated, t + 1)
                        step(nc.vector.tensor_tensor(y[:, t, :], y[:, t, :], rows[:, min(t, 1), :], ALU.mult))
                    step(nc.vector.tensor_tensor(K.x[:, t, :], K.x[:, t, :], y[:, t, :], ALU.add))


def load_w_out(K):
    w = K.io["ab_w_out"][0]

    def load(eng, dst, sem):
        for k in range(KD):
            for g in range(2):
                row = (k * HD + g * D_ATTN // 2) if k < 4 else k * P + g * HD
                eng.dma_start(dst[g * HD:(g + 1) * HD, k, :], w[row:row + HD, :]).then_inc(sem, 16)
    return load


def phase_mixer_even(K):
    nc = K.nc
    with ExitStack() as mem:
        sb = lambda s, n, shape: s.enter_context(nc.sbuf_tensor("ev_" + n, shape, F32))
        mixT = sb(mem, "mixT", [P, KD, T])
        with ExitStack() as mixing:
            u = sb(mixing, "u", [P, 15, T])
            with ExitStack() as first:
                qT, kT, vT = sb(first, "qT", [P, 4, T]), sb(first, "kT", [P, T]), sb(first, "vT", [P, T])
                with ExitStack() as normed:
                    hT = sb(normed, "hT", [P, KD, T])
                    with ExitStack() as token:
                        h = sb(token, "h", [P, NT, D])
                        phase_norm(K, 0, 0, h, hT)
                    phase_inproj(K, hT, qT, kT, vT, u)
                phase_attention(K, qT, kT, vT, mixT)
            q1, q2, k1, k2 = (sb(mixing, n, [P, 2, NCC, T]) for n in ("q1", "q2", "k1", "k2"))
            pc = sb(mixing, "pc", [P, T // CH, 2, NCC])
            phase_scan_prep(K, u, q1, q2, k1, k2, pc, mixT)
            phase_scan(K, "p", 0, T_CTX // CH, u, q1, q2, k1, k2, pc, None, K.outs[4])
            phase_scan(K, "l", T_CTX, T_LAT // CH, u, q1, q2, k1, k2, pc, K.io["state_rwkv"], None)
            phase_scan_out(K, u, q2, mixT)
        phase_outproj(K, "wo_", mixT, load_w_out(K), 2 * KD * 16, 0)


CPAD = T + 4 * PADC
CSEGS = [(0, T_CTX, 0), (T_CTX, T_LAT, T_CTX + 2 * PADC)]


def phase_glu(K, hT, glu):
    nc, io = K.nc, K.io
    RING = 2
    with ExitStack() as mem:
        wring = mem.enter_context(nc.sbuf_tensor("gl_wring", [P, RING, 2, KD, P], F32))
        sg = mem.enter_context(nc.sbuf_tensor("gl_sg", [P, RING, T], F32))
        ps = mem.enter_context(nc.psum_tensor("gl_ps", [P, 2 * RING, 1024], F32))
        w_in = [K.sem(f"gl_w_in{r}") for r in range(RING)]
        block_done, sig_done, glu_done = (K.sem("gl_" + n) for n in ("block_done", "sig_done", "glu_done"))
        w = io["cv_w_pw1"][0].rearrange("(k p) n -> p k n", p=P)
        bias = VEC["cv_b_pw1"]
        with nc.Block() as block:
            @block.sync
            def _(sp):
                with sp.Fori(0, KD // RING) as i:
                    for r in range(RING):
                        sp.wait_ge(block_done, i * RING + (r + 1))
                        for a in range(2):
                            sp.dma_start(wring[:, r, a], w[:, :, bass.ds(i * RING * P + (r * P + a * D), P)]).then_inc(w_in[r], 16)

            @block.tensor
            def _(pe):
                pe.sem_inc(block_done, RING)
                with pe.Fori(0, KD // RING) as i:
                    for r in range(RING):
                        pe.wait_ge(w_in[r], i * 32 + 32)
                        pe.wait_ge(glu_done, i * RING + (r + 1))
                        for a in range(2):
                            for k in range(KD):
                                nc.tensor.matmul(ps[:, 2 * r + a, SQ:512], wring[:, r, a, k, :], hT[:, k, 0:T_CTX], start=(k == 0), stop=(k == KD - 1))
                                last = nc.tensor.matmul(ps[:, 2 * r + a, 512:1024], wring[:, r, a, k, :], hT[:, k, T_CTX:T], start=(k == 0), stop=(k == KD - 1))
                        last.then_inc(block_done, 1)

            @block.scalar
            def _(act):
                with act.Fori(0, KD // RING) as i:
                    for r in range(RING):
                        act.wait_ge(block_done, i * RING + (RING + r + 1))
                        act.wait_ge(glu_done, i * RING + (r + 1))
                        nc.scalar.activation(sg[:, r, :], ps[:, 2 * r + 1, SQ:1024], ACT.Sigmoid,
                                             bias=K.vec[:, bass.ds(i * RING + (bias + KD + r), 1)]).then_inc(sig_done, 1)

            @block.vector
            def _(dve):
                nc.vector.memset(glu[:], 0.0).then_inc(glu_done, RING)
                dve.wait_ge(glu_done, RING)
                with dve.Fori(0, KD // RING) as i:
                    for r in range(RING):
                        dve.wait_ge(sig_done, i * RING + (r + 1))
                        for n, (c, width, start) in enumerate(CSEGS):
                            ins = nc.vector.scalar_tensor_tensor(
                                glu[:, bass.ds(i * RING + r, 1), start + PADC:start + PADC + width].rearrange("p a t -> p (a t)"),
                                ps[:, 2 * r, SQ + c:SQ + c + width], K.vec[:, bass.ds(i * RING + (bias + r), 1)], sg[:, r, c:c + width], ALU.add, ALU.mult)
                        ins.then_inc(glu_done, 1)


def phase_depthwise(K, glu, cv):
    nc = K.nc
    NPE, RING = 3, 8
    with ExitStack() as mem:
        diag = mem.enter_context(nc.sbuf_tensor("dw_diag", [P, RING, P], F32))
        ps = mem.enter_context(nc.psum_tensor("dw_ps", [P, NPE, 1024], F32))
        diag_ready, tap_done, block_out, own = (K.sem("dw_" + n) for n in ("diag_ready", "tap_done", "block_out", "own"))
        tap_col = lambda w, c: K.vec[:, VEC_DW + w * KD + c:VEC_DW + w * KD + c + 1]
        with nc.Block() as block:
            @block.scalar
            def _(act):
                for c in range(NPE):
                    for w in range(CONVW):
                        n = c * CONVW + w
                        if n >= RING:
                            act.wait_ge(tap_done, n - RING + 1)
                        nc.scalar.activation(diag[:, n % RING, :], K.ident[:], ACT.Copy, scale=tap_col(w, c)).then_inc(diag_ready, 1)
                    act.wait_ge(tap_done, (c + 1) * CONVW)
                    b = VEC["cv_b_dw"] + c
                    nc.scalar.activation(cv[:, c, :], ps[:, c, SQ:1024], ACT.Identity, bias=K.vec[:, b:b + 1]).then_inc(block_out, 1)

            @block.tensor
            def _(pe):
                for c in range(NPE):
                    for w in range(CONVW):
                        n = c * CONVW + w
                        pe.wait_ge(diag_ready, n + 1)
                        nc.tensor.matmul(ps[:, c, SQ:512], diag[:, n % RING, :], glu[:, c, CSEGS[0][2] + w:CSEGS[0][2] + w + T_CTX],
                                         start=(w == 0), stop=(w == CONVW - 1))
                        nc.tensor.matmul(ps[:, c, 512:1024], diag[:, n % RING, :], glu[:, c, CSEGS[1][2] + w:CSEGS[1][2] + w + T_LAT],
                                         start=(w == 0), stop=(w == CONVW - 1)).then_inc(tap_done, 1)

            @block.vector
            def _(dve):
                with dve.Fori(0, KD - NPE) as i:
                    for w in range(CONVW):
                        for n, (c, width, start) in enumerate(CSEGS):
                            dst = cv[:, bass.ds(i + NPE, 1), c:c + width].rearrange("p a t -> p (a t)")
                            src = glu[:, bass.ds(i + NPE, 1), start + w:start + w + width].rearrange("p a t -> p (a t)")
                            wt = K.vec[:, bass.ds(i + (VEC_DW + w * KD + NPE), 1)]
                            if w == 0:
                                ins = nc.vector.tensor_scalar(dst, src, wt, K.vec[:, bass.ds(i + (VEC["cv_b_dw"] + NPE), 1)], ALU.mult, ALU.add)
                            else:
                                dve.wait_ge(own, i * (2 * CONVW) + (2 * (w - 1) + n + 1))
                                ins = nc.vector.scalar_tensor_tensor(dst, src, wt, dst, ALU.mult, ALU.add)
                            ins.then_inc(own, 1)


def phase_conv_norm(K, cv):
    nc = K.nc
    with ExitStack() as mem:
        sb = lambda n, s, d=F32: mem.enter_context(nc.sbuf_tensor("cn_" + n, s, d))
        mean = sb("mean", [P, P])
        sq = sb("sq", [P, KD, T])
        sd = sb("sd", [P, T])
        ps = mem.enter_context(nc.psum_tensor("cn_ps", [P, 2, 1024], F32))
        S = {n: K.sem("cn_" + n) for n in ("mean_const", "mean_done", "centred", "squared", "var_done", "root_done", "inverted", "scaled", "out")}
        with nc.Block() as block:
            @block.tensor
            def _(pe):
                pe.wait_ge(S["mean_const"], 1)
                for b, src, ready in ((0, cv, None), (1, sq, S["squared"])):
                    for k in range(KD):
                        if ready is not None:
                            pe.wait_ge(ready, k + 1)
                        nc.tensor.matmul(ps[:, b, SQ:512], mean[:], src[:, k, 0:T_CTX], start=(k == 0), stop=(k == KD - 1))
                        last = nc.tensor.matmul(ps[:, b, 512:1024], mean[:], src[:, k, T_CTX:T], start=(k == 0), stop=(k == KD - 1))
                    last.then_inc(S["mean_done"] if b == 0 else S["var_done"], 1)

            @block.scalar
            def _(act):
                for k in range(KD):
                    act.wait_ge(S["centred"], k + 1)
                    nc.scalar.activation(sq[:, k, :], cv[:, k, :], ACT.Square).then_inc(S["squared"], 1)
                act.wait_ge(S["var_done"], 1)
                nc.scalar.activation(sd[:], ps[:, 1, SQ:1024], ACT.Sqrt, bias=K.gneps[:, 1:2]).then_inc(S["root_done"], 1)
                for k in range(KD):
                    g, b = (K.vec[:, VEC[n] + k:VEC[n] + k + 1] for n in ("cv_ln_g", "cv_ln_b"))
                    act.wait_ge(S["scaled"], k + 1)
                    nc.scalar.activation(cv[:, k, :], cv[:, k, :], ACT.Silu, bias=b, scale=g).then_inc(S["out"], 1)

            @block.vector
            def _(dve):
                nc.vector.memset(mean[:], 1.0 / D).then_inc(S["mean_const"], 1)
                dve.wait_ge(S["mean_done"], 1)
                for k in range(KD):
                    nc.vector.tensor_tensor(cv[:, k, :], cv[:, k, :], ps[:, 0, SQ:1024], ALU.subtract).then_inc(S["centred"], 1)
                dve.wait_ge(S["root_done"], 1)
                nc.vector.reciprocal(sd[:], sd[:]).then_inc(S["inverted"], 1)
                dve.wait_ge(S["inverted"], 1)
                for k in range(KD):
                    nc.vector.tensor_tensor(cv[:, k, :], cv[:, k, :], sd[:], ALU.mult).then_inc(S["scaled"], 1)


def load_pw2(K):
    def load(eng, dst, sem):
        eng.dma_start(dst[:], K.io["cv_w_pw2"][0].rearrange("(k p) n -> p k n", p=P)).then_inc(sem, 16)
    return load


def phase_mixer_odd(K):
    nc = K.nc
    with ExitStack() as mem:
        sb = lambda s, n, shape: s.enter_context(nc.sbuf_tensor("od_" + n, shape, F32))
        cv = sb(mem, "cv", [P, KD, T])
        with ExitStack() as mixing:
            glu = sb(mixing, "glu", [P, KD, CPAD])
            with ExitStack() as first:
                h, hT = sb(first, "h", [P, NT, D]), sb(first, "hT", [P, KD, T])
                phase_norm(K, 1, 0, h, hT)
                phase_glu(K, hT, glu)
            phase_depthwise(K, glu, cv)
        phase_conv_norm(K, cv)
        phase_outproj(K, "pw2_", cv, load_pw2(K), 16, 1, bias=K.io["cv_b_pw2"][0])


def phase_final(K):
    nc, x = K.nc, K.x
    with ExitStack() as mem:
        sb = lambda n, s: mem.enter_context(nc.sbuf_tensor("fin_" + n, s, F32))
        g, y = sb("g", [P, D]), sb("y", [P, NT, D])
        ss, ms, rt, rstd = (sb(n, [P, NT]) for n in ("ss", "ms", "rt", "rstd"))
        g_in, squares, mean_done, root_done, inverted, y_done, out = (K.sem("fin_" + n) for n in ("g_in", "squares", "mean", "root", "inverted", "y", "out"))
        with nc.Block() as block:
            @block.sync
            def _(sp):
                sp.dma_start(g[:], K.io["final_g"].partition_broadcast(P)).then_inc(g_in, 16)
                for t in range(NT):
                    sp.wait_ge(y_done, t + 1)
                    dst = K.outs[0][0] if t == 0 else K.outs[1][0, (t - 1) * P:t * P, :]
                    sp.dma_start(dst, y[:, t, :]).then_inc(out, 16)
                sp.wait_ge(out, 16 * NT)

            @block.scalar
            def _(act):
                for t in range(NT):
                    nc.scalar.activation(y[:, t, :], x[:, t, :], ACT.Square, accum_out=ss[:, t:t + 1]).then_inc(squares, 1)
                act.wait_ge(mean_done, 1)
                nc.scalar.activation(rt[:], ms[:], ACT.Sqrt).then_inc(root_done, 1)

            @block.vector
            def _(dve):
                dve.wait_ge(squares, NT)
                nc.vector.tensor_scalar(ms[:], ss[:], 1.0 / D, 1e-6, ALU.mult, ALU.add).then_inc(mean_done, 1)
                dve.wait_ge(root_done, 1)
                nc.vector.reciprocal(rstd[:], rt[:]).then_inc(inverted, 1)
                dve.wait_ge(inverted, 1)
                dve.wait_ge(g_in, 16)
                for t in range(NT):
                    nc.vector.scalar_tensor_tensor(y[:, t, :], x[:, t, :], rstd[:, t:t + 1], g[:], ALU.mult, ALU.mult).then_inc(y_done, 1)


def all_phases(K):
    phase_mixer_even(K)
    K.recycle()
    phase_peer(K, 0)
    K.recycle()
    phase_mixer_odd(K)
    phase_peer(K, 1)
    phase_final(K)


def build(nc, io, const, outs, phases=all_phases, dump=None):
    with ExitStack() as stack:
        K = Ctx(nc, io)
        K.const, K.outs, K.dump = const, outs, dump
        sb = lambda n, s, d=F32: stack.enter_context(nc.sbuf_tensor(n, s, d))
        K.x = sb("x", [P, NT, D])
        K.ident = sb("ident", [P, P])
        K.vec = sb("vec", [P, P + 2 * TAP_ROWS])
        K.gneps = sb("gneps", [P, 2])
        K.modrows = nc.dram_tensor("modrows", (2, DEPTH * 6 * D), F32, kind="Internal").ap()
        x_in = K.sem("x_in")
        eps_set = K.sem("eps_set")
        with nc.Block() as block:
            @block.vector
            def _(dve):
                nc.vector.memset(K.gneps[:, 0:1], 64e-5).then_inc(eps_set, 1)
                nc.vector.memset(K.gneps[:, 1:2], 1e-5).then_inc(eps_set, 1)

            @block.sync
            def _(sp):
                sp.dma_start(K.x[:, 0, :], io["x_prompt"][0]).then_inc(x_in, 16)
                sp.dma_start(K.x[:, 1:NT, :], io["x_sample"][0].rearrange("(t p) d -> p t d", p=P)).then_inc(x_in, 16)
                sp.dma_start(K.ident[:], const["ident"]).then_inc(x_in, 16)
                sp.wait_ge(x_in, 48)
        phase_vectors(K)
        phase_modulation(K)
        phases(K)


INPUTS = ["x_prompt", "x_sample", "cache_k", "cache_v", "state_rwkv", "c", "c_ctx", "mod_w", "mod_b", "norm_g", "ab_w_in",
          "ab_w_out", "ab_sink", "ab_shift_w", "ab_k_k", "ab_k_a", "ab_r_k", "ab_w0", "ab_w2", "ab_a0", "ab_a2", "ab_g2",
          "ab_gn_g", "ab_gn_b", "cv_w_pw1", "cv_b_pw1", "cv_w_dw", "cv_b_dw", "cv_ln_g", "cv_ln_b", "cv_w_pw2", "cv_b_pw2",
          "peer_w_q", "peer_keys", "peer_u", "peer_v", "final_g"]
OUTPUTS = [(1, T_CTX, D), (1, T_LAT, D), (1, 1, T_CTX, KV, HD), (1, 1, T_CTX, KV, HD), (1, 1, 2, HEADS, HD, HD)]


def kernel(**inputs):
    import concourse.bacc as bacc
    from concourse.bass_utils import run_bass_kernel_spmd

    nc = bacc.Bacc("TRN2", target_bir_lowering=False, num_devices=1)
    arrays, io, const = {}, {}, {}
    for group, named in ((io, {n: np.ascontiguousarray(inputs[n]) for n in INPUTS}), (const, shape_constants())):
        for name, a in named.items():
            full = ("in_" if group is io else "const_") + name
            arrays[full] = a
            group[name] = nc.dram_tensor(full, a.shape, mybir.dt.from_np(a.dtype), kind="ExternalInput").ap()
    outs = [nc.dram_tensor(f"out_{i}", shape, F32, kind="ExternalOutput").ap() for i, shape in enumerate(OUTPUTS)]
    build(nc, io, const, outs)
    r = run_bass_kernel_spmd(nc, [arrays], core_ids=[0])
    return tuple(r.results[0][f"out_{i}"] for i in range(len(OUTPUTS)))
```
